# Optimizing a Trainium2 kernel written in Bass

```python
import math
import jax, jax.numpy as jnp
from jax import lax
import numpy as np

D_MODEL = 1024
BATCH = 1
SEQ = 128
DEPTH = 2
DEC_BATCH = 1
DEC_SEQ = 512
PAST_LEN = 128

GRID_W = 64
H_A = 4
DQK_A = 64
DV_A = 128
QK_W_A = H_A * 2 * DQK_A
W_A = H_A * DV_A
G_B = 4
DG_B = 64
W_B = G_B * DG_B
CHUNK_B = 128
H_C = 4
DK_C = 64
DV_C = 64
WK_C = H_C * DK_C
W_C = H_C * DV_C
CHUNK_C = 64
MIX_W = W_A + W_B + W_C
OFF_QA = 0
OFF_KA = OFF_QA + QK_W_A
OFF_VA = OFF_KA + QK_W_A
OFF_UB = OFF_VA + W_A
OFF_VB = OFF_UB + W_B
OFF_IC = OFF_VB + W_B
OFF_FC = OFF_IC + W_C
OFF_QC = OFF_FC + 2 * WK_C
OFF_GC = OFF_QC + 2 * WK_C
N_IN = OFF_GC + W_C
Q_BLOCK = 128
ROPE_THETA = 10000.0
N_EXP = 16
N_GROUP = 4
EXP_PER_GROUP = N_EXP // N_GROUP
TOP_K = 2
GROUP_TOP = 2
D_FF_E = 512
MOE_BLOCK = 128
LN_EPS = 1e-5
ALPHA = (2 * DEPTH) ** 0.25
BETA = (8 * DEPTH) ** -0.25

kernel_name = 'hybrid_diffusion_step'

def layer_norm(x, g, b):
    xf = x.astype(jnp.float32)
    mu = xf.mean(-1, keepdims=True)
    var = jnp.square(xf - mu).mean(-1, keepdims=True)
    y = (xf - mu) * lax.rsqrt(var + LN_EPS)
    return (y * g.astype(jnp.float32) + b.astype(jnp.float32)).astype(x.dtype)

def rms_norm(x, g):
    xf = x.astype(jnp.float32)
    y = xf * lax.rsqrt(jnp.mean(xf * xf, -1, keepdims=True) + LN_EPS)
    return (y * g.astype(jnp.float32)).astype(x.dtype)

def ada_modulation(cond, w, b):
    m = jax.nn.silu(cond) @ w + b
    return m.reshape(cond.shape[0], 6, D_MODEL)

def modulate(x, shift, scale):
    return x * (1 + scale[:, None, :]) + shift[:, None, :]

def axial_rope(x):
    L = x.shape[1]
    rows_n = L // GRID_W
    row = jnp.repeat(jnp.arange(rows_n), GRID_W).astype(jnp.float32)
    col = jnp.tile(jnp.arange(GRID_W), rows_n).astype(jnp.float32)
    half = DQK_A // 2
    quarter = half // 2
    inv = ROPE_THETA ** (-jnp.arange(quarter, dtype=jnp.float32) / quarter)

    def rot(xp, pos):
        ang = pos[:, None] * inv
        cos = jnp.cos(ang)[None, :, None, None, :]
        sin = jnp.sin(ang)[None, :, None, None, :]
        x1, x2 = xp[..., :quarter], xp[..., quarter:]
        return jnp.concatenate([x1 * cos - x2 * sin, x2 * cos + x1 * sin], -1)

    out = jnp.concatenate([rot(x[..., :half], row), rot(x[..., half:], col)], -1)
    return out.astype(x.dtype)

def attn_split(proj):
    B, L = proj.shape[:2]
    q = proj[..., OFF_QA:OFF_QA + QK_W_A].reshape(B, L, H_A, 2, DQK_A)
    k = proj[..., OFF_KA:OFF_KA + QK_W_A].reshape(B, L, H_A, 2, DQK_A)
    v = proj[..., OFF_VA:OFF_VA + W_A].reshape(B, L, H_A, DV_A)
    return q, k, v

def diff_attention(q, k, v, lam):
    B, Lq = q.shape[:2]
    nb = Lq // Q_BLOCK
    qb = q.reshape(B, nb, Q_BLOCK, H_A, 2, DQK_A).swapaxes(0, 1)
    scale = DQK_A ** -0.5

    def one(qblk):
        s = jnp.einsum('bqhmd,bkhmd->bhmqk', qblk, k).astype(jnp.float32) * scale
        p = jax.nn.softmax(s, axis=-1)
        pd = p[:, :, 0] - lam * p[:, :, 1]
        return jnp.einsum('bhqk,bkhe->bqhe', pd.astype(v.dtype), v)

    o = lax.map(one, qb)
    return o.swapaxes(0, 1).reshape(B, Lq, H_A, DV_A)

def diff_attn_out(o, g, lam_init):
    B, L = o.shape[:2]
    return (rms_norm(o, g) * (1.0 - lam_init)).reshape(B, L, W_A)

def chunk_mlp(proj, ln_g, ln_b, w_s, b_s):
    B, L = proj.shape[:2]
    u = jax.nn.gelu(proj[..., OFF_UB:OFF_UB + W_B])
    v = layer_norm(jax.nn.gelu(proj[..., OFF_VB:OFF_VB + W_B]), ln_g, ln_b)
    vr = v.reshape(B, L // CHUNK_B, CHUNK_B, G_B, DG_B)
    mixed = jnp.einsum('gij,bnjgd->bnigd', w_s, vr) + b_s.T[None, None, :, :, None]
    return u * mixed.reshape(B, L, W_B)

def hgrn_lower_bounds(lb_logits):
    p = jax.nn.softmax(lb_logits.astype(jnp.float32), axis=1)
    cs = jnp.cumsum(p, axis=1)
    return cs - cs[:, :1]

def hgrn_scan(q, k, logf, i, s0):
    B, L = q.shape[:2]
    n = L // CHUNK_C

    def chunks(t):
        return t.astype(jnp.float32).reshape(B, n, CHUNK_C, *t.shape[2:]).swapaxes(0, 1)

    mask = jnp.tril(jnp.ones((CHUNK_C, CHUNK_C), bool))[None, :, :, None, None]

    def step(S, inp):
        qc, kc, gc, ic = inp
        b = jnp.cumsum(gc, axis=1)
        o_inter = jnp.einsum('bthd,bhde->bthe', qc * jnp.exp(b), S)
        diff = b[:, :, None] - b[:, None, :]
        dec = jnp.exp(jnp.where(mask, diff, -jnp.inf))
        a = jnp.einsum('bthd,bshd,btshd->bhts', qc, kc, dec)
        o_intra = jnp.einsum('bhts,bshe->bthe', a, ic)
        b_last = b[:, -1]
        S_new = jnp.exp(b_last)[..., None] * S + jnp.einsum(
            'bshd,bshe->bhde', kc * jnp.exp(b_last[:, None] - b), ic)
        return S_new, o_inter + o_intra

    s_fin, o = lax.scan(step, s0.astype(jnp.float32), (chunks(q), chunks(k), chunks(logf), chunks(i)))
    return o.swapaxes(0, 1).reshape(B, L, H_C, DV_C), s_fin

def hgrn_mixer(proj, lb, norm_g, s_fwd0, s_bwd0):
    B, L = proj.shape[:2]
    i = proj[..., OFF_IC:OFF_IC + W_C].reshape(B, L, H_C, DV_C)
    gate = proj[..., OFF_GC:OFF_GC + W_C]
    outs = []
    states = []
    for d, s0 in enumerate((s_fwd0, s_bwd0)):
        fpre = proj[..., OFF_FC + d * WK_C:OFF_FC + (d + 1) * WK_C].astype(jnp.float32)
        q = proj[..., OFF_QC + d * WK_C:OFF_QC + (d + 1) * WK_C].reshape(B, L, H_C, DK_C)
        f = lb[d] + (1.0 - lb[d]) * jax.nn.sigmoid(fpre)
        logf = jnp.log(f).reshape(B, L, H_C, DK_C)
        k = (1.0 - f).reshape(B, L, H_C, DK_C)
        ii = i
        if d == 1:
            q, k, logf, ii = jnp.flip(q, 1), jnp.flip(k, 1), jnp.flip(logf, 1), jnp.flip(ii, 1)
        o, s = hgrn_scan(q, k, logf, ii, s0)
        if d == 1:
            o = jnp.flip(o, 1)
        outs.append(o)
        states.append(s)
    o = rms_norm(outs[0] + outs[1], norm_g.reshape(H_C, DV_C)).astype(proj.dtype)
    o = o.reshape(B, L, W_C) * jax.nn.silu(gate)
    return o, jnp.stack(states, axis=1)

def moe_ffn(h, w_router, router_bias, wg, wu, wd):
    B, L, D = h.shape
    T = B * L
    xt = h.reshape(T, D)
    scores = jax.nn.sigmoid((xt @ w_router).astype(jnp.float32))
    sel = scores + router_bias.astype(jnp.float32)
    gscore = lax.top_k(sel.reshape(T, N_GROUP, EXP_PER_GROUP), GROUP_TOP)[0].sum(-1)
    gbest = jnp.argmax(gscore, axis=-1)
    in_grp = (jnp.arange(N_EXP) // EXP_PER_GROUP)[None, :] == gbest[:, None]
    _, eidx = lax.top_k(jnp.where(in_grp, sel, -jnp.inf), TOP_K)
    wsel = jnp.take_along_axis(scores, eidx, axis=-1)
    wsel = wsel / wsel.sum(-1, keepdims=True)
    A = T * TOP_K
    e_flat = eidx.reshape(-1)
    t_flat = jnp.repeat(jnp.arange(T, dtype=jnp.int32), TOP_K)
    w_flat = wsel.reshape(-1)
    order = jnp.argsort(e_flat)
    e_s, t_s, w_s = e_flat[order], t_flat[order], w_flat[order]
    counts = jax.ops.segment_sum(jnp.ones((A,), jnp.int32), e_flat, num_segments=N_EXP)
    starts = jnp.cumsum(counts) - counts
    pcounts = (counts + MOE_BLOCK - 1) // MOE_BLOCK * MOE_BLOCK
    pends = jnp.cumsum(pcounts)
    pstarts = pends - pcounts
    dest = pstarts[e_s] + jnp.arange(A, dtype=jnp.int32) - starts[e_s]
    n_blocks = (A + MOE_BLOCK - 1) // MOE_BLOCK + N_EXP
    n_rows = n_blocks * MOE_BLOCK
    row_tok = jnp.zeros((n_rows,), jnp.int32).at[dest].set(t_s)
    row_w = jnp.zeros((n_rows,), jnp.float32).at[dest].set(w_s)
    block_e = jnp.minimum(
        jnp.searchsorted(pends, jnp.arange(n_blocks, dtype=jnp.int32) * MOE_BLOCK, side='right'),
        N_EXP - 1)
    xb = xt[row_tok].reshape(n_blocks, MOE_BLOCK, D)

    def expert_block(args):
        xblk, e = args
        a = jax.nn.silu(xblk @ wg[e]) * (xblk @ wu[e])
        return a @ wd[e]

    yb = lax.map(expert_block, (xb, block_e)).reshape(n_rows, D)
    y = jax.ops.segment_sum(yb * row_w[:, None].astype(yb.dtype), row_tok, num_segments=T)
    return y.reshape(B, L, D)

def residual_ffn(x, m, mixed, w_out, ln_g, ln_b, w_router, router_bias, wg, wu, wd):
    x = layer_norm(ALPHA * x + m[:, 2][:, None, :] * (mixed @ w_out), ln_g[0], ln_b[0])
    h = modulate(x, m[:, 3], m[:, 4])
    y = moe_ffn(h, w_router, router_bias, wg, wu, wd)
    return layer_norm(ALPHA * x + m[:, 5][:, None, :] * y, ln_g[1], ln_b[1])

def setup_inputs(seed: int = 0) -> dict:
    key = jax.random.key(seed)
    ks = jax.random.split(key, 26)
    f32 = jnp.float32
    nrm = lambda k, s: jax.random.normal(k, s, f32)
    return {
        'x_prompt': nrm(ks[0], (BATCH, SEQ, D_MODEL)),
        'x_sample': nrm(ks[1], (DEC_BATCH, DEC_SEQ, D_MODEL)),
        'c': nrm(ks[2], (DEC_BATCH, D_MODEL)),
        'cache_k': nrm(ks[3], (DEC_BATCH, DEPTH, PAST_LEN, H_A, 2, DQK_A)),
        'cache_v': nrm(ks[4], (DEC_BATCH, DEPTH, PAST_LEN, H_A, DV_A)),
        'state_hgrn': 0.5 * nrm(ks[5], (DEC_BATCH, DEPTH, 2, H_C, DK_C, DV_C)),
        'c_ctx': nrm(ks[6], (D_MODEL,)),
        'w_ada': 0.5 * D_MODEL ** -0.5 * nrm(ks[7], (DEPTH, D_MODEL, 6 * D_MODEL)),
        'b_ada': 0.02 * nrm(ks[8], (DEPTH, 6 * D_MODEL)),
        'w_in': D_MODEL ** -0.5 * nrm(ks[9], (DEPTH, D_MODEL, N_IN)),
        'w_out': BETA * MIX_W ** -0.5 * nrm(ks[10], (DEPTH, MIX_W, D_MODEL)),
        'diff_lambda': 0.1 * nrm(ks[11], (DEPTH, 4, DQK_A)),
        'attn_norm_g': 1.0 + 0.02 * nrm(ks[12], (DEPTH, DV_A)),
        'mlp_ln_g': 1.0 + 0.02 * nrm(ks[13], (DEPTH, W_B)),
        'mlp_ln_b': 0.02 * nrm(ks[14], (DEPTH, W_B)),
        'w_spatial': CHUNK_B ** -0.5 * nrm(ks[15], (DEPTH, G_B, CHUNK_B, CHUNK_B)),
        'b_spatial': 1.0 + 0.02 * nrm(ks[16], (DEPTH, G_B, CHUNK_B)),
        'hgrn_lb': nrm(ks[17], (2, DEPTH, WK_C)),
        'hgrn_norm_g': 1.0 + 0.02 * nrm(ks[18], (DEPTH, W_C)),
        'ln_g': 1.0 + 0.02 * nrm(ks[19], (DEPTH, 2, D_MODEL)),
        'ln_b': 0.02 * nrm(ks[20], (DEPTH, 2, D_MODEL)),
        'w_router': D_MODEL ** -0.5 * nrm(ks[21], (D_MODEL, N_EXP)),
        'router_bias': 0.01 * nrm(ks[22], (N_EXP,)),
        'w_gate': D_MODEL ** -0.5 * nrm(ks[23], (DEPTH, N_EXP, D_MODEL, D_FF_E)),
        'w_up': D_MODEL ** -0.5 * nrm(ks[24], (DEPTH, N_EXP, D_MODEL, D_FF_E)),
        'w_down': BETA * D_FF_E ** -0.5 * nrm(ks[25], (DEPTH, N_EXP, D_FF_E, D_MODEL)),
    }

def reference(x_prompt, x_sample, c, cache_k, cache_v, state_hgrn, c_ctx, w_ada, b_ada, w_in, w_out,
              diff_lambda, attn_norm_g, mlp_ln_g, mlp_ln_b, w_spatial, b_spatial, hgrn_lb, hgrn_norm_g,
              ln_g, ln_b, w_router, router_bias, w_gate, w_up, w_down):
    lb_all = hgrn_lower_bounds(hgrn_lb)
    xp, xs = x_prompt, x_sample
    zero_state = jnp.zeros((xp.shape[0], H_C, DK_C, DV_C), jnp.float32)
    new_k, new_v, new_s = [], [], []
    for l in range(DEPTH):
        lam_init = 0.8 - 0.6 * math.exp(-0.3 * l)
        dl = diff_lambda[l].astype(jnp.float32)
        lam = jnp.exp(jnp.sum(dl[0] * dl[1])) - jnp.exp(jnp.sum(dl[2] * dl[3])) + lam_init

        m_p = ada_modulation(c_ctx[None, :], w_ada[l], b_ada[l])
        h = modulate(xp, m_p[:, 0], m_p[:, 1])
        proj = h @ w_in[l]
        q, k, v = attn_split(proj)
        o_a = diff_attn_out(diff_attention(q, k, v, lam), attn_norm_g[l], lam_init)
        o_b = chunk_mlp(proj, mlp_ln_g[l], mlp_ln_b[l], w_spatial[l], b_spatial[l])
        o_c, s_ctx = hgrn_mixer(proj, lb_all[:, l], hgrn_norm_g[l], zero_state, zero_state)
        mixed = jnp.concatenate([o_a.astype(proj.dtype), o_b, o_c], axis=-1)
        xp = residual_ffn(xp, m_p, mixed, w_out[l], ln_g[l], ln_b[l], w_router, router_bias,
                          w_gate[l], w_up[l], w_down[l])
        new_k.append(k)
        new_v.append(v)
        new_s.append(s_ctx.astype(xp.dtype))

        m_s = ada_modulation(c, w_ada[l], b_ada[l])
        h = modulate(xs, m_s[:, 0], m_s[:, 1])
        proj = h @ w_in[l]
        q, k, v = attn_split(proj)
        q, k = axial_rope(q), axial_rope(k)
        k_all = jnp.concatenate([cache_k[:, l].astype(k.dtype), k], axis=1)
        v_all = jnp.concatenate([cache_v[:, l].astype(v.dtype), v], axis=1)
        o_a = diff_attn_out(diff_attention(q, k_all, v_all, lam), attn_norm_g[l], lam_init)
        o_b = chunk_mlp(proj, mlp_ln_g[l], mlp_ln_b[l], w_spatial[l], b_spatial[l])
        o_c, _ = hgrn_mixer(proj, lb_all[:, l], hgrn_norm_g[l], state_hgrn[:, l, 0], state_hgrn[:, l, 1])
        mixed = jnp.concatenate([o_a.astype(proj.dtype), o_b, o_c], axis=-1)
        xs = residual_ffn(xs, m_s, mixed, w_out[l], ln_g[l], ln_b[l], w_router, router_bias,
                          w_gate[l], w_up[l], w_down[l])
    return (xp, xs, jnp.stack(new_k, axis=1), jnp.stack(new_v, axis=1), jnp.stack(new_s, axis=1))


_drawn_inputs = setup_inputs


def setup_inputs(seed=0):
    import zlib

    import numpy as np

    out = dict(_drawn_inputs(seed))
    spreads = {}
    factors = {'cache_k': 3.676,
     'cache_v': 3.416,
     'state_hgrn': 8.0,
     'diff_lambda': 5.68,
     'attn_norm_g': 30.709,
     'mlp_ln_g': 37.9,
     'mlp_ln_b': 39.354,
     'b_spatial': 37.042,
     'hgrn_norm_g': 40.309}
    for name, (base, spread) in spreads.items():
        noise = np.random.default_rng([zlib.crc32(name.encode()), seed]).standard_normal(out[name].shape)
        drawn = base * np.exp(spread * noise) if base else spread * noise
        out[name] = __import__('jax').numpy.asarray(drawn.astype(out[name].dtype))
    for name, factor in factors.items():
        out[name] = (out[name] * factor).astype(out[name].dtype)
    return out
```

```python
import math
from contextlib import ExitStack

import concourse.bass as bass
from concourse import mybir
from concourse.alu_op_type import AluOpType as ALU

ACT = mybir.ActivationFunctionType
AXX = mybir.AxisListType.X
F32 = mybir.dt.float32
I32 = mybir.dt.int32
U8 = mybir.dt.uint8

P = 128
D = 1024
DEPTH = 2
NT = 5
T = NT * P
KD = D // P
NIN = 3584
HA = 4
DQ = 64
SCALE = DQ ** -0.5
HC = 4
LEVELS = [64, 32, 16, 8, 4, 2, 1]
NL = len(LEVELS)
GB = 4
NE = 16
DFF = 512
OVB = 9
NB = NE + OVB
NEG = 1e30
ALPHA = (2 * DEPTH) ** 0.25
EPS = 1e-5
W = 512
SLOT = KD * W

COLS = {"F": 2304, "Q": 2816, "I": 2048, "G": 3328, "UV": 1536, "VA": 1024, "KA": 512, "QA": 0}

N_PJ, N_PJA, N_PJV, N_TR = 45, 25, 20, 30

C_ID, C_TRI, C_W4, C_W16, C_E128, C_J, C_TOK, C_COS, C_SIN, C_SCAN, C_END = (
    0, 128, 384, 388, 404, 420, 429, 434, 690, 946, 1591)


def nth(l, per, n):
    return l * per + n


def loadsA(l, j, uses):
    return l * (192 if j == 2 else 176) + (128 + 16 * uses + (16 if j == 2 else 0))


def lam_init(l):
    return 0.8 - 0.6 * math.exp(-0.3 * l)


def build_program(nc, A):
    with ExitStack() as ctx:
        def sb(name, shape, dt=F32):
            return ctx.enter_context(nc.sbuf_tensor("sb_" + name, shape, dt))

        def sem(name):
            return ctx.enter_context(nc.semaphore(name))

        def dram(name, shape):
            return nc.dram_tensor(name, shape, F32, kind="Internal").ap()

        mod_dram = dram("mod_dram", [DEPTH, 2, 6 * D])
        tok_dram = dram("tok_dram", [T, D])
        exp_dram = dram("exp_dram", [NB * P, D])
        idt_dram = dram("idt_dram", [NB * P, 1])

        wA = sb("wA", [P, 3 * SLOT])
        x = sb("x", [P, NT, D])
        gate_mod = sb("gate_mod", [P, 2, D])
        cst = sb("cst", [P, C_END])
        masks = sb("masks", [P, 2 * NL + 1, P], U8)
        prm = sb("prm", [P, 1412])
        rw = sb("rw", [P, KD, NE])
        rbias = sb("rbias", [P, NE])
        condT = sb("condT", [P, KD, 2])
        small = sb("small", [P, 640])
        ismall = sb("ismall", [P, 64], I32)
        arena = sb("arena", [P, 28956])
        psum = ctx.enter_context(nc.psum_tensor("psum", [P, 4096], F32))

        ident = cst[:, C_ID:C_ID + P]
        ar = arena

        def view(off, n, pattern=None, **kw):
            v = ar[:, off:off + n]
            return v.rearrange(pattern, **kw) if pattern else v

        HG = 5120
        hT = view(0, 5120, "p (k t) -> p k t", k=KD)
        kf = view(HG, 2560, "p (c t) -> p c t", c=4)
        qf = view(HG + 2560, 2560, "p (c t) -> p c t", c=4)
        BW = NT * (P + 1)
        bsum = view(HG + 5120, 4 * BW, "p (c w j) -> p c w j", c=4, w=NT)
        bsum2 = view(HG + 5120, 4 * BW, "p (c w) -> p c w", c=4)
        gpad = view(HG + 7700, BW, "p (w j) -> p w j", w=NT)
        gpad2 = view(HG + 7700, BW)
        Qb = view(HG + 8345, 1280, "p (s t) -> p s t", s=2)
        Kb = view(HG + 9625, 1280, "p (s t) -> p s t", s=2)
        Eb = view(HG + 10905, 1280, "p (s t) -> p s t", s=2)
        KEn = view(HG + 12185, 640, "p (w d) -> p w d", w=NT)
        AT = view(HG + 12825, 2560, "p (r h t) -> p r h t", r=2, h=2)
        AT2 = view(HG + 12825, 2560)
        S = view(HG + 15385, 1792, "p (r s e) -> p r s e", r=2, s=7)
        S2 = view(HG + 15385, 1792)
        ishift = view(HG + 8345, 4096, "p (y m d) -> p y m d", y=2, m=2)
        hin = view(HG + 12825, 2048, "p (s d) -> p s d", s=2)
        qT = view(HG, 2560, "p (h t) -> p h t", h=HA)
        kT = view(HG + 2560, 3072, "p (h t) -> p h t", h=HA)
        vv = view(HG + 5632, 3072, "p (s c) -> p s c", s=6)
        oa = view(HG + 8704, 2560, "p (t c) -> p t c", t=NT)
        Pb = view(HG + 11264, 2560, "p (s m k) -> p s m k", s=2, m=2)
        pd = view(HG + 13824, 1280, "p (s k) -> p s k", s=2)
        pdT = view(HG + 15104, 1280, "p (s k) -> p s k", s=2)
        nat = view(HG + 11264, 1024, "p (s c) -> p s c", s=2)
        ropeb = view(HG + 12288, 512)
        lnb = view(HG + 11264, 2048, "p (m d) -> p m d", m=2)
        ig = view(22300, 2560, "p (t c) -> p t c", t=NT)
        oc = view(24860, 1280, "p (t c) -> p t c", t=NT)
        uv = view(26140, 2560, "p (t c) -> p t c", t=NT)
        wB = 0
        shift2 = view(18432, 4096, "p (y m d) -> p y m d", y=2, m=2)
        hh = view(22528, 2048, "p (s d) -> p s d", s=2)
        hTt = view(24860, 1024, "p (k t) -> p k t", k=KD)
        xg = [view(25884 + 1024 * s, 1024) for s in range(2)]
        xgT = [view(12288 + 1024 * s, 1024, "p (k t) -> p k t", k=KD) for s in range(2)]
        av = [view(14336 + 512 * s, 512) for s in range(2)]
        aT = [view(15360 + 512 * s, 512, "p (k t) -> p k t", k=4) for s in range(2)]
        x1t = [view(12288 + 512 * s, 512) for s in range(2)]
        sg = [view(22528 + 512 * s, 512) for s in range(2)]
        yb = [view(23552, 1024), view(27932, 1024)]
        mrow = ar[0:2, 0:DEPTH * 6 * D]
        zrow = ar[0:NB, 28672:28672 + P]
        idrow = ar[0:NB, 22528:22528 + P]

        def slotA(j):
            return wA[:, j * SLOT:(j + 1) * SLOT]

        def slotB(j):
            return ar[:, wB + j * SLOT:wB + (j + 1) * SLOT]

        def bank(i, n=512):
            return psum[:, i * 512:i * 512 + n]

        ag, hg, mg, mb = prm[:, 0:128], prm[:, 128:384], prm[:, 384:640], prm[:, 640:896]
        wsT = prm[:, 896:1408].rearrange("p (g i) -> p g i", g=GB)
        bsT = prm[:, 1408:1412]

        o = [0]

        def sm(n):
            o[0] += n
            return small[:, o[0] - n:o[0]]

        lbt = sm(DEPTH * 4).rearrange("p (l c) -> p l c", l=DEPTH)
        lbx = sm(DEPTH * 4).rearrange("p (l c) -> p l c", l=DEPTH)
        lbm, lb, omlb, nomlb = sm(4), sm(4), sm(4), sm(4)
        lams, lamn, lamn_l, oml, oml_l = sm(DEPTH * 2), sm(DEPTH), sm(1), sm(DEPTH), sm(1)
        eB = sm(20).rearrange("p (c w) -> p c w", c=4)
        stats = sm(60).rearrange("p (t s f) -> p t s f", t=NT, s=2)
        mv = sm(10).rearrange("p (t f) -> p t f", t=NT)
        rstd = sm(NT)
        ms, rs = sm(20), sm(20)
        nmx, negm = sm(2), sm(40)
        Z, rZ, cc = sm(40), sm(40), sm(20)
        score = sm(80).rearrange("p (t e) -> p t e", t=NT)
        gt = sm(20).rearrange("p (t g) -> p t g", t=NT)
        ovc, ovi, ovx = sm(NE), sm(NE), sm(NE)
        wt = sm(10).rearrange("p (t k) -> p t k", t=NT)
        psn = sm(10).rearrange("p (t k) -> p t k", t=NT)
        wsum = sm(NT)
        mhalf = sm(20)
        spare = sm(OVB)
        posi = ismall[:, 0:10].rearrange("p (t k) -> p t k", t=NT)
        ids = ismall[:, 10:10 + NB]
        novi = ismall[:, 36:37]
        bexi = ismall[:, 40:40 + OVB]
        R = [view(25884 + 80 * i, 80, "p (t e) -> p t e", t=NT) for i in range(12)]
        R9 = view(25884 + 960, OVB * NE, "p (j e) -> p j e", j=OVB)
        R9s = view(25884 + 960 + 144, OVB)
        lamb = view(12288, DEPTH * 4 * 64, "p (l f d) -> p l f d", l=DEPTH, f=4)
        maskf = view(14336, (2 * NL + 1) * P, "p (m t) -> p m t", m=2 * NL + 1)
        lamp = view(13312, DEPTH * 2 * 64, "p (l f d) -> p l f d", l=DEPTH, f=2)

        x_in, consts, lam_in = sem("x_in"), sem("consts"), sem("lam_in")
        bias_in = sem("bias_in")
        cond_ready, ada_mm, ada_free = sem("cond_ready"), sem("ada_mm"), sem("ada_free")
        ada_ready, mod_out = sem("ada_ready"), sem("mod_out")
        zero_ready, zero_out = sem("zero_ready"), sem("zero_out")
        pe_setup, lb_exp, setup_done = sem("pe_setup"), sem("lb_exp"), sem("setup_done")
        lbs_ready = sem("lbs_ready")
        landedA = [sem(f"landedA{j}") for j in range(3)]
        landedB = [sem(f"landedB{j}") for j in range(3)]
        slots_free = sem("slots_free")
        x_ready = sem("x_ready")
        m01_in, m2_in, prm_in, ln1_in = sem("m01_in"), sem("m2_in"), sem("prm_in"), sem("ln1_in")
        m34_in, m5_in, ln2_in, kv_in = sem("m34_in"), sem("m5_in"), sem("ln2_in"), sem("kv_in")
        h_ready, tr_done, tr_evac = sem("h_ready"), sem("tr_done"), sem("tr_evac")
        pj_done, pjA, pjV = sem("pj_done"), sem("pjA_evac"), sem("pjV_evac")
        f_ready, g_ready, k_ready = sem("f_ready"), sem("g_ready"), sem("k_ready")
        D_ready, E_ready, Q_ready, K_ready = sem("D_ready"), sem("E_ready"), sem("Q_ready"), sem("K_ready")
        lv_mm, lv_acc, at_zero = sem("lv_mm"), sem("lv_acc"), sem("at_zero")
        s_zero, s_init, s_ready = sem("s_zero"), sem("s_init"), sem("s_ready")
        ke_t, ke_evac, ds_mm = sem("ke_t"), sem("ke_evac"), sem("ds_mm")
        o_mm, o_evac = sem("o_mm"), sem("o_evac")
        var_ready, rstd_ready = sem("var_ready"), sem("rstd_ready")
        v_ready, sp_mm, hg_done = sem("v_ready"), sem("sp_mm"), sem("hg_done")
        r_ready, r_tr, r_evac = sem("r_ready"), sem("r_tr"), sem("r_evac")
        sc_done, nm_ready, p_ready, pd_ready = sem("sc_done"), sem("nm_ready"), sem("p_ready"), sem("pd_ready")
        sc_first = sem("sc_first")
        at_tr, at_evac, pv_done, oa_evac = sem("at_tr"), sem("at_evac"), sem("pv_done"), sem("oa_evac")
        mix_ready, x1_ready = sem("mix_ready"), sem("x1_ready")
        h_stored = [sem("h_stored0"), sem("h_stored1")]
        rt_mm, rt_score, m_ready, rank_mm = sem("rt_mm"), sem("rt_score"), sem("m_ready"), sem("rank_mm")
        pos_ready, id_scat, id_row, id_tr, ids_ready = (
            sem("pos_ready"), sem("id_scat"), sem("id_row"), sem("id_tr"), sem("ids_ready"))
        xg_in = [sem("xg_in0"), sem("xg_in1")]
        xT_done, xT_act, xT_dve = sem("xT_done"), sem("xT_act"), sem("xT_dve")
        gate_done, up_done, sg_ready, a_ready = sem("gate_done"), sem("up_done"), sem("sg_ready"), sem("a_ready")
        aT_done, aT_ready, y_done = sem("aT_done"), sem("aT_ready"), sem("y_done")
        yA_evac, yB_evac = sem("yA_evac"), sem("yB_evac")
        y_stored = [sem("y_stored0"), sem("y_stored1")]
        ov_w, ov_g, ov_pe, ov_act, ov_dve, ov_st = (
            sem("ov_w"), sem("ov_g"), sem("ov_pe"), sem("ov_act"), sem("ov_dve"), sem("ov_st"))
        cmb_in = [sem("cmb_in0"), sem("cmb_in1")]
        cmb_used = sem("cmb_used")
        out_k, out_v, out_s, out_y = sem("out_k"), sem("out_v"), sem("out_s"), sem("out_y")

        passed = {e.engine: sem("passed_" + nm) for nm, e in (
            ("sp", nc.sync), ("pe", nc.tensor), ("act", nc.scalar), ("gp", nc.gpsimd), ("dve", nc.vector))}
        PRE = 2

        def until(eng, signal, n):
            eng.wait_ge(signal, n)
            eng.sem_inc(passed[eng.engine], 1)

        def in_block(l, c0, w=W):
            return bass.AP(A["w_in"].tensor, l * (D * NIN) + c0, [[NIN, P], [P * NIN, KD], [1, w]])

        def out_block(l, c0):
            return bass.AP(A["w_out"].tensor, l * (D * D) + c0, [[D, P], [P * D, KD], [1, W]])

        def gate_up(name, l, e):
            return bass.AP(A[name].tensor, (l * NE + e) * (D * DFF), [[DFF, P], [P * DFF, KD], [1, DFF]])

        def down(l, e):
            return bass.AP(A["w_down"].tensor, (l * NE + e) * (D * DFF), [[D, P], [P * D, 4], [1, D]])

        def rows(name, off, n):
            return bass.AP(A[name].tensor, off, [[0, P], [1, n]])

        def mod_rows(l, m, n):
            return bass.AP(mod_dram.tensor, l * (12 * D) + m * D, [[0, P], [6 * D, 2], [1, n * D]])

        def s3(v, k=KD):
            return v.rearrange("p (k c) -> p k c", k=k)

        block = ctx.enter_context(nc.Block())

        @block.sync
        def _(sp):
            sp.dma_start(condT[:], A["condT"]).then_inc(bias_in, 16)
            sp.dma_start(mrow, bass.AP(A["b_ada"].tensor, 0, [[0, 2], [1, DEPTH * 6 * D]])).then_inc(bias_in, 16)
            with sp.Fori(0, DEPTH) as la:
                with sp.Fori(0, 4) as i:
                    for j in range(3):
                        until(sp, ada_mm, la * 12 + i * 3 + j + 1)
                        src = bass.AP(A["w_ada"].tensor, la * (6 * D * D) + (i * (3 * W) + j * W),
                                      [[6 * D, P], [P * 6 * D, KD], [1, W]])
                        sp.dma_start(s3(slotA(j)), src).then_inc(landedA[j], 16)
            with sp.Fori(0, DEPTH) as l:
                order = ["F", "Q", "I", "UV", "VA", "KA", "QA"]
                until(sp, slots_free, l + 1)
                for b, nm in enumerate(order):
                    if b >= 3:
                        until(sp, pj_done, nth(l, N_PJ, 5 * (b - 2)))
                    dst = s3(slotA(b % 3))
                    if nm == "I":
                        sp.dma_start(dst[:, :, 0:256], in_block(l, COLS["I"], 256)).then_inc(landedA[2], 16)
                        sp.dma_start(dst[:, :, 256:512], in_block(l, COLS["G"], 256)).then_inc(landedA[2], 16)
                    else:
                        sp.dma_start(dst, in_block(l, COLS[nm])).then_inc(landedA[b % 3], 16)
                for half in range(2):
                    b = 7 + half
                    until(sp, pj_done, nth(l, N_PJ, 5 * (b - 2)))
                    sp.dma_start(s3(slotA(b % 3)), out_block(l, half * W)).then_inc(landedA[b % 3], 16)
                until(sp, pj_done, nth(l, N_PJ, N_PJ))
                with sp.Fori(0, NE // 2) as i:
                    for p in range(2):
                        slot, landed = ((slotA, landedA), (slotB, landedB))[p]
                        until(sp, gate_done, nth(l, NE, i * 2 + p + PRE - 1))
                        sp.dma_start(s3(slot(0)), gate_up("w_gate", l, i * 2 + p)).then_inc(landed[0], 16)
                        until(sp, up_done, nth(l, NE, i * 2 + p + PRE - 1))
                        sp.dma_start(s3(slot(1)), gate_up("w_up", l, i * 2 + p)).then_inc(landed[1], 16)
                        until(sp, y_done, nth(l, 2 * NE, i * 4 + 2 * p + 2))
                        sp.dma_start(s3(slot(2), 4), down(l, i * 2 + p)).then_inc(landed[2], 16)
                until(sp, y_done, nth(l, 2 * NE, 2 * NE + 2 * PRE))
                until(sp, pos_ready, l + 1)
                nov = sp.value_load(novi[0:1, :], min_val=0, max_val=OVB)
                with sp.Fori(0, OVB) as j:
                    with sp.If(nov > j):
                        until(sp, ov_pe, l * (6 * OVB) + j * 6 + 1)
                        ex = sp.value_load(bexi[0:1, bass.ds(j, 1)], min_val=0, max_val=NE - 1)
                        sp.dma_start(s3(slotA(0)), gate_up("w_gate", l, ex)).then_inc(ov_w, 16)
                        sp.dma_start(s3(slotA(1)), gate_up("w_up", l, ex)).then_inc(ov_w, 16)
                        sp.dma_start(s3(slotA(2), 4), down(l, ex)).then_inc(ov_w, 16)
                        until(sp, ov_w, l * (48 * OVB) + j * 48 + 48)
                    with sp.Else():
                        sp.sem_inc(ov_w, 48)
            until(sp, x_ready, DEPTH + 1)
            sp.dma_start(A["y"].rearrange("(t p) d -> p t d", p=P), x[:]).then_inc(out_y, 16)
            until(sp, out_y, 16)
            until(sp, out_k, 16 * DEPTH)
            until(sp, out_v, 16 * DEPTH)
            until(sp, out_s, 128 * DEPTH)

        @block.tensor
        def _(pe):
            pe.sem_inc(ada_mm, 3)
            pe.wait_ge(cond_ready, 1)
            pe.wait_ge(consts, 16 * 5)
            with pe.Fori(0, 4 * DEPTH) as i:
                for j in range(3):
                    pe.wait_ge(landedA[j], i * 16 + 16)
                    pe.wait_ge(ada_free, i * 3 + j + 1)
                    w = s3(slotA(j))
                    for k in range(KD):
                        mm = pe.matmul(bank(j)[0:2, :], condT[:, k, :], w[:, k, :], start=k == 0, stop=k == KD - 1)
                    mm.then_inc(ada_mm, 1)
            pe.sem_inc(gate_done, PRE)
            pe.sem_inc(up_done, PRE)
            pe.sem_inc(y_done, 2 * PRE)
            pe.sem_inc(xT_done, 2 * PRE)
            pe.sem_inc(ov_pe, 1)
            pe.drain()
            pe.sem_inc(slots_free, 1)

            with pe.Fori(0, DEPTH) as l:
                pe.wait_ge(x_ready, l + 1)

                def tile_transposes(n, chunks):
                    for half in range(2):
                        if n > 0:
                            pe.wait_ge(tr_evac, nth(l, N_TR, 2 * n - 1 + half))
                        for q in range(4):
                            mm = pe.transpose(bank(6 + half)[:, q * P:(q + 1) * P], chunks[4 * half + q], ident)
                        mm.then_inc(tr_done, 1)

                for t in range(NT):
                    pe.wait_ge(h_ready, nth(l, 2 * NT, t + 1))
                    tile_transposes(t, [hin[:, t % 2, k * P:(k + 1) * P] for k in range(KD)])
                pe.wait_ge(tr_evac, nth(l, N_TR, 2 * NT))

                def bank_free(n):
                    if 3 <= n < N_PJA + 3:
                        pe.wait_ge(pjA, nth(l, N_PJA, n - 2))
                    elif n >= N_PJA + 3:
                        pe.wait_ge(pjV, nth(l, N_PJV, n - 2 - N_PJA))

                def landed(b):
                    pe.wait_ge(landedA[b % 3], loadsA(l, b % 3, b // 3 + 1))

                def features_unit(b, c):
                    w, n = s3(slotA(b % 3)), 5 * b + c
                    bank_free(n)
                    for cc_ in ([c] if c < 4 else range(4)):
                        out, tok = ((bank(n % 3), slice(P, T)) if c < 4
                                    else (bank(n % 3)[:, cc_ * P:(cc_ + 1) * P], slice(0, P)))
                        for k in range(KD):
                            mm = pe.matmul(out, w[:, k, cc_ * P:(cc_ + 1) * P], hT[:, k, tok],
                                           start=k == 0, stop=k == KD - 1)
                    mm.then_inc(pj_done, 1)

                def tokens_unit(b, t):
                    w, n = s3(slotA(b % 3)), 5 * b + t
                    bank_free(n)
                    for k in range(KD):
                        mm = pe.matmul(bank(n % 3), hT[:, k, t * P:(t + 1) * P], w[:, k, :],
                                       start=k == 0, stop=k == KD - 1)
                    mm.then_inc(pj_done, 1)

                for b in range(2):
                    landed(b)
                    for c in range(5):
                        features_unit(b, c)

                def U(h):
                    return psum[:, (3 + 2 * h) * 512:(3 + 2 * h) * 512 + T]

                landed(2)
                plan = [(0, [(2, t) for t in range(5)]), (2, [(3, 0), (3, 1)]), (1, [(3, 2), (3, 3)]), (3, [(3, 4)])]
                for ci, (c, units) in enumerate(plan):
                    if ci == 1:
                        landed(3)
                    for b, t in units:
                        tokens_unit(b, t)
                    pair, dr = c % 2, c // 2
                    pe.wait_ge(k_ready, nth(l, 4, ci + 1))
                    if ci == 0:
                        pe.wait_ge(pjA, nth(l, N_PJA, 10))
                    for j in range(NL + 1):
                        if j:
                            pe.wait_ge(Q_ready, nth(l, 32, 8 * ci + j))
                            pe.wait_ge(K_ready, nth(l, 32, 8 * ci + j))
                        ks, qs = (kf[:, c], qf[:, c]) if j == 0 else (Kb[:, j % 2], Qb[:, j % 2])
                        for h in range(2):
                            if j:
                                pe.wait_ge(lv_acc, nth(l, 64, 16 * ci + 2 * j - 1 + h))
                            elif ci == 2:
                                pe.wait_ge(o_evac, nth(l, 4, h + 1))
                            elif ci and h == 1:
                                pe.wait_ge(s_ready, nth(l, 4, ci))
                            r = slice(64 * h, 64 * h + 64)
                            for w in range(NT):
                                tk = slice(w * P, (w + 1) * P)
                                mm = pe.matmul(U(h)[:, tk], ks[r, tk], qs[r, tk], start=True, stop=True)
                            mm.then_inc(lv_mm, 1)
                    pe.wait_ge(K_ready, nth(l, 32, 8 * ci + 8))
                    pe.wait_ge(lv_acc, nth(l, 64, 16 * ci + 16))
                    for w in range(NT):
                        mm = pe.transpose(U(0)[:, w * P:(w + 1) * P], kf[:, c, w * P:(w + 1) * P], ident)
                    mm.then_inc(ke_t, 1)
                    pe.wait_ge(ke_evac, nth(l, 4, ci + 1))
                    for w in range(NT):
                        mm = pe.matmul(U(1)[:, w * P:(w + 1) * P], KEn[:, w, :], ig[:, w, pair * P:(pair + 1) * P],
                                       start=True, stop=True)
                    mm.then_inc(ds_mm, 1)
                    if dr == 1:
                        pe.wait_ge(s_ready, nth(l, 4, ci + 1))
                        pe.wait_ge(Q_ready, nth(l, 32, 8 * ci + 8))
                        for h in range(2):
                            r = slice(64 * h, 64 * h + 64)
                            for w in range(NT):
                                tk = slice(w * P, (w + 1) * P)
                                out = U(h)[:, tk]
                                iw = ig[:, w, pair * P:(pair + 1) * P]
                                pe.matmul(out, AT[:, 0, h, tk], iw, start=True, stop=False)
                                pe.matmul(out, AT[:, 1, h, tk], iw, start=False, stop=False)
                                ent = (0 if w == 0 else 1 + w, 1 if w == 0 else 2 + w)
                                pe.matmul(out, qf[r, pair, tk], S[r, 0, ent[0], :], start=False, stop=False)
                                mm = pe.matmul(out, qf[r, 2 + pair, tk], S[r, 1, ent[1], :], start=False, stop=True)
                            mm.then_inc(o_mm, 1)

                pe.wait_ge(v_ready, l + 1)
                pe.wait_ge(o_evac, nth(l, 4, 4))
                pe.wait_ge(prm_in, nth(l, 96, 96))
                for t in range(NT):
                    for g in range(GB):
                        out = psum[:, 1536 + t * 256 + g * 64:1536 + t * 256 + g * 64 + 64]
                        mm = pe.matmul(out, wsT[:, g, :], uv[:, t, 256 + g * 64:256 + g * 64 + 64], start=True, stop=True)
                mm.then_inc(sp_mm, 1)

                landed(4)
                for t in range(NT):
                    tokens_unit(4, t)

                def rope_transposes(u):
                    bk = bank(7 if u % 2 else 6)
                    pe.wait_ge(r_ready, nth(l, 10, u + 1))
                    if u >= 2:
                        pe.wait_ge(r_evac, nth(l, 10, u - 1))
                    for q in range(4):
                        mm = pe.transpose(bk[:, q * P:(q + 1) * P], nat[:, u % 2, q * P:(q + 1) * P], ident)
                    mm.then_inc(r_tr, 1)

                for u in range(10):
                    if u % 5 == 0:
                        landed(5 + u // 5)
                    tokens_unit(5 + u // 5, u % 5)
                    if u:
                        rope_transposes(u - 1)
                rope_transposes(9)

                def region(n):
                    return psum[:, (n % 2) * 1536:(n % 2) * 1536 + 1280]

                def keys(t):
                    return (640, 768, [5]) if t == 0 else (0, 640, list(range(5)))

                def scores(n):
                    t, h = n // 4, n % 4
                    k0, k1, _ = keys(t)
                    if n >= 2:
                        pe.wait_ge(at_evac, nth(l, 20, n - 1))
                    parts = ([(0, 0, P), (1, 0, P)] if t == 0 else
                             [(0, 512, 640), (0, 0, 512), (1, 384, 640), (1, 0, 384)])
                    for i, (m, a, b) in enumerate(parts):
                        r = slice(64 * m, 64 * m + 64)
                        if i == len(parts) - 1:
                            pe.wait_ge(sc_first, nth(l, 20, n + 1))
                        mm = pe.matmul(region(n)[:, m * 640 + a:m * 640 + b], qT[r, h, t * P:(t + 1) * P],
                                       kT[r, h, k0 + a:k0 + b], start=True, stop=True)
                        if i == 0:
                            mm.then_inc(sc_first, 1)
                    mm.then_inc(sc_done, 1)

                def probs_v(n):
                    t, h = n // 4, n % 4
                    pe.wait_ge(at_evac, nth(l, 20, n + 1))
                    if h == 0 and t >= 2:
                        pe.wait_ge(oa_evac, nth(l, NT, t - 1))
                    vs = keys(t)[2]
                    for i, s_ in enumerate(vs):
                        mm = pe.matmul(bank(6 + t % 2)[:, h * P:(h + 1) * P], pdT[:, n % 2, i * P:(i + 1) * P],
                                       vv[:, s_, h * P:(h + 1) * P], start=i == 0, stop=i == len(vs) - 1)
                    mm.then_inc(pv_done, 1)

                pe.wait_ge(r_evac, nth(l, 10, 10))
                pe.wait_ge(kv_in, nth(l, 32, 32))
                pe.wait_ge(pjA, nth(l, N_PJA, N_PJA))
                pe.wait_ge(pjV, nth(l, N_PJV, 10))
                scores(0)
                for n in range(20):
                    if n + 1 < 20:
                        scores(n + 1)
                    if n:
                        probs_v(n - 1)
                    pe.wait_ge(pd_ready, nth(l, 20, n + 1))
                    for i in range(len(keys(n // 4)[2])):
                        mm = pe.transpose(region(n)[:, i * P:(i + 1) * P], pd[:, n % 2, i * P:(i + 1) * P], ident)
                    mm.then_inc(at_tr, 1)
                probs_v(19)

                pe.wait_ge(mix_ready, l + 1)
                for t in range(NT):
                    tile_transposes(NT + t, [oa[:, t, k * P:(k + 1) * P] for k in range(4)]
                                    + [uv[:, t, k * P:(k + 1) * P] for k in range(2)]
                                    + [oc[:, t, k * P:(k + 1) * P] for k in range(2)])
                landed(7)
                landed(8)
                for t in range(NT):
                    pe.wait_ge(tr_evac, nth(l, N_TR, 2 * NT + 2 * t + 2))
                    for half in range(2):
                        n = 35 + 2 * t + half
                        if n >= 38:
                            bank_free(n)
                        w = s3(slotA((7 + half) % 3))
                        for k in range(KD):
                            mm = pe.matmul(bank(n % 3), hT[:, k, t * P:(t + 1) * P], w[:, k, :],
                                           start=k == 0, stop=k == KD - 1)
                        mm.then_inc(pj_done, 1)

                for t in range(NT):
                    pe.wait_ge(h_ready, nth(l, 2 * NT, NT + t + 1))
                    tile_transposes(2 * NT + t, [hh[:, t % 2, k * P:(k + 1) * P] for k in range(KD)])
                    pe.wait_ge(tr_evac, nth(l, N_TR, 4 * NT + 2 * t + 2))
                    for k in range(KD):
                        mm = pe.matmul(bank(3)[:, t * NE:(t + 1) * NE], hTt[:, k, :], rw[:, k, :],
                                       start=k == 0, stop=k == KD - 1)
                    mm.then_inc(rt_mm, 1)
                pe.wait_ge(m_ready, l + 1)
                M = R[0]
                for t in range(NT):
                    for u in range(t + 1):
                        tri = cst[:, C_TRI + (P if u < t else 0):C_TRI + (P if u < t else 0) + P]
                        pe.matmul(bank(4)[:, t * NE:(t + 1) * NE], tri, M[:, u, :], start=u == 0, stop=u == t)
                for u in range(NT):
                    mm = pe.matmul(bank(4)[:, 80:96], cst[:, C_TRI + P:C_TRI + 2 * P], M[:, u, :],
                                   start=u == 0, stop=u == NT - 1)
                mm.then_inc(rank_mm, 1)
                until(pe, id_row, l * 16 + 16)
                pe.transpose(bank(5)[:, 0:NB], idrow, ident[0:NB, 0:NB]).then_inc(id_tr, 1)
                until(pe, ids_ready, l + 1)

                def gather_transposed(p, src, s0, s1):
                    for half in range(2):
                        for q in range(4):
                            k = 4 * half + q
                            mm = pe.transpose(bank(6 + half)[:, q * P:(q + 1) * P], src[:, k * P:(k + 1) * P], ident)
                        mm.then_inc(s0 if half == 0 else s1, 1)

                with pe.Fori(0, NE // 2) as i:
                    for p in range(2):
                        pe.wait_ge(xg_in[p], l * 128 + i * 16 + 16)
                        if p:
                            pe.wait_ge(xT_act, nth(l, NE, i * 2 + 1))
                            pe.wait_ge(xT_dve, nth(l, NE, i * 2 + 1))
                        gather_transposed(p, xg[p], xT_done, xT_done)
                    for p in range(2):
                        landed_ = (landedA, landedB)[p]
                        slot = (slotA, slotB)[p]
                        base = [loadsA(l, j, 3) if p == 0 else l * 128 for j in range(3)]
                        pe.wait_ge(xT_act, nth(l, NE, i * 2 + p + 1))
                        pe.wait_ge(xT_dve, nth(l, NE, i * 2 + p + 1))
                        pe.wait_ge(landed_[0], base[0] + i * 16 + 16)
                        for k in range(KD):
                            mm = pe.matmul(bank(2 * p), xgT[p][:, k, :], s3(slot(0))[:, k, :],
                                           start=k == 0, stop=k == KD - 1)
                        mm.then_inc(gate_done, 1)
                        pe.wait_ge(landed_[1], base[1] + i * 16 + 16)
                        for k in range(KD):
                            mm = pe.matmul(bank(2 * p + 1), xgT[p][:, k, :], s3(slot(1))[:, k, :],
                                           start=k == 0, stop=k == KD - 1)
                        mm.then_inc(up_done, 1)
                    for p in range(2):
                        pe.wait_ge(a_ready, nth(l, NE, i * 2 + p + 1))
                        for q in range(4):
                            mm = pe.transpose(bank(6 + p)[:, q * P:(q + 1) * P], av[p][:, q * P:(q + 1) * P], ident)
                        mm.then_inc(aT_done, 1)
                        pe.wait_ge(aT_ready, nth(l, NE, i * 2 + p + 1))
                        pe.wait_ge((landedA, landedB)[p][2], (loadsA(l, 2, 3) if p == 0 else l * 128) + i * 16 + 16)
                        if p:
                            pe.wait_ge(yA_evac, nth(l, NE, i * 2 + 2))
                        else:
                            pe.wait_ge(yB_evac, nth(l, NE, i * 2 + 2))
                        for half in range(2):
                            for k in range(4):
                                mm = pe.matmul(bank(4 + half), aT[p][:, k, :],
                                               s3((slotA, slotB)[p](2), 4)[:, k, half * W:(half + 1) * W],
                                               start=k == 0, stop=k == 3)
                            mm.then_inc(y_done, 1)
                until(pe, yB_evac, nth(l, NE, NE + 2))
                nov = pe.value_load(novi[0:1, :], min_val=0, max_val=OVB)
                with pe.Fori(0, OVB) as j:
                    with pe.If(nov > j):
                        pe.wait_ge(ov_g, l * (16 * OVB) + j * 16 + 16)
                        for half in range(2):
                            for q in range(4):
                                k = 4 * half + q
                                mm = pe.transpose(bank(6 + half)[:, q * P:(q + 1) * P], xg[0][:, k * P:(k + 1) * P], ident)
                        mm.then_inc(ov_pe, 1)
                        pe.wait_ge(ov_act, l * (4 * OVB) + j * 4 + 1)
                        pe.wait_ge(ov_w, l * (48 * OVB) + j * 48 + 48)
                        for s_ in range(2):
                            for k in range(KD):
                                mm = pe.matmul(bank(s_), xgT[0][:, k, :], s3(slotA(s_))[:, k, :],
                                               start=k == 0, stop=k == KD - 1)
                            mm.then_inc(ov_pe, 1)
                        pe.wait_ge(ov_dve, l * OVB + j + 1)
                        for q in range(4):
                            mm = pe.transpose(bank(6)[:, q * P:(q + 1) * P], av[0][:, q * P:(q + 1) * P], ident)
                        mm.then_inc(ov_pe, 1)
                        pe.wait_ge(ov_act, l * (4 * OVB) + j * 4 + 3)
                        for half in range(2):
                            for k in range(4):
                                mm = pe.matmul(bank(4 + half), aT[0][:, k, :],
                                               s3(slotA(2), 4)[:, k, half * W:(half + 1) * W],
                                               start=k == 0, stop=k == 3)
                            mm.then_inc(ov_pe, 1)
                    with pe.Else():
                        pe.drain()
                        pe.sem_inc(ov_pe, 6)
                pe.drain()
                pe.sem_inc(slots_free, 1)

        @block.scalar
        def _(act):
            act.dma_start(cst[:], A["cst"]).then_inc(consts, 16)
            act.dma_start(maskf, A["masks"]).then_inc(consts, 16)
            act.dma_start(rw[:], A["w_router"].rearrange("(k p) e -> p k e", p=P)).then_inc(consts, 16)
            act.dma_start(rbias[:], rows("router_bias", 0, NE)).then_inc(consts, 16)
            act.dma_start(lbt, A["lbT"]).then_inc(consts, 16)
            act.dma_start(lamb, bass.AP(A["diff_lambda"].tensor, 0, [[0, P], [1, DEPTH * 256]])
                          .rearrange("p (l f d) -> p l f d", l=DEPTH, f=4)).then_inc(lam_in, 16)
            act.dma_start(x[:], A["x"].rearrange("(t p) d -> p t d", p=P)).then_inc(x_in, 16)
            act.wait_ge(bias_in, 32)
            act.activation(condT[:], condT[:], ACT.Silu).then_inc(cond_ready, 1)
            act.wait_ge(lbs_ready, 1)
            act.activation(lbx, lbx, ACT.Exp)
            act.activation(lams, lams, ACT.Exp).then_inc(lb_exp, 1)
            act.wait_ge(zero_ready, 2)
            act.dma_start(idt_dram.rearrange("(b r) o -> b (r o)", r=P), zrow).then_inc(zero_out, 16)
            act.dma_start(exp_dram[NE * P:, :].rearrange("(b r) d -> r b d", r=P),
                          yb[0].unsqueeze(1).to_broadcast([P, OVB, D])).then_inc(zero_out, 16)
            act.wait_ge(ada_ready, 1)
            act.dma_start(mod_dram.rearrange("l y d -> y l d"),
                          mrow.rearrange("y (l d) -> y l d", l=DEPTH)).then_inc(mod_out, 16)
            act.wait_ge(mod_out, 16)
            act.wait_ge(zero_out, 32)

            with act.Fori(0, DEPTH) as l:
                act.wait_ge(x_ready, l + 1)
                act.dma_start(ishift.rearrange("p y m d -> p y (m d)"), mod_rows(l, 0, 2)).then_inc(m01_in, 16)
                act.dma_start(gate_mod[:], mod_rows(l, 2, 1)).then_inc(m2_in, 16)
                act.dma_start(ag, rows("attn_norm_g", l * 128, 128)).then_inc(prm_in, 16)
                act.dma_start(hg, rows("hgrn_norm_g", l * 256, 256)).then_inc(prm_in, 16)
                act.dma_start(mg, rows("mlp_ln_g", l * 256, 256)).then_inc(prm_in, 16)
                act.dma_start(mb, rows("mlp_ln_b", l * 256, 256)).then_inc(prm_in, 16)
                act.dma_start(wsT.rearrange("p g i -> p (g i)"), bass.AP(A["wsT"].tensor, l * (P * 512), [[512, P], [1, 512]])).then_inc(prm_in, 16)
                act.dma_start(bsT, bass.AP(A["bsT"].tensor, l * (P * 4), [[4, P], [1, 4]])).then_inc(prm_in, 16)

                def tile_evac(n, dst):
                    for half in range(2):
                        act.wait_ge(tr_done, nth(l, N_TR, 2 * n + half + 1))
                        act.activation(dst[:, 4 * half:4 * half + 4, :],
                                       bank(6 + half).rearrange("p (k t) -> p k t", k=4), ACT.Copy).then_inc(tr_evac, 1)

                for t in range(NT):
                    tile_evac(t, hT[:, :, t * P:(t + 1) * P])

                def unit_ready(n):
                    act.wait_ge(pj_done, nth(l, N_PJ, n + 1))
                    return bank(n % 3)

                for b, dst, fn in ((0, kf, ACT.Sigmoid), (1, qf, ACT.Copy)):
                    for c in range(5):
                        pb = unit_ready(5 * b + c)
                        if c < 4:
                            a = act.activation(dst[:, c, P:T], pb, fn)
                        else:
                            a = act.activation(dst[:, :, 0:P], pb.rearrange("p (c t) -> p c t", c=4), fn)
                        a.then_inc(pjA, 1)

                plan = [(0, [10, 11, 12, 13, 14]), (2, [15, 16]), (1, [17, 18]), (3, [19])]
                for ci, (c, units) in enumerate(plan):
                    act.wait_ge(f_ready, nth(l, 4, ci + 1))
                    act.activation(gpad[:, :, 1:P + 1], gpad[:, :, 1:P + 1], ACT.Ln).then_inc(g_ready, 1)
                    if ci % 2 == 0:
                        act.wait_ge(s_zero, nth(l, 2, ci // 2 + 1))
                        for h in range(2):
                            for dr in range(2):
                                src = bass.AP(A["state"].tensor, l * 32768 + (dr * 16384 + (ci + h) * 4096), [[64, 64], [1, 64]])
                                act.dma_start(S[64 * h:64 * h + 64, dr, (2, 6)[dr], 64 * h:64 * h + 64], src).then_inc(s_init, 16)
                    for n in units:
                        pb, t = unit_ready(n), n % 5
                        if n < 15:
                            act.activation(ig[:, t, 0:256], pb[:, 0:256], ACT.Copy)
                            a = act.activation(ig[:, t, 256:512], pb[:, 256:512], ACT.Silu)
                        else:
                            a = act.activation(uv[:, t, :], pb, ACT.Gelu_apprx_tanh)
                        a.then_inc(pjA, 1)
                    for j in range(NL):
                        act.wait_ge(D_ready, nth(l, 32, 8 * ci + j + 1))
                        act.activation(Eb[:, j % 2], Eb[:, j % 2], ACT.Exp).then_inc(E_ready, 1)
                    act.wait_ge(Q_ready, nth(l, 32, 8 * ci + 6))
                    act.wait_ge(K_ready, nth(l, 32, 8 * ci + 6))
                    beta = bsum[:, c, :, 1:P + 1] if c < 2 else bsum[:, c, :, 0:P]
                    act.activation(Eb[:, 1].rearrange("p (w t) -> p w t", w=NT), beta, ACT.Exp).then_inc(E_ready, 1)
                    act.wait_ge(D_ready, nth(l, 32, 8 * ci + 8))
                    act.activation(Eb[:, 0], Eb[:, 0], ACT.Exp).then_inc(E_ready, 1)
                    act.activation(eB[:, c, :], bsum[:, c, :, P], ACT.Exp).then_inc(E_ready, 1)
                    act.wait_ge(ke_t, nth(l, 4, ci + 1))
                    act.activation(KEn.rearrange("p w d -> p (w d)"), psum[:, 1536:1536 + T], ACT.Copy).then_inc(ke_evac, 1)
                    if c >= 2:
                        act.wait_ge(s_ready, nth(l, 4, ci + 1))
                        for h in range(2):
                            for dr in range(2):
                                dst = bass.AP(A["new_s"].tensor, l * 32768 + (dr * 16384 + (c - 2 + c - 2 + h) * 4096), [[64, 64], [1, 64]])
                                act.dma_start(dst, S[64 * h:64 * h + 64, dr, (1, 0)[dr], 64 * h:64 * h + 64]).then_inc(out_s, 16)

                act.wait_ge(hg_done, l + 1)
                act.wait_ge(out_s, l * 128 + 128)
                act.dma_start(kT[:, :, 0:P], bass.AP(A["kcT"].tensor, l * 65536, [[512, P], [P, 4], [1, P]])).then_inc(kv_in, 16)
                act.dma_start(vv[:, 0, :], bass.AP(A["cache_v"].tensor, l * 65536, [[512, P], [1, 512]])).then_inc(kv_in, 16)
                for t in range(NT):
                    pb = unit_ready(20 + t)
                    act.activation(vv[:, 5 if t == 0 else t, :], pb, ACT.Copy).then_inc(pjA, 1)
                act.wait_ge(pjA, nth(l, N_PJA, 21))
                act.dma_start(bass.AP(A["new_v"].tensor, l * 65536, [[512, P], [1, 512]]), vv[:, 5, :]).then_inc(out_v, 16)
                for u in range(10):
                    if u == 0:
                        act.wait_ge(r_ready, nth(l, 10, 1))
                        act.dma_start(bass.AP(A["new_k"].tensor, l * 65536, [[512, P], [1, 512]]), nat[:, 0, :]).then_inc(out_k, 16)
                    act.wait_ge(r_tr, nth(l, 10, u + 1))
                    t = u % 5
                    if u < 5:
                        k0 = 640 if t == 0 else t * P
                        dst = kT[:, :, k0:k0 + P]
                    else:
                        dst = qT[:, :, t * P:(t + 1) * P]
                    act.activation(dst, bank(7 if u % 2 else 6).rearrange("p (h t) -> p h t", h=HA), ACT.Copy).then_inc(r_evac, 1)

                def exps(n):
                    nk = P if n < 4 else T
                    act.wait_ge(nm_ready, nth(l, 20, n + 1))
                    for m in range(2):
                        a = act.activation(Pb[:, n % 2, m, 0:nk], psum[:, (n % 2) * 1536 + m * 640:(n % 2) * 1536 + m * 640 + nk],
                                           ACT.Exp, bias=negm[:, 2 * n + m:2 * n + m + 1], scale=SCALE,
                                           accum_out=Z[:, 2 * n + m:2 * n + m + 1])
                    a.then_inc(p_ready, 1)

                exps(0)
                for n in range(20):
                    nk = P if n < 4 else T
                    if n + 1 < 20:
                        exps(n + 1)
                    act.wait_ge(at_tr, nth(l, 20, n + 1))
                    if n >= 2:
                        act.wait_ge(pv_done, nth(l, 20, n - 1))
                    act.activation(pdT[:, n % 2, 0:nk], psum[:, (n % 2) * 1536:(n % 2) * 1536 + nk], ACT.Copy).then_inc(at_evac, 1)

                act.wait_ge(mix_ready, l + 1)
                act.dma_start(lnb[:, 0, :], rows("ln_g", l * 2048, D)).then_inc(ln1_in, 16)
                act.dma_start(lnb[:, 1, :], rows("ln_b", l * 2048, D)).then_inc(ln1_in, 16)
                act.dma_start(shift2.rearrange("p y m d -> p y (m d)"), mod_rows(l, 3, 2)).then_inc(m34_in, 16)
                for t in range(NT):
                    tile_evac(NT + t, hT[:, :, t * P:(t + 1) * P])
                act.wait_ge(pjV, nth(l, N_PJV, N_PJV))
                act.dma_start(gate_mod[:], mod_rows(l, 5, 1)).then_inc(m5_in, 16)
                for t in range(NT):
                    act.wait_ge(h_ready, nth(l, 2 * NT, NT + t + 1))
                    act.dma_start(tok_dram[t * P:(t + 1) * P, :], hh[:, t % 2, :]).then_inc(h_stored[t % 2], 16)
                    if t:
                        act.wait_ge(rt_mm, nth(l, NT, t))
                    tile_evac(2 * NT + t, hTt)
                act.wait_ge(x1_ready, l + 1)
                act.dma_start(lnb[:, 0, :], rows("ln_g", l * 2048 + D, D)).then_inc(ln2_in, 16)
                act.dma_start(lnb[:, 1, :], rows("ln_b", l * 2048 + D, D)).then_inc(ln2_in, 16)
                act.wait_ge(rt_mm, nth(l, NT, NT))
                act.activation(score.rearrange("p t e -> p (t e)"), bank(3)[:, 0:80], ACT.Sigmoid).then_inc(rt_score, 1)

                with act.Fori(0, NE // 2) as i:
                    for p in range(2):
                        act.wait_ge(xT_done, nth(l, 2 * NE, i * 4 + 2 * p + 1 + 2 * PRE))
                        act.activation(xgT[p][:, 0:4, :], bank(6).rearrange("p (k t) -> p k t", k=4), ACT.Copy).then_inc(xT_act, 1)
                    for p in range(2):
                        act.wait_ge(gate_done, nth(l, NE, i * 2 + p + 1 + PRE))
                        act.activation(sg[p], bank(2 * p), ACT.Silu).then_inc(sg_ready, 1)
                    for p in range(2):
                        act.wait_ge(aT_done, nth(l, NE, i * 2 + p + 1))
                        act.activation(aT[p], bank(6 + p).rearrange("p (k t) -> p k t", k=4), ACT.Copy).then_inc(aT_ready, 1)
                    act.wait_ge(yA_evac, nth(l, NE, i * 2 + 2))
                    act.dma_start(bass.AP(exp_dram.tensor, i * (2 * P * D), [[D, P], [1, D]]), yb[0]).then_inc(y_stored[0], 16)
                    for half in range(2):
                        act.wait_ge(y_done, nth(l, 2 * NE, i * 4 + 3 + half + 2 * PRE))
                        if half == 0:
                            act.wait_ge(y_stored[1], l * 128 + i * 16 + 16)
                        act.activation(yb[1][:, half * W:(half + 1) * W], bank(4 + half), ACT.Copy).then_inc(yB_evac, 1)
                    act.wait_ge(yB_evac, nth(l, NE, i * 2 + 2 + 2))
                    act.dma_start(bass.AP(exp_dram.tensor, i * (2 * P * D) + P * D, [[D, P], [1, D]]), yb[1]).then_inc(y_stored[1], 16)

                until(act, y_stored[0], l * 128 + 144)
                until(act, pos_ready, l + 1)
                nov = act.value_load(novi[0:1, :], min_val=0, max_val=OVB)
                with act.Fori(0, OVB) as j:
                    with act.If(nov > j):
                        act.wait_ge(ov_pe, l * (6 * OVB) + j * 6 + 2)
                        act.activation(xgT[0], psum[:, 3072:4096].rearrange("p (k t) -> p k t", k=KD), ACT.Copy).then_inc(ov_act, 1)
                        act.wait_ge(ov_pe, l * (6 * OVB) + j * 6 + 3)
                        act.activation(sg[0], bank(0), ACT.Silu).then_inc(ov_act, 1)
                        act.wait_ge(ov_pe, l * (6 * OVB) + j * 6 + 5)
                        act.activation(aT[0], bank(6).rearrange("p (k t) -> p k t", k=4), ACT.Copy).then_inc(ov_act, 1)
                        act.wait_ge(ov_pe, l * (6 * OVB) + j * 6 + 7)
                        act.activation(yb[0], psum[:, 2048:3072], ACT.Copy).then_inc(ov_act, 1)
                        act.wait_ge(ov_act, l * (4 * OVB) + j * 4 + 4)
                        act.dma_start(bass.AP(exp_dram.tensor, j * (P * D) + NE * P * D, [[D, P], [1, D]]), yb[0]).then_inc(ov_st, 16)
                        until(act, ov_st, l * (16 * OVB) + j * 16 + 16)
                    with act.Else():
                        act.drain()
                        act.sem_inc(ov_act, 4)
                        act.sem_inc(ov_st, 16)

        @block.gpsimd
        def _(gp):
            gp.memset(mhalf, -0.5)
            gp.memset(zrow, 0.0).then_inc(zero_ready, 1)
            gp.memset(yb[0], 0.0).then_inc(zero_ready, 1)
            with gp.Fori(0, DEPTH) as l:
                until(gp, x_ready, l + 1)

                def inv_sqrt(n, dst, src):
                    until(gp, var_ready, nth(l, 5, n))
                    gp.tensor_scalar(dst, src, EPS, None, ALU.add)
                    gp.drain()
                    gp.tensor_tensor(dst, dst, mhalf[:, 0:dst.shape[1]], ALU.pow).then_inc(rstd_ready, 1)

                order = [0, 2, 1, 3]
                for ci, c in enumerate(order):
                    if ci % 2 == 0:
                        if ci:
                            until(gp, o_mm, nth(l, 4, 2))
                        else:
                            until(gp, tr_done, nth(l, N_TR, 10))
                        gp.memset(AT2, 0.0).then_inc(at_zero, 1)
                    until(gp, k_ready, nth(l, 4, ci + 1))
                    for j in range(1, NL + 1):
                        until(gp, E_ready, nth(l, 40, 10 * ci + j))
                        if ci or j > 1:
                            until(gp, lv_mm, nth(l, 64, 16 * ci + 2 * j - 2))
                        gp.tensor_tensor(Kb[:, j % 2], kf[:, c], Eb[:, (j - 1) % 2], ALU.mult).then_inc(K_ready, 1)
                    until(gp, E_ready, nth(l, 40, 10 * ci + (9 if c < 2 else 8)))
                    until(gp, K_ready, nth(l, 32, 8 * ci + 7))
                    gp.tensor_tensor(kf[:, c], kf[:, c], Eb[:, 0 if c < 2 else 1], ALU.mult).then_inc(K_ready, 1)
                inv_sqrt(1, rstd, mv[:, :, 1])
                inv_sqrt(2, rs, ms)
                inv_sqrt(3, rs, ms)
                inv_sqrt(4, rstd, mv[:, :, 1])
                until(gp, pos_ready, l + 1)
                for t in range(NT):
                    for q in range(2):
                        gp.indirect_dma_start(idt_dram, bass.IndirectOffsetOnAxis(ap=posi[:, t, q:q + 1], axis=0),
                                              cst[:, C_TOK + t:C_TOK + t + 1], None).then_inc(id_scat, 16)
                until(gp, id_scat, l * 160 + 160)
                until(gp, h_stored[0], l * 48 + 48)
                until(gp, h_stored[1], l * 32 + 32)
                gp.dma_start(idrow, idt_dram.rearrange("(b r) o -> b (r o)", r=P)).then_inc(id_row, 16)
                until(gp, ids_ready, l + 1)
                with gp.Fori(0, NE // 2) as i:
                    for p in range(2):
                        until(gp, xT_done, nth(l, 2 * NE, i * 4 + 2 * p + 2))
                        gp.tensor_copy(ismall[:, 60 + p:61 + p], ismall[:, bass.ds(i * 2 + (10 + p), 1)])
                        gp.drain()
                        gp.indirect_dma_start(xg[p], None, tok_dram,
                                              bass.IndirectOffsetOnAxis(ap=ismall[:, 60 + p:61 + p], axis=0)).then_inc(xg_in[p], 16)
                until(gp, xT_done, nth(l, 2 * NE, 2 * NE + 2 * PRE))
                nov = gp.value_load(novi[0:1, :], min_val=0, max_val=OVB)
                with gp.Fori(0, OVB) as j:
                    with gp.If(nov > j):
                        until(gp, ov_pe, l * (6 * OVB) + j * 6 + 1)
                        gp.tensor_copy(ismall[:, 62:63], ismall[:, bass.ds(j + (10 + NE), 1)])
                        gp.drain()
                        gp.indirect_dma_start(xg[0], None, tok_dram,
                                              bass.IndirectOffsetOnAxis(ap=ismall[:, 62:63], axis=0)).then_inc(ov_g, 16)
                    with gp.Else():
                        gp.dma_start(spare[0:1, bass.ds(j, 1)], idt_dram[0:1, :]).then_inc(ov_g, 16)
                    until(gp, ov_g, l * (16 * OVB) + j * 16 + 16)
                until(gp, y_stored[0], l * 128 + 144)
                until(gp, y_stored[1], l * 128 + 144)
                until(gp, ov_st, l * (16 * OVB) + 16 * OVB)
                for t in range(NT):
                    if t >= 2:
                        until(gp, cmb_used, nth(l, NT, t - 1))
                    for q, dst in enumerate((xg[t % 2], yb[t % 2])):
                        gp.indirect_dma_start(dst, None, exp_dram,
                                              bass.IndirectOffsetOnAxis(ap=posi[:, t, q:q + 1], axis=0)).then_inc(cmb_in[t % 2], 16)
                inv_sqrt(5, rstd, mv[:, :, 1])

        @block.vector
        def _(v):
            dr_ = v.drain

            def tt(out, a, b, op=ALU.mult):
                return v.tensor_tensor(out, a, b, op)

            def ts(out, a, s1, s2=None, op0=ALU.mult, op1=ALU.add):
                return v.tensor_scalar(out, a, s1, s2, op0) if s2 is None else v.tensor_scalar(out, a, s1, s2, op0, op1)

            def stt(out, a, s, b, op0, op1):
                return v.scalar_tensor_tensor(out, a, s, b, op0, op1)

            v.wait_ge(consts, 80)
            v.wait_ge(lam_in, 16)
            v.tensor_copy(masks[:], maskf)
            v.tensor_copy(lbm, lbt[:, 0, :])
            for l_ in range(1, DEPTH):
                dr_()
                tt(lbm, lbm, lbt[:, l_, :], ALU.max)
            dr_()
            tt(lbx, lbt, lbm.unsqueeze(1).to_broadcast([P, DEPTH, 4]), ALU.subtract)
            tt(lamp[:, :, 0, :], lamb[:, :, 0, :], lamb[:, :, 1, :])
            tt(lamp[:, :, 1, :], lamb[:, :, 2, :], lamb[:, :, 3, :])
            dr_()
            v.tensor_reduce(lams.rearrange("p (l f) -> p l f", l=DEPTH), lamp, AXX, ALU.add).then_inc(lbs_ready, 1)
            v.wait_ge(lb_exp, 1)
            v.tensor_copy(lbm, lbx[:, 0, :])
            for l_ in range(1, DEPTH):
                dr_()
                tt(lbm, lbm, lbx[:, l_, :], ALU.add)
            dr_()
            v.reciprocal(lbm, lbm)
            dr_()
            tt(lbx, lbx, lbm.unsqueeze(1).to_broadcast([P, DEPTH, 4]))
            v.memset(lbt[:, 0, :], 0.0)
            for l_ in range(1, DEPTH):
                dr_()
                tt(lbt[:, l_, :], lbt[:, l_ - 1, :], lbx[:, l_, :], ALU.add)
            for l_ in range(DEPTH):
                dr_()
                tt(lamn[:, l_:l_ + 1], lams[:, 2 * l_ + 1:2 * l_ + 2], lams[:, 2 * l_:2 * l_ + 1], ALU.subtract)
                dr_()
                ts(lamn[:, l_:l_ + 1], lamn[:, l_:l_ + 1], -lam_init(l_), None, ALU.add)
                v.memset(oml[:, l_:l_ + 1], 1.0 - lam_init(l_))
            v.sem_inc(ada_free, 3)
            v.wait_ge(bias_in, 32)
            with v.Fori(0, 4 * DEPTH) as i:
                for j in range(3):
                    v.wait_ge(ada_mm, i * 3 + j + 4)
                    m_ = ar[0:2, bass.ds(i * (3 * W) + j * W, W)]
                    tt(m_, m_, bank(j)[0:2, :], ALU.add).then_inc(ada_free, 1)
            dr_()
            v.sem_inc(ada_ready, 1)
            v.wait_ge(mod_out, 16)
            v.sem_inc(yB_evac, 2)
            v.sem_inc(y_stored[0], 16)
            v.sem_inc(y_stored[1], 16)
            v.wait_ge(x_in, 16)
            v.sem_inc(x_ready, 1)

            with v.Fori(0, DEPTH) as l:
                dr_()
                v.tensor_copy(lb, lbt[:, bass.ds(l, 1), :].rearrange("p l c -> p (l c)"))
                v.tensor_copy(lamn_l, lamn[:, bass.ds(l, 1)])
                v.tensor_copy(oml_l, oml[:, bass.ds(l, 1)])
                dr_()
                ts(omlb, lb, -1.0, 1.0)
                dr_()
                ts(nomlb, omlb, -1.0)

                def modulated(dst, t, m):
                    y = 0 if t == 0 else 1
                    stt(dst, m[:, y, 1, :], 1.0, x[:, t, :], ALU.add, ALU.mult)
                    dr_()
                    return tt(dst, dst, m[:, y, 0, :], ALU.add)

                v.wait_ge(m01_in, l * 16 + 16)
                for t in range(NT):
                    if t >= 2:
                        v.wait_ge(tr_done, nth(l, N_TR, 2 * (t - 1)))
                    modulated(hin[:, t % 2, :], t, ishift).then_inc(h_ready, 1)

                dr_()
                v.wait_ge(tr_done, nth(l, N_TR, 10))
                v.memset(gpad[:, :, 0:1], 0.0)
                v.wait_ge(prm_in, nth(l, 96, 96))
                ts(ag, ag, oml_l)
                order = [0, 2, 1, 3]

                def w5(ap):
                    return ap.rearrange("p (w t) -> p w t", w=NT)

                def distance(c, j, dst):
                    m = LEVELS[j]
                    nb = P // (2 * m)
                    b0 = 1 if c < 2 else 0
                    beta = bsum[:, c, :, b0:b0 + P].rearrange("p w (b u m) -> p w b u m", b=nb, u=2)
                    out = dst.rearrange("p (w b u m) -> p w b u m", w=NT, b=nb, u=2)
                    mid = bsum[:, c, :, 1:P + 1].rearrange("p w (b u m) -> p w b u m", b=nb, u=2)[:, :, :, 0, m - 1:m]
                    midb = mid.to_broadcast([P, NT, nb, m])
                    tt(out[:, :, :, 1, :], beta[:, :, :, 1, :], midb, ALU.subtract)
                    return tt(out[:, :, :, 0, :], midb, beta[:, :, :, 0, :], ALU.subtract)

                for ci, c in enumerate(order):
                    pair, dr = c % 2, c // 2
                    if ci == 0:
                        until(v, pjA, nth(l, N_PJA, 5))
                    if ci % 2 == 0:
                        if ci:
                            until(v, o_mm, nth(l, 4, 2))
                            until(v, out_s, l * 128 + 64)
                        dr_()
                        v.memset(S2, 0.0)
                        dr_()
                        v.sem_inc(s_zero, 1)
                    dr_()
                    ts(gpad[:, :, 1:P + 1], w5(kf[:, c]), omlb[:, c:c + 1], lb[:, c:c + 1]).then_inc(f_ready, 1)
                    dr_()
                    ts(kf[:, c], kf[:, c], nomlb[:, c:c + 1], omlb[:, c:c + 1]).then_inc(k_ready, 1)
                    v.wait_ge(g_ready, nth(l, 4, ci + 1))
                    v.tensor_tensor_scan(bsum2[:, c], cst[:, C_SCAN:C_SCAN + BW], gpad2, 0.0, ALU.mult, ALU.add)
                    dr_()
                    if ci:
                        v.wait_ge(K_ready, nth(l, 32, 8 * ci))
                    distance(c, 0, Eb[:, 0]).then_inc(D_ready, 1)
                    distance(c, 1, Eb[:, 1]).then_inc(D_ready, 1)
                    if ci % 2 == 0:
                        until(v, at_zero, nth(l, 2, ci // 2 + 1))

                    def take(j):
                        mk = masks[:, 0 if j == 0 else dr * NL + j, :].unsqueeze(1).to_broadcast([P, NT, P])
                        for h in range(2):
                            dr_()
                            until(v, lv_mm, nth(l, 64, 16 * ci + 2 * j + h + 1))
                            v.copy_predicated(w5(AT[:, dr, h, :]), mk,
                                              w5(psum[:, (3 + 2 * h) * 512:(3 + 2 * h) * 512 + T])).then_inc(lv_acc, 1)

                    if ci == 0:
                        v.wait_ge(pjA, nth(l, N_PJA, 10))
                    for j in range(1, NL + 1):
                        v.wait_ge(E_ready, nth(l, 40, 10 * ci + j))
                        if ci or j > 1:
                            v.wait_ge(lv_mm, nth(l, 64, 16 * ci + 2 * j - 2))
                        tt(Qb[:, j % 2], qf[:, c], Eb[:, (j - 1) % 2]).then_inc(Q_ready, 1)
                        take(j - 1)
                        if j + 1 < NL:
                            dr_()
                            v.wait_ge(K_ready, nth(l, 32, 8 * ci + j))
                            distance(c, j + 1, Eb[:, (j + 1) % 2]).then_inc(D_ready, 1)
                    take(NL)
                    dr_()
                    v.wait_ge(K_ready, nth(l, 32, 8 * ci + 7))
                    b0 = 1 if c < 2 else 0
                    tt(w5(Eb[:, 0]), bsum[:, c, :, P:P + 1].to_broadcast([P, NT, P]), bsum[:, c, :, b0:b0 + P],
                       ALU.subtract).then_inc(D_ready, 1)
                    v.wait_ge(E_ready, nth(l, 40, 10 * ci + (8 if c < 2 else 9)))
                    tt(qf[:, c], qf[:, c], Eb[:, 1 if c < 2 else 0]).then_inc(Q_ready, 1)
                    v.wait_ge(E_ready, nth(l, 40, 10 * ci + 10))
                    v.wait_ge(ds_mm, nth(l, 4, ci + 1))
                    if ci % 2 == 0:
                        v.wait_ge(s_init, l * 128 + 64 * (ci // 2 + 1))
                    for w in ([0, 1, 2, 3] if dr == 0 else [0, 4, 3, 2]):
                        ent = (0 if w == 0 else 1 + w) if dr == 0 else (1 if w == 0 else 2 + w)
                        nxt = ent + 1 if dr == 0 else ent - 1
                        st = stt(S[:, dr, nxt, :], S[:, dr, ent, :], eB[:, c, w:w + 1],
                                 psum[:, 2560 + w * P:2560 + (w + 1) * P], ALU.mult, ALU.add)
                        dr_()
                    v.sem_inc(s_ready, 1)
                    if dr == 1:
                        for h in range(2):
                            v.wait_ge(o_mm, nth(l, 4, 2 * pair + h + 1))
                            c0 = (3 + 2 * h) * 512
                            v.tensor_copy(oc[:, :, (2 * pair + h) * 64:(2 * pair + h) * 64 + 64],
                                          w5(psum[:, c0:c0 + T])[:, :, 64 * h:64 * h + 64]).then_inc(o_evac, 1)

                v.wait_ge(pjA, nth(l, N_PJA, 20))
                vv_ = uv[:, :, 256:512]
                for t in range(NT):
                    v.bn_stats(stats[:, t, 0, :], uv[:, t, 256:512])
                dr_()
                for t in range(NT):
                    v.bn_aggr(mv[:, t, :], stats[:, t, 0, :])
                dr_()
                v.sem_inc(var_ready, 1)
                v.wait_ge(rstd_ready, nth(l, 5, 1))
                for t in range(NT):
                    ts(uv[:, t, 256:512], uv[:, t, 256:512], mv[:, t, 0:1], rstd[:, t:t + 1], ALU.subtract, ALU.mult)
                dr_()
                tt(vv_, vv_, mg.unsqueeze(1).to_broadcast([P, NT, 256]))
                dr_()
                tt(vv_, vv_, mb.unsqueeze(1).to_broadcast([P, NT, 256]), ALU.add).then_inc(v_ready, 1)
                sq = view(HG + 8345, 1280, "p (t c) -> p t c", t=NT)
                sq4 = view(HG + 8345, 1280, "p (t h e) -> p (t h) e", t=NT, h=HC)
                oc4 = view(24860, 1280, "p (g e) -> p g e", e=64)
                tt(sq, oc, oc)
                dr_()
                v.tensor_reduce(ms, sq4, AXX, ALU.add)
                dr_()
                ts(ms, ms, 1.0 / 64)
                dr_()
                v.sem_inc(var_ready, 1)
                v.wait_ge(rstd_ready, nth(l, 5, 2))
                tt(oc4, oc4, rs.unsqueeze(2).to_broadcast([P, 20, 64]))
                dr_()
                tt(oc, oc, hg.unsqueeze(1).to_broadcast([P, NT, 256]))
                dr_()
                tt(oc, oc, ig[:, :, 256:512])
                v.wait_ge(sp_mm, l + 1)
                for g in range(GB):
                    c0 = 1536 + g * 64
                    src = psum[:, 1536:2816].rearrange("p (t c) -> p t c", t=NT)[:, :, g * 64:g * 64 + 64]
                    ug = uv[:, :, g * 64:g * 64 + 64]
                    stt(ug, src, bsT[:, g:g + 1], ug, ALU.add, ALU.mult)
                dr_()
                v.sem_inc(hg_done, 1)

                v.wait_ge(out_s, l * 128 + 128)
                for u in range(10):
                    t = u % 5
                    n = 25 + u
                    if u >= 2:
                        v.wait_ge(r_tr, nth(l, 10, u - 1))
                    if u == 2:
                        v.wait_ge(out_k, l * 16 + 16)
                    v.wait_ge(pj_done, nth(l, N_PJ, n + 1))
                    pb = bank(n % 3)
                    dst = nat[:, u % 2, :]
                    if t == 0:
                        v.tensor_copy(dst, pb).then_inc(pjV, 1)
                        dr_()
                        v.sem_inc(r_ready, 1)
                        continue
                    cos = cst[:, C_COS + (t - 1) * 64:C_COS + t * 64]
                    sin = cst[:, C_SIN + (t - 1) * 64:C_SIN + t * 64]
                    tt(dst.rearrange("p (g d) -> p g d", g=8), pb.rearrange("p (g d) -> p g d", g=8),
                       cos.unsqueeze(1).to_broadcast([P, 8, 64]))
                    dr_()
                    for s_ in range(2):
                        src = pb.rearrange("p (g a s e) -> p g a s e", g=8, a=2, s=2)[:, :, :, 1 - s_, :]
                        sn = sin.rearrange("p (a s e) -> p a s e", a=2, s=2)[:, :, s_, :]
                        out = ropeb.rearrange("p (g a s e) -> p g a s e", g=8, a=2, s=2)[:, :, :, s_, :]
                        r_ = tt(out, src, sn.unsqueeze(1).to_broadcast([P, 8, 2, 16]))
                    r_.then_inc(pjV, 1)
                    dr_()
                    tt(dst, dst, ropeb, ALU.add).then_inc(r_ready, 1)

                def maxima(n):
                    nk = P if n < 4 else T
                    v.wait_ge(sc_done, nth(l, 20, n + 1))
                    c0 = (n % 2) * 1536
                    v.tensor_reduce(nmx, psum[:, c0:c0 + 1280].rearrange("p (m k) -> p m k", m=2)[:, :, 0:nk], AXX, ALU.max)
                    dr_()
                    ts(negm[:, 2 * n:2 * n + 2], nmx, -SCALE).then_inc(nm_ready, 1)
                    dr_()

                dr_()
                maxima(0)
                for n in range(20):
                    nk = P if n < 4 else T
                    if n + 1 < 20:
                        maxima(n + 1)
                    v.wait_ge(p_ready, nth(l, 20, n + 1))
                    v.reciprocal(rZ[:, 2 * n:2 * n + 2], Z[:, 2 * n:2 * n + 2])
                    dr_()
                    stt(cc[:, n:n + 1], Z[:, 2 * n:2 * n + 1], lamn_l, rZ[:, 2 * n + 1:2 * n + 2], ALU.mult, ALU.mult)
                    dr_()
                    if n >= 2:
                        v.wait_ge(at_tr, nth(l, 20, n - 1))
                    stt(pd[:, n % 2, 0:nk], Pb[:, n % 2, 1, 0:nk], cc[:, n:n + 1], Pb[:, n % 2, 0, 0:nk],
                        ALU.mult, ALU.add).then_inc(pd_ready, 1)
                    t = n // 4 - 1
                    if n % 4 == 1 and t >= 0 or n == 19:
                        for t in ([t] if n < 19 else [4]):
                            until(v, pv_done, nth(l, 20, 4 * t + 4))
                            rz0 = rZ[:, 8 * t:8 * t + 8].rearrange("p (h m) -> p h m", h=HA)[:, :, 0:1]
                            dr_()
                            tt(oa[:, t, :].rearrange("p (h e) -> p h e", h=HA),
                               bank(6 + t % 2).rearrange("p (h e) -> p h e", h=HA),
                               rz0.to_broadcast([P, HA, P])).then_inc(oa_evac, 1)
                dr_()
                sqa = view(HG + 13824, 2560, "p (t c) -> p t c", t=NT)
                tt(sqa, oa, oa)
                dr_()
                v.tensor_reduce(ms, view(HG + 13824, 2560, "p (g e) -> p g e", g=20), AXX, ALU.add)
                dr_()
                ts(ms, ms, 1.0 / P)
                dr_()
                v.sem_inc(var_ready, 1)
                v.wait_ge(rstd_ready, nth(l, 5, 3))
                oa4 = view(HG + 8704, 2560, "p (g e) -> p g e", g=20)
                tt(oa4, oa4, rs.unsqueeze(2).to_broadcast([P, 20, P]))
                dr_()
                tt(oa4, oa4, ag.unsqueeze(1).to_broadcast([P, 20, P])).then_inc(mix_ready, 1)

                def layer_norm(n, landed, each):
                    dr_()
                    for t in range(NT):
                        v.bn_aggr(mv[:, t, :], stats[:, t, :, :].rearrange("p s f -> p (s f)"))
                    dr_()
                    v.sem_inc(var_ready, 1)
                    v.wait_ge(landed, l * 32 + 32)
                    v.wait_ge(rstd_ready, nth(l, 5, n))
                    for t in range(NT):
                        ts(x[:, t, :], x[:, t, :], mv[:, t, 0:1], rstd[:, t:t + 1], ALU.subtract, ALU.mult)
                        dr_()
                        tt(x[:, t, :], x[:, t, :], lnb[:, 0, :])
                        dr_()
                        tt(x[:, t, :], x[:, t, :], lnb[:, 1, :], ALU.add)
                        dr_()
                        each(t)

                until(v, m2_in, l * 16 + 16)
                for t in range(NT):
                    y = 0 if t == 0 else 1
                    for half in range(2):
                        n = 35 + 2 * t + half
                        cs = slice(half * W, (half + 1) * W)
                        dr_()
                        v.wait_ge(pj_done, nth(l, N_PJ, n + 1))
                        tt(x1t[half], bank(n % 3), gate_mod[:, y, cs]).then_inc(pjV, 1)
                        dr_()
                        stt(x[:, t, cs], x[:, t, cs], ALPHA, x1t[half], ALU.mult, ALU.add)
                        dr_()
                        v.bn_stats(stats[:, t, half, :], x[:, t, cs])

                until(v, m34_in, l * 16 + 16)

                def moe_input(t):
                    if t >= 2:
                        v.wait_ge(tr_done, nth(l, N_TR, 4 * NT + 2 * (t - 1)))
                        v.wait_ge(h_stored[t % 2], (l * 48 if t % 2 == 0 else l * 32) + 16 * (t // 2))
                    modulated(hh[:, t % 2, :], t, shift2).then_inc(h_ready, 1)

                layer_norm(4, ln1_in, moe_input)
                dr_()
                v.sem_inc(x1_ready, 1)

                M, oh1, oh2, sel, key, eq, inm, pos, t1, t2 = R[0], R[1], R[2], R[3], R[4], R[5], R[6], R[7], R[8], R[9]
                g4 = [view(25884 + 800 + 20 * i, 20, "p (t g) -> p t g", t=NT) for i in range(8)]

                def over(v1, n=NE):
                    return v1.unsqueeze(1).to_broadcast([P, NT, n])

                def each_of(vt, n=NE):
                    return vt.to_broadcast([P, NT, n])

                v.wait_ge(rt_score, l + 1)
                tt(sel, score, over(rbias[:]), ALU.add)
                dr_()
                s4 = sel.rearrange("p t (g e) -> p (t g) e", g=4)

                def col(i):
                    return s4[:, :, i]

                def f(i):
                    return g4[i].rearrange("p t g -> p (t g)")

                tt(f(0), col(0), col(1), ALU.max)
                tt(f(1), col(0), col(1), ALU.min)
                tt(f(2), col(2), col(3), ALU.max)
                tt(f(3), col(2), col(3), ALU.min)
                dr_()
                tt(f(4), f(0), f(2), ALU.max)
                tt(f(5), f(0), f(2), ALU.min)
                tt(f(6), f(1), f(3), ALU.max)
                dr_()
                tt(f(5), f(5), f(6), ALU.max)
                dr_()
                tt(gt, g4[4], g4[5], ALU.add)
                dr_()

                def first_best(val, n, wts, best, eq_, onehot):
                    v.tensor_reduce(best, val, AXX, ALU.max)
                    dr_()
                    tt(eq_, val, best.unsqueeze(2).to_broadcast([P, NT, n]), ALU.is_equal)
                    dr_()
                    tt(eq_, eq_, over(wts, n))
                    dr_()
                    v.tensor_reduce(best, eq_, AXX, ALU.max)
                    dr_()
                    tt(onehot, eq_, best.unsqueeze(2).to_broadcast([P, NT, n]), ALU.is_equal)
                    dr_()

                bst = wsum
                first_best(gt, 4, cst[:, C_W4:C_W4 + 4], bst, g4[0], g4[1])
                inm4 = inm.rearrange("p t (g e) -> p (t g) e", g=4)
                v.tensor_copy(inm4, f(1).unsqueeze(2).to_broadcast([P, 20, 4]))
                dr_()
                tt(sel, sel, inm)
                ts(t1, inm, NEG, -NEG)
                dr_()
                tt(sel, sel, t1, ALU.add)
                dr_()
                first_best(sel, NE, cst[:, C_W16:C_W16 + NE], bst, key, oh1)
                stt(sel, oh1, -2 * NEG, sel, ALU.mult, ALU.add)
                dr_()
                first_best(sel, NE, cst[:, C_W16:C_W16 + NE], bst, key, oh2)
                tt(M, oh1, oh2, ALU.add).then_inc(m_ready, 1)
                for q, oh in enumerate((oh1, oh2)):
                    dr_()
                    tt(t1, oh, score)
                    dr_()
                    v.tensor_reduce(wt[:, :, q], t1, AXX, ALU.add)
                dr_()
                tt(wsum, wt[:, :, 0], wt[:, :, 1], ALU.add)
                dr_()
                v.reciprocal(wsum, wsum)
                dr_()
                tt(wt, wt, wsum.unsqueeze(2).to_broadcast([P, NT, 2]))
                v.wait_ge(rank_mm, l + 1)
                rank = bank(4)[:, 0:80].rearrange("p (t e) -> p t e", t=NT)
                cnt = bank(4)[:, 80:96]
                ts(ovc, cnt, 128.0, None, ALU.is_gt)
                for r_ in (256.0, 384.0, 512.0):
                    dr_()
                    stt(ovc, cnt, r_, ovc, ALU.is_gt, ALU.add)
                dr_()
                v.tensor_tensor_scan(ovi, cst[:, C_TRI + P:C_TRI + P + NE], ovc, 0.0, ALU.mult, ALU.add)
                dr_()
                tt(ovx, ovi, ovc, ALU.subtract)
                v.tensor_copy(novi, ovi[:, NE - 1:NE])
                tt(R9, ovi.unsqueeze(1).to_broadcast([P, OVB, NE]),
                   cst[:, C_J:C_J + OVB].unsqueeze(2).to_broadcast([P, OVB, NE]), ALU.is_le)
                dr_()
                v.tensor_reduce(R9s, R9, AXX, ALU.add)
                dr_()
                ts(R9s, R9s, float(NE - 1), None, ALU.min)
                dr_()
                v.tensor_copy(bexi, R9s)
                e128 = cst[:, C_E128:C_E128 + NE]
                ts(ovx, ovx, 128.0, float(NE * P - P))
                dr_()
                tt(ovx, ovx, e128, ALU.subtract)
                tt(pos, rank, over(e128), ALU.add)
                ts(t1, rank, 128.0, None, ALU.is_ge)
                dr_()
                tt(t1, t1, over(ovx))
                dr_()
                tt(pos, pos, t1, ALU.add)
                for q, oh in enumerate((oh1, oh2)):
                    dr_()
                    tt(t2, oh, pos)
                    dr_()
                    v.tensor_reduce(psn[:, :, q], t2, AXX, ALU.add)
                dr_()
                v.tensor_copy(posi, psn)
                dr_()
                v.sem_inc(pos_ready, 1)
                v.wait_ge(id_tr, l + 1)
                v.tensor_copy(ids, bank(5)[:, 0:NB])
                dr_()
                v.sem_inc(ids_ready, 1)

                with v.Fori(0, NE // 2) as i:
                    for p in range(2):
                        v.wait_ge(xT_done, nth(l, 2 * NE, i * 4 + 2 * p + 2 + 2 * PRE))
                        v.tensor_copy(xgT[p][:, 4:8, :], bank(7).rearrange("p (k t) -> p k t", k=4)).then_inc(xT_dve, 1)
                    for p in range(2):
                        v.wait_ge(up_done, nth(l, NE, i * 2 + p + 1 + PRE))
                        v.wait_ge(sg_ready, nth(l, NE, i * 2 + p + 1))
                        tt(av[p], sg[p], bank(2 * p + 1)).then_inc(a_ready, 1)
                    for half in range(2):
                        v.wait_ge(y_done, nth(l, 2 * NE, i * 4 + 1 + half + 2 * PRE))
                        if half == 0:
                            v.wait_ge(y_stored[0], l * 128 + i * 16 + 16)
                        v.tensor_copy(yb[0][:, half * W:(half + 1) * W], bank(4 + half)).then_inc(yA_evac, 1)
                dr_()
                nov = v.value_load(novi[0:1, :], min_val=0, max_val=OVB)
                with v.Fori(0, OVB) as j:
                    with v.If(nov > j):
                        v.wait_ge(ov_pe, l * (6 * OVB) + j * 6 + 4)
                        v.wait_ge(ov_act, l * (4 * OVB) + j * 4 + 2)
                        tt(av[0], sg[0], bank(1)).then_inc(ov_dve, 1)
                    with v.Else():
                        v.drain()
                        v.sem_inc(ov_dve, 1)

                until(v, m5_in, l * 16 + 16)
                for t in range(NT):
                    y = 0 if t == 0 else 1
                    a, b = xg[t % 2], yb[t % 2]
                    dr_()
                    v.wait_ge(cmb_in[t % 2], (l * 96 if t % 2 == 0 else l * 64) + 32 * (t // 2 + 1))
                    ts(a, a, wt[:, t, 0:1])
                    dr_()
                    stt(a, b, wt[:, t, 1:2], a, ALU.mult, ALU.add)
                    dr_()
                    tt(a, a, gate_mod[:, y, :])
                    dr_()
                    stt(x[:, t, :], x[:, t, :], ALPHA, a, ALU.mult, ALU.add).then_inc(cmb_used, 1)
                    dr_()
                    for half in range(2):
                        v.bn_stats(stats[:, t, half, :], x[:, t, half * W:(half + 1) * W])
                layer_norm(5, ln2_in, lambda t: None)
                v.sem_inc(x_ready, 1)


def shape_constants(np):
    c = np.zeros((P, C_END), np.float32)
    c[:, C_ID:C_ID + P] = np.eye(P)
    c[:, C_TRI:C_TRI + P] = np.triu(np.ones((P, P)), 1)
    c[:, C_TRI + P:C_TRI + 2 * P] = 1.0
    c[:, C_W4:C_W4 + 4] = np.arange(4, 0, -1)
    c[:, C_W16:C_W16 + NE] = np.arange(NE, 0, -1)
    c[:, C_E128:C_E128 + NE] = np.arange(NE) * P
    c[:, C_J:C_J + OVB] = np.arange(OVB)
    c[:, C_TOK:C_TOK + NT] = np.arange(P)[:, None] + P * np.arange(NT)[None]
    inv = (10000.0 ** (-np.arange(16, dtype=np.float32) / 16)).astype(np.float32)
    pos = np.arange(512)
    cos, sin = np.zeros((512, 64), np.float32), np.zeros((512, 64), np.float32)
    for half, q in enumerate((pos // 64, pos % 64)):
        ang = q[:, None].astype(np.float32) * inv
        o = half * 32
        cos[:, o:o + 16] = cos[:, o + 16:o + 32] = np.cos(ang)
        sin[:, o:o + 16], sin[:, o + 16:o + 32] = -np.sin(ang), np.sin(ang)
    c[:, C_COS:C_COS + 256] = cos.reshape(4, P, 64).transpose(1, 0, 2).reshape(P, 256)
    c[:, C_SIN:C_SIN + 256] = sin.reshape(4, P, 64).transpose(1, 0, 2).reshape(P, 256)
    scan = np.ones((NT, P + 1), np.float32)
    scan[:, 0] = 0
    c[:, C_SCAN:C_END] = scan.reshape(1, -1)
    m = np.zeros((P, 2 * NL + 1, P), np.float32)
    s, t = np.arange(P)[:, None], np.arange(P)[None]
    m[:, 0] = s == t
    for j, h in enumerate(LEVELS):
        same = s // (2 * h) == t // (2 * h)
        su, tu = (s // h) % 2, (t // h) % 2
        m[:, 1 + j] = same & (su == 0) & (tu == 1)
        m[:, 1 + NL + j] = same & (su == 1) & (tu == 0)
    return c, m


def kernel(**inputs):
    import numpy as np
    import concourse.bacc as bacc
    from concourse import mybir as mb
    from concourse.bass_utils import run_bass_kernel_spmd as run

    g = {k: np.asarray(a) for k, a in inputs.items()}
    cst, masks = shape_constants(np)
    cond = np.stack([g["c_ctx"], g["c"][0]])
    arrays = {
        "x": np.concatenate([g["x_prompt"][0], g["x_sample"][0]]),
        "condT": cond.reshape(2, KD, P).transpose(2, 1, 0),
        "w_ada": g["w_ada"], "b_ada": g["b_ada"], "w_in": g["w_in"], "w_out": g["w_out"],
        "diff_lambda": g["diff_lambda"], "attn_norm_g": g["attn_norm_g"],
        "mlp_ln_g": g["mlp_ln_g"], "mlp_ln_b": g["mlp_ln_b"],
        "wsT": g["w_spatial"].transpose(0, 3, 1, 2), "bsT": g["b_spatial"].transpose(0, 2, 1),
        "lbT": g["hgrn_lb"].reshape(2, DEPTH, 2, P).transpose(3, 1, 0, 2).reshape(P, DEPTH, 4),
        "hgrn_norm_g": g["hgrn_norm_g"], "ln_g": g["ln_g"], "ln_b": g["ln_b"],
        "w_router": g["w_router"], "router_bias": g["router_bias"],
        "w_gate": g["w_gate"], "w_up": g["w_up"], "w_down": g["w_down"],
        "kcT": g["cache_k"][0].transpose(0, 3, 4, 2, 1).reshape(DEPTH, P, HA, P),
        "cache_v": g["cache_v"][0].reshape(DEPTH, P, 512),
        "state": g["state_hgrn"][0],
        "cst": cst, "masks": masks,
    }
    outs = {"y": (T, D), "new_k": (DEPTH, P, 512), "new_v": (DEPTH, P, 512), "new_s": (DEPTH, 2, HC, 64, 64)}
    nc = bacc.Bacc("TRN2", target_bir_lowering=False, num_devices=1)
    A = {}
    for name in arrays:
        arrays[name] = np.ascontiguousarray(arrays[name])
        A[name] = nc.dram_tensor(name, list(arrays[name].shape), mb.dt.from_np(arrays[name].dtype), kind="ExternalInput").ap()
    for name, shape in outs.items():
        A[name] = nc.dram_tensor(name, list(shape), mb.dt.float32, kind="ExternalOutput").ap()
    build_program(nc, A)
    r = run(nc, [arrays], core_ids=[0]).results[0]
    y = r["y"]
    return (y[:P].reshape(1, P, D), y[P:].reshape(1, T - P, D),
            r["new_k"].reshape(1, DEPTH, P, HA, 2, DQ), r["new_v"].reshape(1, DEPTH, P, HA, 128),
            r["new_s"].reshape(1, DEPTH, 2, HC, 64, 64))
```

```python
import math
from contextlib import ExitStack

import concourse.bass as bass
from concourse import mybir
from concourse.alu_op_type import AluOpType as ALU

ACT = mybir.ActivationFunctionType
AXX = mybir.AxisListType.X
F32 = mybir.dt.float32
I32 = mybir.dt.int32
U8 = mybir.dt.uint8

P = 128
D = 1024
DEPTH = 2
NT = 5
T = NT * P
KD = D // P
NIN = 3584
HA = 4
DQ = 64
SCALE = DQ ** -0.5
HC = 4
JOBS = [0, 2, 1, 3]
UNITS = [[10, 11, 12, 13, 14, 15, 16], [17, 18, 19, 20, 21, 22], [23, 24, 25, 26, 27, 28], [29, 30, 31, 32, 33, 34]]
PLACE = [0, 1, 2, 3, 4, 7, 8]
LEVELS = [64, 32, 16, 8, 4, 2, 1]
NL = len(LEVELS)
GB = 4
NE = 16
DFF = 512
OVB = 9
NB = NE + OVB
NEG = 1e30
ALPHA = (2 * DEPTH) ** 0.25
EPS = 1e-5
W = 512
SLOT = KD * W

COLS = {"F": 2304, "Q": 2816, "I": 2048, "G": 3328, "UV": 1536, "VA": 1024, "KA": 512, "QA": 0}

N_PJ, N_PJA, N_PJV, N_TR, N_VAR = 45, 35, 10, 30, 3 + 2 * NT

C_ID, C_TRI, C_W4, C_W16, C_E128, C_IOTA, C_TOK, C_COS, C_SIN, C_SCAN, C_END = (
    0, 128, 384, 388, 404, 420, 548, 553, 809, 1065, 1710)


def nth(l, per, n):
    return l * per + n


def loadsA(l, j, uses):
    return l * (192 if j == 2 else 176) + (128 + 16 * uses + (16 if j == 2 else 0))


def lam_init(l):
    return 0.8 - 0.6 * math.exp(-0.3 * l)


def build_program(nc, A):
    with ExitStack() as ctx:
        def sb(name, shape, dt=F32):
            return ctx.enter_context(nc.sbuf_tensor("sb_" + name, shape, dt))

        def sem(name):
            return ctx.enter_context(nc.semaphore(name))

        def dram(name, shape):
            return nc.dram_tensor(name, shape, F32, kind="Internal").ap()

        mod_dram = dram("mod_dram", [DEPTH, 2, 6 * D])
        tok_dram = dram("tok_dram", [T, D])
        x_dram = dram("x_dram", [T, D])
        exp_dram = dram("exp_dram", [NB * P, D])

        wA = sb("wA", [P, 3 * SLOT])
        x = sb("x", [P, NT, D])
        gate_mod = sb("gate_mod", [P, 2, D])
        cst = sb("cst", [P, C_END])
        masks = sb("masks", [P, 2 * NL + 1, P], U8)
        prm = sb("prm", [P, 1412])
        rw = sb("rw", [P, KD, NE])
        rbias = sb("rbias", [P, NE])
        condT = sb("condT", [P, KD, 2])
        small = sb("small", [P, 640])
        ismall = sb("ismall", [P, 64], I32)
        arena = sb("arena", [P, 28956])
        psum = ctx.enter_context(nc.psum_tensor("psum", [P, 4096], F32))

        ident = cst[:, C_ID:C_ID + P]

        def nat(u):
            return x[:, u % 5, (u // 5) * 512:(u // 5) * 512 + 512]
        ar = arena

        def view(off, n, pattern=None, **kw):
            v = ar[:, off:off + n]
            return v.rearrange(pattern, **kw) if pattern else v

        HG = 5120
        hT = view(0, 5120, "p (k t) -> p k t", k=KD)
        kf = view(HG, 2560, "p (c t) -> p c t", c=4)
        qf = view(HG + 2560, 2560, "p (c t) -> p c t", c=4)
        BW = NT * (P + 1)
        bsum = view(HG + 5120, 2 * BW, "p (s w j) -> p s w j", s=2, w=NT)
        bsum2 = view(HG + 5120, 2 * BW, "p (s w) -> p s w", s=2)
        gpad = view(HG + 7700, BW, "p (w j) -> p w j", w=NT)
        gpad2 = view(HG + 7700, BW)
        Qb = view(HG + 8345, 1280, "p (s t) -> p s t", s=2)
        Kb = view(HG + 9625, 1280, "p (s t) -> p s t", s=2)
        Eb = view(HG + 10905, 1280, "p (s t) -> p s t", s=2)
        KEn = view(HG + 12185, 640, "p (w d) -> p w d", w=NT)
        AT = view(HG + 12825, 2560, "p (r h t) -> p r h t", r=2, h=2)
        AT2 = view(HG + 12825, 2560)
        S = view(HG + 15385, 1792, "p (r s e) -> p r s e", r=2, s=7)
        S2 = view(HG + 15385, 1792)
        ishift = view(HG + 7168, 4096, "p (y m d) -> p y m d", y=2, m=2)
        hin = view(HG + 13312, 2048, "p (s d) -> p s d", s=2)
        qT = view(HG, 2560, "p (h t) -> p h t", h=HA)
        kT = view(HG + 2560, 3072, "p (h t) -> p h t", h=HA)
        vv = [gate_mod[:, s // 2, (s % 2) * 512:(s % 2) * 512 + 512] for s in range(4)] + [
            view(HG + 6410, 512), view(HG + 6922, 512)]
        oa = view(HG + 8704, 2560, "p (t c) -> p t c", t=NT)
        Pb = view(HG + 11264, 2560, "p (s m k) -> p s m k", s=2, m=2)
        pd = view(HG + 13824, 1280, "p (s k) -> p s k", s=2)
        pdT = view(HG + 15104, 1280, "p (s k) -> p s k", s=2)
        ropeb = view(28700, 256)
        lnb = view(HG + 11264, 2048, "p (m d) -> p m d", m=2)
        ig = view(22300, 2560, "p (t c) -> p t c", t=NT)
        oc = view(24860, 1280, "p (t c) -> p t c", t=NT)
        uv = view(26140, 2560, "p (t c) -> p t c", t=NT)
        wB = 0
        shift2 = view(18432, 4096, "p (y m d) -> p y m d", y=2, m=2)
        hh = view(22528, 2048, "p (s d) -> p s d", s=2)
        hTt = view(24860, 1024, "p (k t) -> p k t", k=KD)
        xg = [view(25884 + 1024 * s, 1024) for s in range(2)]
        xgT = [view(12288 + 1024 * s, 1024, "p (k t) -> p k t", k=KD) for s in range(2)]
        av = [view(14336 + 512 * s, 512) for s in range(2)]
        aT = [view(15360 + 512 * s, 512, "p (k t) -> p k t", k=4) for s in range(2)]
        x1t = [view(12288 + 512 * s, 512) for s in range(2)]
        sg = [view(22528 + 512 * s, 512) for s in range(2)]
        yb = [view(23552, 1024), view(27932, 1024)]
        mrow = ar[0:2, 0:DEPTH * 6 * D]
        at_row = view(12288, 10 * P, "p (a r) -> p a r", a=10)
        at_block = view(12288 + 10 * P, 10 * NB, "p (a b) -> p a b", a=10)

        def slotA(j):
            return wA[:, j * SLOT:(j + 1) * SLOT]

        def slotB(j):
            return ar[:, wB + j * SLOT:wB + (j + 1) * SLOT]

        def bank(i, n=512):
            return psum[:, i * 512:i * 512 + n]

        ag, hg, mg, mb = prm[:, 0:128], prm[:, 128:384], prm[:, 384:640], prm[:, 640:896]
        wsT = prm[:, 896:1408].rearrange("p (g i) -> p g i", g=GB)
        bsT = prm[:, 1408:1412]

        o = [0]

        def sm(n):
            o[0] += n
            return small[:, o[0] - n:o[0]]

        lbt = sm(DEPTH * 4).rearrange("p (l c) -> p l c", l=DEPTH)
        lbx = sm(DEPTH * 4).rearrange("p (l c) -> p l c", l=DEPTH)
        lbm, lb, omlb, nomlb = sm(4), sm(4), sm(4), sm(4)
        lams, lamn, lamn_l, oml, oml_l = sm(DEPTH * 2), sm(DEPTH), sm(1), sm(DEPTH), sm(1)
        eB = sm(20).rearrange("p (c w) -> p c w", c=4)
        stats = sm(60).rearrange("p (t s f) -> p t s f", t=NT, s=2)
        mv = sm(10).rearrange("p (t f) -> p t f", t=NT)
        rstd = sm(NT)
        ms, rs = sm(20), sm(20)
        nmx, negm = sm(2), sm(40)
        Z, rZ, cc = sm(40), sm(40), sm(20)
        score = sm(80).rearrange("p (t e) -> p t e", t=NT)
        gt = sm(20).rearrange("p (t g) -> p t g", t=NT)
        ovc, ovi, ovx = sm(NE), sm(NE), sm(NE)
        wt = sm(10).rearrange("p (t k) -> p t k", t=NT)
        psn = sm(10).rearrange("p (t k) -> p t k", t=NT)
        wsum = sm(NT)
        mhalf = sm(20)
        spare = sm(OVB)
        posi = ismall[:, 0:10].rearrange("p (t k) -> p t k", t=NT)
        rowi, blki = ismall[:, 50:60], sb("blki", [P, 10], I32)[:]
        rowf, blkf = sm(10), sm(10)
        ids = ismall[:, 10:10 + NB]
        novi = ismall[:, 36:37]
        bexi = ismall[:, 40:40 + OVB]
        R = [view(25884 + 80 * i, 80, "p (t e) -> p t e", t=NT) for i in range(12)]
        R9 = view(25884 + 960, OVB * NE, "p (j e) -> p j e", j=OVB)
        R9s = view(25884 + 960 + 144, OVB)
        lamb = view(12288, DEPTH * 4 * 64, "p (l f d) -> p l f d", l=DEPTH, f=4)
        maskf = view(14336, (2 * NL + 1) * P, "p (m t) -> p m t", m=2 * NL + 1)
        lamp = view(13312, DEPTH * 2 * 64, "p (l f d) -> p l f d", l=DEPTH, f=2)

        x_in, consts, lam_in = sem("x_in"), sem("consts"), sem("lam_in")
        bias_in = sem("bias_in")
        cond_ready, ada_mm, ada_free = sem("cond_ready"), sem("ada_mm"), sem("ada_free")
        ada_ready, mod_out = sem("ada_ready"), sem("mod_out")
        zero_ready, zero_out = sem("zero_ready"), sem("zero_out")
        pe_setup, lb_exp, setup_done = sem("pe_setup"), sem("lb_exp"), sem("setup_done")
        lbs_ready = sem("lbs_ready")
        landedA = [sem(f"landedA{j}") for j in range(3)]
        landedB = [sem(f"landedB{j}") for j in range(3)]
        slots_free = sem("slots_free")
        x_ready, x_spilled, x_back = sem("x_ready"), sem("x_spilled"), sem("x_back")
        m01_in, m2_in, prm_in, ln1_in = sem("m01_in"), sem("m2_in"), sem("prm_in"), sem("ln1_in")
        m34_in, m5_in, ln2_in, kv_in = sem("m34_in"), sem("m5_in"), sem("ln2_in"), sem("kv_in")
        h_ready, tr_done, tr_evac = sem("h_ready"), sem("tr_done"), sem("tr_evac")
        pj_done, pjA, pjV = sem("pj_done"), sem("pjA_evac"), sem("pjV_evac")
        f_ready, g_ready, k_ready = sem("f_ready"), sem("g_ready"), sem("k_ready")
        D_ready, E_ready, Q_ready, K_ready = sem("D_ready"), sem("E_ready"), sem("Q_ready"), sem("K_ready")
        lv_mm, lv_acc, at_zero = sem("lv_mm"), sem("lv_acc"), sem("at_zero")
        s_zero, s_init, s_ready = sem("s_zero"), sem("s_init"), sem("s_ready")
        ke_t, ke_evac, ds_mm = sem("ke_t"), sem("ke_evac"), sem("ds_mm")
        o_mm, o_evac = sem("o_mm"), sem("o_evac")
        var_ready, rstd_ready, scaled = sem("var_ready"), sem("rstd_ready"), sem("scaled")
        v_ready, sp_mm, sp_used = sem("v_ready"), sem("sp_mm"), sem("sp_used")
        r_ready, r_tr, r_evac = sem("r_ready"), sem("r_tr"), sem("r_evac")
        sc_done, nm_ready, p_ready, pd_ready = sem("sc_done"), sem("nm_ready"), sem("p_ready"), sem("pd_ready")
        sc_first = sem("sc_first")
        at_tr, at_evac, pv_done, oa_evac = sem("at_tr"), sem("at_evac"), sem("pv_done"), sem("oa_evac")
        mix_ready, x1_ready = sem("mix_ready"), sem("x1_ready")
        h_stored = [sem("h_stored0"), sem("h_stored1")]
        rt_mm, rt_score, m_ready, rank_mm = sem("rt_mm"), sem("rt_score"), sem("m_ready"), sem("rank_mm")
        pos_ready, at_ready, id_mm, ids_ready = sem("pos_ready"), sem("at_ready"), sem("id_mm"), sem("ids_ready")
        xg_in = [sem("xg_in0"), sem("xg_in1")]
        xT_done, xT_act, xT_dve = sem("xT_done"), sem("xT_act"), sem("xT_dve")
        gate_done, up_done, sg_ready, a_ready = sem("gate_done"), sem("up_done"), sem("sg_ready"), sem("a_ready")
        aT_done, aT_ready, y_done = sem("aT_done"), sem("aT_ready"), sem("y_done")
        yA_evac, yB_evac = sem("yA_evac"), sem("yB_evac")
        y_stored = [sem("y_stored0"), sem("y_stored1")]
        ov_w, ov_g, ov_pe, ov_act, ov_dve, ov_st = (
            sem("ov_w"), sem("ov_g"), sem("ov_pe"), sem("ov_act"), sem("ov_dve"), sem("ov_st"))
        cmb_in = [sem("cmb_in0"), sem("cmb_in1")]
        cmb_used, weighed = sem("cmb_used"), sem("weighed")
        out_k, out_v, out_s, out_y = sem("out_k"), sem("out_v"), sem("out_s"), sem("out_y")

        passed = {e.engine: sem("passed_" + nm) for nm, e in (
            ("sp", nc.sync), ("pe", nc.tensor), ("act", nc.scalar), ("gp", nc.gpsimd), ("dve", nc.vector))}
        PRE = 2

        def until(eng, signal, n):
            eng.wait_ge(signal, n)
            eng.sem_inc(passed[eng.engine], 1)

        def in_block(l, c0, w=W):
            return bass.AP(A["w_in"].tensor, l * (D * NIN) + c0, [[NIN, P], [P * NIN, KD], [1, w]])

        def out_block(l, c0):
            return bass.AP(A["w_out"].tensor, l * (D * D) + c0, [[D, P], [P * D, KD], [1, W]])

        def gate_up(name, l, e):
            return bass.AP(A[name].tensor, (l * NE + e) * (D * DFF), [[DFF, P], [P * DFF, KD], [1, DFF]])

        def down(l, e):
            return bass.AP(A["w_down"].tensor, (l * NE + e) * (D * DFF), [[D, P], [P * D, 4], [1, D]])

        def rows(name, off, n):
            return bass.AP(A[name].tensor, off, [[0, P], [1, n]])

        def mod_rows(l, m, n):
            return bass.AP(mod_dram.tensor, l * (12 * D) + m * D, [[0, P], [6 * D, 2], [1, n * D]])

        def s3(v, k=KD):
            return v.rearrange("p (k c) -> p k c", k=k)

        block = ctx.enter_context(nc.Block())

        @block.sync
        def _(sp):
            sp.dma_start(condT[:], A["condT"]).then_inc(bias_in, 16)
            sp.dma_start(mrow, bass.AP(A["b_ada"].tensor, 0, [[0, 2], [1, DEPTH * 6 * D]])).then_inc(bias_in, 16)
            with sp.Fori(0, DEPTH) as la:
                with sp.Fori(0, 4) as i:
                    for j in range(3):
                        until(sp, ada_mm, la * 12 + i * 3 + j + 1)
                        src = bass.AP(A["w_ada"].tensor, la * (6 * D * D) + (i * (3 * W) + j * W),
                                      [[6 * D, P], [P * 6 * D, KD], [1, W]])
                        sp.dma_start(s3(slotA(j)), src).then_inc(landedA[j], 16)
            with sp.Fori(0, DEPTH) as l:
                order = ["F", "Q", "I", "UV", "VA", "KA", "QA"]
                until(sp, slots_free, l + 1)
                for b, nm in enumerate(order):
                    if b >= 3:
                        until(sp, pj_done, nth(l, N_PJ, 5 * (b - 2)))
                    dst = s3(slotA(b % 3))
                    if nm == "I":
                        sp.dma_start(dst[:, :, 0:256], in_block(l, COLS["I"], 256)).then_inc(landedA[2], 16)
                        sp.dma_start(dst[:, :, 256:512], in_block(l, COLS["G"], 256)).then_inc(landedA[2], 16)
                    else:
                        sp.dma_start(dst, in_block(l, COLS[nm])).then_inc(landedA[b % 3], 16)
                for half in range(2):
                    b = 7 + half
                    until(sp, pj_done, nth(l, N_PJ, 5 * (b - 2)))
                    sp.dma_start(s3(slotA(b % 3)), out_block(l, half * W)).then_inc(landedA[b % 3], 16)
                until(sp, pj_done, nth(l, N_PJ, N_PJ))
                with sp.Fori(0, NE // 2) as i:
                    for p in range(2):
                        slot, landed = ((slotA, landedA), (slotB, landedB))[p]
                        until(sp, gate_done, nth(l, NE, i * 2 + p + PRE - 1))
                        sp.dma_start(s3(slot(0)), gate_up("w_gate", l, i * 2 + p)).then_inc(landed[0], 16)
                        until(sp, up_done, nth(l, NE, i * 2 + p + PRE - 1))
                        sp.dma_start(s3(slot(1)), gate_up("w_up", l, i * 2 + p)).then_inc(landed[1], 16)
                        until(sp, y_done, nth(l, 2 * NE, i * 4 + 2 * p + 2))
                        sp.dma_start(s3(slot(2), 4), down(l, i * 2 + p)).then_inc(landed[2], 16)
                until(sp, pos_ready, l + 1)
                nov = sp.value_load(novi[0:1, :], min_val=0, max_val=OVB)
                with sp.Fori(0, OVB) as j:
                    with sp.If(nov > j):
                        ex = sp.value_load(bexi[0:1, bass.ds(j, 1)], min_val=0, max_val=NE - 1)
                        until(sp, gate_done, nth(l, NE, NE - 1 + PRE))
                        until(sp, ov_pe, l * (6 * OVB) + j * 6 + 2)
                        sp.dma_start(s3(slotA(0)), gate_up("w_gate", l, ex)).then_inc(ov_w, 16)
                        until(sp, up_done, nth(l, NE, NE - 1 + PRE))
                        until(sp, ov_pe, l * (6 * OVB) + j * 6 + 3)
                        sp.dma_start(s3(slotA(1)), gate_up("w_up", l, ex)).then_inc(ov_w, 16)
                        until(sp, y_done, nth(l, 2 * NE, 2 * NE - 2 + 2 * PRE))
                        until(sp, ov_pe, l * (6 * OVB) + j * 6 + 6)
                        sp.dma_start(s3(slotA(2), 4), down(l, ex)).then_inc(ov_w, 16)
                        until(sp, ov_w, l * (48 * OVB) + j * 48 + 48)
                    with sp.Else():
                        sp.sem_inc(ov_w, 48)
            until(sp, x_ready, (DEPTH + 1) * NT)
            sp.dma_start(A["y"].rearrange("(t p) d -> p t d", p=P), x[:]).then_inc(out_y, 16)
            until(sp, out_y, 16)
            until(sp, out_k, 16 * DEPTH)
            until(sp, out_v, 16 * DEPTH)
            until(sp, out_s, 128 * DEPTH)

        @block.tensor
        def _(pe):
            pe.sem_inc(ada_mm, 3)
            pe.wait_ge(cond_ready, 1)
            pe.wait_ge(consts, 16 * 5)
            with pe.Fori(0, 4 * DEPTH) as i:
                for j in range(3):
                    pe.wait_ge(landedA[j], i * 16 + 16)
                    pe.wait_ge(ada_free, i * 3 + j + 1)
                    w = s3(slotA(j))
                    for k in range(KD):
                        mm = pe.matmul(bank(j)[0:2, :], condT[:, k, :], w[:, k, :], start=k == 0, stop=k == KD - 1)
                    mm.then_inc(ada_mm, 1)
            pe.sem_inc(gate_done, PRE)
            pe.sem_inc(up_done, PRE)
            pe.sem_inc(y_done, 2 * PRE)
            pe.sem_inc(xT_done, 2 * PRE)
            pe.sem_inc(ov_pe, 6)
            pe.drain()
            pe.sem_inc(slots_free, 1)

            with pe.Fori(0, DEPTH) as l:

                def tile_transposes(n, chunks):
                    for half in range(2):
                        if n > 0:
                            pe.wait_ge(tr_evac, nth(l, N_TR, 2 * n - 1 + half))
                        for q in range(4):
                            mm = pe.transpose(bank(6 + half)[:, q * P:(q + 1) * P], chunks[4 * half + q], ident)
                        mm.then_inc(tr_done, 1)

                for t in range(NT):
                    pe.wait_ge(h_ready, nth(l, 2 * NT, t + 1))
                    tile_transposes(t, [hin[:, t % 2, k * P:(k + 1) * P] for k in range(KD)])
                pe.wait_ge(tr_evac, nth(l, N_TR, 2 * NT))

                def bank_free(n):
                    if 3 <= n < N_PJA + 3:
                        pe.wait_ge(pjA, nth(l, N_PJA, n - 2))
                    elif n >= N_PJA + 3:
                        pe.wait_ge(pjV, nth(l, N_PJV, n - 2 - N_PJA))

                def landed(b):
                    pe.wait_ge(landedA[b % 3], loadsA(l, b % 3, b // 3 + 1))

                def features_unit(b, c):
                    w, n = s3(slotA(b % 3)), 5 * b + c
                    bank_free(n)
                    for cc_ in ([c] if c < 4 else range(4)):
                        out, tok = ((bank(n % 3), slice(P, T)) if c < 4
                                    else (bank(n % 3)[:, cc_ * P:(cc_ + 1) * P], slice(0, P)))
                        for k in range(KD):
                            mm = pe.matmul(out, w[:, k, cc_ * P:(cc_ + 1) * P], hT[:, k, tok],
                                           start=k == 0, stop=k == KD - 1)
                    mm.then_inc(pj_done, 1)

                def tokens_unit(b, t):
                    w, n = s3(slotA(b % 3)), 5 * b + t
                    bank_free(n)
                    for k in range(KD):
                        mm = pe.matmul(bank(n % 3), hT[:, k, t * P:(t + 1) * P], w[:, k, :],
                                       start=k == 0, stop=k == KD - 1)
                    mm.then_inc(pj_done, 1)

                for b in range(2):
                    landed(b)
                    for c in range(5):
                        features_unit(b, c)

                def U(h):
                    return psum[:, (3 + 2 * h) * 512:(3 + 2 * h) * 512 + T]

                for ci, c in enumerate(JOBS):
                    def projections(place):
                        for n, at in zip(UNITS[ci], PLACE):
                            if at == place:
                                if n % 5 == 0:
                                    landed(n // 5)
                                tokens_unit(n // 5, n % 5)

                    pair, dr = c % 2, c // 2
                    pe.wait_ge(k_ready, nth(l, 4, ci + 1))
                    if ci == 0:
                        pe.wait_ge(pjA, nth(l, N_PJA, 10))
                    for j in range(NL + 1):
                        if j:
                            pe.wait_ge(Q_ready, nth(l, 32, 8 * ci + j))
                            pe.wait_ge(K_ready, nth(l, 32, 8 * ci + j))
                        ks, qs = (kf[:, c], qf[:, c]) if j == 0 else (Kb[:, j % 2], Qb[:, j % 2])
                        for h in range(2):
                            if j:
                                pe.wait_ge(lv_acc, nth(l, 64, 16 * ci + 2 * j - 1 + h))
                            elif ci == 2:
                                pe.wait_ge(o_evac, nth(l, 4, h + 1))
                            elif ci and h == 1:
                                pe.wait_ge(s_ready, nth(l, 4, ci))
                            r = slice(64 * h, 64 * h + 64)
                            for w in range(NT):
                                tk = slice(w * P, (w + 1) * P)
                                mm = pe.matmul(U(h)[:, tk], ks[r, tk], qs[r, tk], start=True, stop=True)
                            mm.then_inc(lv_mm, 1)
                        if j < 7:
                            projections(j)
                    pe.wait_ge(K_ready, nth(l, 32, 8 * ci + 8))
                    pe.wait_ge(lv_acc, nth(l, 64, 16 * ci + 16))
                    for w in range(NT):
                        mm = pe.transpose(U(0)[:, w * P:(w + 1) * P], kf[:, c, w * P:(w + 1) * P], ident)
                    mm.then_inc(ke_t, 1)
                    projections(7)
                    pe.wait_ge(ke_evac, nth(l, 4, ci + 1))
                    for w in range(NT):
                        mm = pe.matmul(U(1)[:, w * P:(w + 1) * P], KEn[:, w, :], ig[:, w, pair * P:(pair + 1) * P],
                                       start=True, stop=True)
                    mm.then_inc(ds_mm, 1)
                    projections(8)
                    if dr == 1:
                        pe.wait_ge(s_ready, nth(l, 4, ci + 1))
                        pe.wait_ge(Q_ready, nth(l, 32, 8 * ci + 8))
                        for h in range(2):
                            r = slice(64 * h, 64 * h + 64)
                            for w in range(NT):
                                tk = slice(w * P, (w + 1) * P)
                                out = U(h)[:, tk]
                                iw = ig[:, w, pair * P:(pair + 1) * P]
                                pe.matmul(out, AT[:, 0, h, tk], iw, start=True, stop=False)
                                pe.matmul(out, AT[:, 1, h, tk], iw, start=False, stop=False)
                                ent = (0 if w == 0 else 1 + w, 1 if w == 0 else 2 + w)
                                pe.matmul(out, qf[r, pair, tk], S[r, 0, ent[0], :], start=False, stop=False)
                                mm = pe.matmul(out, qf[r, 2 + pair, tk], S[r, 1, ent[1], :], start=False, stop=True)
                            mm.then_inc(o_mm, 1)

                pe.wait_ge(o_evac, nth(l, 4, 4))
                for u in range(10):
                    if u % 5 == 0:
                        pe.wait_ge(pjA, nth(l, N_PJA, 26 + u))
                    else:
                        pe.wait_ge(r_ready, nth(l, 8, u - u // 5))
                    if u >= 2:
                        pe.wait_ge(r_evac, nth(l, 10, u - 1))
                    for q in range(4):
                        mm = pe.transpose(bank(7 if u % 2 else 6)[:, q * P:(q + 1) * P], nat(u)[:, q * P:(q + 1) * P], ident)
                    mm.then_inc(r_tr, 1)

                pe.wait_ge(v_ready, l + 1)
                pe.wait_ge(prm_in, nth(l, 96, 96))
                for t in range(NT):
                    for g in range(GB):
                        out = psum[:, 1536 + t * 256 + g * 64:1536 + t * 256 + g * 64 + 64]
                        mm = pe.matmul(out, wsT[:, g, :], uv[:, t, 256 + g * 64:256 + g * 64 + 64], start=True, stop=True)
                mm.then_inc(sp_mm, 1)

                def region(n):
                    return psum[:, (n % 2) * 1536:(n % 2) * 1536 + 1280]

                def keys(t):
                    return (640, 768, [5]) if t == 0 else (0, 640, list(range(5)))

                def scores(n):
                    t, h = n // 4, n % 4
                    k0, k1, _ = keys(t)
                    if n >= 2:
                        pe.wait_ge(at_evac, nth(l, 20, n - 1))
                    parts = ([(0, 0, P), (1, 0, P)] if t == 0 else
                             [(0, 512, 640), (0, 0, 512), (1, 384, 640), (1, 0, 384)])
                    for i, (m, a, b) in enumerate(parts):
                        r = slice(64 * m, 64 * m + 64)
                        if i == len(parts) - 1:
                            pe.wait_ge(sc_first, nth(l, 20, n + 1))
                        mm = pe.matmul(region(n)[:, m * 640 + a:m * 640 + b], qT[r, h, t * P:(t + 1) * P],
                                       kT[r, h, k0 + a:k0 + b], start=True, stop=True)
                        if i == 0:
                            mm.then_inc(sc_first, 1)
                    mm.then_inc(sc_done, 1)

                def probs_v(n):
                    t, h = n // 4, n % 4
                    pe.wait_ge(at_evac, nth(l, 20, n + 1))
                    if h == 0 and t >= 2:
                        pe.wait_ge(oa_evac, nth(l, NT, t - 1))
                    vs = keys(t)[2]
                    for i, s_ in enumerate(vs):
                        mm = pe.matmul(bank(6 + t % 2)[:, h * P:(h + 1) * P], pdT[:, n % 2, i * P:(i + 1) * P],
                                       vv[s_][:, h * P:(h + 1) * P], start=i == 0, stop=i == len(vs) - 1)
                    mm.then_inc(pv_done, 1)

                pe.wait_ge(r_evac, nth(l, 10, 10))
                pe.wait_ge(kv_in, nth(l, 32, 32))
                pe.wait_ge(pjA, nth(l, N_PJA, N_PJA))
                pe.wait_ge(sp_used, l + 1)
                scores(0)
                for n in range(20):
                    if n + 1 < 20:
                        scores(n + 1)
                    if n:
                        probs_v(n - 1)
                    pe.wait_ge(pd_ready, nth(l, 20, n + 1))
                    for i in range(len(keys(n // 4)[2])):
                        mm = pe.transpose(region(n)[:, i * P:(i + 1) * P], pd[:, n % 2, i * P:(i + 1) * P], ident)
                    mm.then_inc(at_tr, 1)
                probs_v(19)

                pe.wait_ge(mix_ready, l + 1)
                for t in range(NT):
                    tile_transposes(NT + t, [oa[:, t, k * P:(k + 1) * P] for k in range(4)]
                                    + [uv[:, t, k * P:(k + 1) * P] for k in range(2)]
                                    + [oc[:, t, k * P:(k + 1) * P] for k in range(2)])
                landed(7)
                landed(8)
                def router(t):
                    pe.wait_ge(h_ready, nth(l, 2 * NT, NT + t + 1))
                    tile_transposes(2 * NT + t, [hh[:, t % 2, k * P:(k + 1) * P] for k in range(KD)])
                    pe.wait_ge(tr_evac, nth(l, N_TR, 4 * NT + 2 * t + 2))
                    for k in range(KD):
                        mm = pe.matmul(bank(3)[:, t * NE:(t + 1) * NE], hTt[:, k, :], rw[:, k, :],
                                       start=k == 0, stop=k == KD - 1)
                    mm.then_inc(rt_mm, 1)

                for t in range(NT):
                    pe.wait_ge(tr_evac, nth(l, N_TR, 2 * NT + 2 * t + 2))
                    for half in range(2):
                        n = 35 + 2 * t + half
                        if n >= 38:
                            bank_free(n)
                        w = s3(slotA((7 + half) % 3))
                        for k in range(KD):
                            mm = pe.matmul(bank(n % 3), hT[:, k, t * P:(t + 1) * P], w[:, k, :],
                                           start=k == 0, stop=k == KD - 1)
                        mm.then_inc(pj_done, 1)
                    if t >= 2:
                        router(t - 2)
                router(NT - 2)
                router(NT - 1)
                pe.wait_ge(m_ready, l + 1)
                M = R[0]
                for t in range(NT):
                    for u in range(t + 1):
                        tri = cst[:, C_TRI + (P if u < t else 0):C_TRI + (P if u < t else 0) + P]
                        pe.matmul(bank(4)[:, t * NE:(t + 1) * NE], tri, M[:, u, :], start=u == 0, stop=u == t)
                for u in range(NT):
                    mm = pe.matmul(bank(4)[:, 80:96], cst[:, C_TRI + P:C_TRI + 2 * P], M[:, u, :],
                                   start=u == 0, stop=u == NT - 1)
                mm.then_inc(rank_mm, 1)
                pe.wait_ge(at_ready, l + 1)
                for a in range(2 * NT):
                    mm = pe.matmul(bank(5)[:, 0:NB], at_row[:, a, :], at_block[:, a, :],
                                   start=a == 0, stop=a == 2 * NT - 1)
                mm.then_inc(id_mm, 1)

                def gather_transposed(p, src, s0, s1):
                    for half in range(2):
                        for q in range(4):
                            k = 4 * half + q
                            mm = pe.transpose(bank(6 + half)[:, q * P:(q + 1) * P], src[:, k * P:(k + 1) * P], ident)
                        mm.then_inc(s0 if half == 0 else s1, 1)

                with pe.Fori(0, NE // 2) as i:
                    for p in range(2):
                        pe.wait_ge(xg_in[p], l * 128 + i * 16 + 16)
                        if p:
                            pe.wait_ge(xT_act, nth(l, NE, i * 2 + 1))
                            pe.wait_ge(xT_dve, nth(l, NE, i * 2 + 1))
                        gather_transposed(p, xg[p], xT_done, xT_done)
                    for p in range(2):
                        landed_ = (landedA, landedB)[p]
                        slot = (slotA, slotB)[p]
                        base = [loadsA(l, j, 3) if p == 0 else l * 128 for j in range(3)]
                        pe.wait_ge(xT_act, nth(l, NE, i * 2 + p + 1))
                        pe.wait_ge(xT_dve, nth(l, NE, i * 2 + p + 1))
                        pe.wait_ge(landed_[0], base[0] + i * 16 + 16)
                        for k in range(KD):
                            mm = pe.matmul(bank(2 * p), xgT[p][:, k, :], s3(slot(0))[:, k, :],
                                           start=k == 0, stop=k == KD - 1)
                        mm.then_inc(gate_done, 1)
                        pe.wait_ge(landed_[1], base[1] + i * 16 + 16)
                        for k in range(KD):
                            mm = pe.matmul(bank(2 * p + 1), xgT[p][:, k, :], s3(slot(1))[:, k, :],
                                           start=k == 0, stop=k == KD - 1)
                        mm.then_inc(up_done, 1)
                    for p in range(2):
                        pe.wait_ge(a_ready, nth(l, NE, i * 2 + p + 1))
                        for q in range(4):
                            mm = pe.transpose(bank(6 + p)[:, q * P:(q + 1) * P], av[p][:, q * P:(q + 1) * P], ident)
                        mm.then_inc(aT_done, 1)
                        pe.wait_ge(aT_ready, nth(l, NE, i * 2 + p + 1))
                        pe.wait_ge((landedA, landedB)[p][2], (loadsA(l, 2, 3) if p == 0 else l * 128) + i * 16 + 16)
                        if p:
                            pe.wait_ge(yA_evac, nth(l, NE, i * 2 + 2))
                        else:
                            pe.wait_ge(yB_evac, nth(l, NE, i * 2 + 2))
                        for half in range(2):
                            for k in range(4):
                                mm = pe.matmul(bank(4 + half), aT[p][:, k, :],
                                               s3((slotA, slotB)[p](2), 4)[:, k, half * W:(half + 1) * W],
                                               start=k == 0, stop=k == 3)
                            mm.then_inc(y_done, 1)
                until(pe, yB_evac, nth(l, NE, NE + 2))
                nov = pe.value_load(novi[0:1, :], min_val=0, max_val=OVB)
                with pe.Fori(0, OVB) as j:
                    with pe.If(nov > j):
                        pe.wait_ge(ov_g, l * (16 * OVB) + j * 16 + 16)
                        for half in range(2):
                            for q in range(4):
                                k = 4 * half + q
                                mm = pe.transpose(bank(6 + half)[:, q * P:(q + 1) * P], xg[0][:, k * P:(k + 1) * P], ident)
                        mm.then_inc(ov_pe, 1)
                        pe.wait_ge(ov_act, l * (4 * OVB) + j * 4 + 1)
                        pe.wait_ge(ov_w, l * (48 * OVB) + j * 48 + 48)
                        for s_ in range(2):
                            for k in range(KD):
                                mm = pe.matmul(bank(s_), xgT[0][:, k, :], s3(slotA(s_))[:, k, :],
                                               start=k == 0, stop=k == KD - 1)
                            mm.then_inc(ov_pe, 1)
                        pe.wait_ge(ov_dve, l * OVB + j + 1)
                        for q in range(4):
                            mm = pe.transpose(bank(6)[:, q * P:(q + 1) * P], av[0][:, q * P:(q + 1) * P], ident)
                        mm.then_inc(ov_pe, 1)
                        pe.wait_ge(ov_act, l * (4 * OVB) + j * 4 + 3)
                        for half in range(2):
                            for k in range(4):
                                mm = pe.matmul(bank(4 + half), aT[0][:, k, :],
                                               s3(slotA(2), 4)[:, k, half * W:(half + 1) * W],
                                               start=k == 0, stop=k == 3)
                            mm.then_inc(ov_pe, 1)
                    with pe.Else():
                        pe.drain()
                        pe.sem_inc(ov_pe, 6)
                pe.drain()
                pe.sem_inc(slots_free, 1)

        @block.scalar
        def _(act):
            act.dma_start(cst[:], A["cst"]).then_inc(consts, 16)
            act.dma_start(maskf, A["masks"]).then_inc(consts, 16)
            act.dma_start(rw[:], A["w_router"].rearrange("(k p) e -> p k e", p=P)).then_inc(consts, 16)
            act.dma_start(rbias[:], rows("router_bias", 0, NE)).then_inc(consts, 16)
            act.dma_start(lbt, A["lbT"]).then_inc(consts, 16)
            act.dma_start(lamb, bass.AP(A["diff_lambda"].tensor, 0, [[0, P], [1, DEPTH * 256]])
                          .rearrange("p (l f d) -> p l f d", l=DEPTH, f=4)).then_inc(lam_in, 16)
            act.dma_start(x[:], A["x"].rearrange("(t p) d -> p t d", p=P)).then_inc(x_in, 16)
            act.wait_ge(bias_in, 32)
            act.activation(condT[:], condT[:], ACT.Silu).then_inc(cond_ready, 1)
            act.wait_ge(lbs_ready, 1)
            act.activation(lbx, lbx, ACT.Exp)
            act.activation(lams, lams, ACT.Exp).then_inc(lb_exp, 1)
            act.wait_ge(zero_ready, 1)
            act.dma_start(exp_dram[NE * P:, :].rearrange("(b r) d -> r b d", r=P),
                          yb[0].unsqueeze(1).to_broadcast([P, OVB, D])).then_inc(zero_out, 16)
            act.wait_ge(ada_ready, 1)
            act.dma_start(mod_dram.rearrange("l y d -> y l d"),
                          mrow.rearrange("y (l d) -> y l d", l=DEPTH)).then_inc(mod_out, 16)
            act.wait_ge(mod_out, 16)
            act.wait_ge(zero_out, 16)

            with act.Fori(0, DEPTH) as l:
                act.dma_start(ishift.rearrange("p y m d -> p y (m d)"), mod_rows(l, 0, 2)).then_inc(m01_in, 16)
                act.dma_start(ag, rows("attn_norm_g", l * 128, 128)).then_inc(prm_in, 16)
                act.dma_start(hg, rows("hgrn_norm_g", l * 256, 256)).then_inc(prm_in, 16)
                act.dma_start(mg, rows("mlp_ln_g", l * 256, 256)).then_inc(prm_in, 16)
                act.dma_start(mb, rows("mlp_ln_b", l * 256, 256)).then_inc(prm_in, 16)
                act.dma_start(wsT.rearrange("p g i -> p (g i)"), bass.AP(A["wsT"].tensor, l * (P * 512), [[512, P], [1, 512]])).then_inc(prm_in, 16)
                act.dma_start(bsT, bass.AP(A["bsT"].tensor, l * (P * 4), [[4, P], [1, 4]])).then_inc(prm_in, 16)
                act.wait_ge(x_ready, nth(l, NT, NT))
                act.dma_start(vv[0], bass.AP(A["cache_v"].tensor, l * 65536, [[512, P], [1, 512]])).then_inc(kv_in, 16)
                act.dma_start(x_dram.rearrange("(t p) d -> p t d", p=P), x[:]).then_inc(x_spilled, 16)

                def tile_evac(n, dst):
                    for half in range(2):
                        act.wait_ge(tr_done, nth(l, N_TR, 2 * n + half + 1))
                        act.activation(dst[:, 4 * half:4 * half + 4, :],
                                       bank(6 + half).rearrange("p (k t) -> p k t", k=4), ACT.Copy).then_inc(tr_evac, 1)

                for t in range(NT):
                    tile_evac(t, hT[:, :, t * P:(t + 1) * P])

                def unit_ready(n):
                    act.wait_ge(pj_done, nth(l, N_PJ, n + 1))
                    return bank(n % 3)

                for b, dst, fn in ((0, kf, ACT.Sigmoid), (1, qf, ACT.Copy)):
                    for c in range(5):
                        pb = unit_ready(5 * b + c)
                        if c < 4:
                            a = act.activation(dst[:, c, P:T], pb, fn)
                        else:
                            a = act.activation(dst[:, :, 0:P], pb.rearrange("p (c t) -> p c t", c=4), fn)
                        a.then_inc(pjA, 1)

                def projected(n):
                    pb, b, t = unit_ready(n), n // 5, n % 5
                    if b == 2:
                        act.activation(ig[:, t, 0:256], pb[:, 0:256], ACT.Copy)
                        a = act.activation(ig[:, t, 256:512], pb[:, 256:512], ACT.Silu)
                    elif b == 3:
                        a = act.activation(uv[:, t, :], pb, ACT.Gelu_apprx_tanh)
                    elif b == 4:
                        a = act.activation(vv[5 if t == 0 else t], pb, ACT.Copy)
                    else:
                        if n == 25:
                            act.wait_ge(x_spilled, l * 16 + 16)
                        a = act.activation(nat(n - 25), pb, ACT.Copy)
                    a.then_inc(pjA, 1)
                    if n == 20 or n == 25:
                        act.wait_ge(pjA, nth(l, N_PJA, n + 1))
                        name, src, done = ("new_v", vv[5], out_v) if n == 20 else ("new_k", nat(0), out_k)
                        act.dma_start(bass.AP(A[name].tensor, l * 65536, [[512, P], [1, 512]]), src).then_inc(done, 16)

                for ci, c in enumerate(JOBS):
                    at = dict(zip(PLACE, UNITS[ci]))
                    act.wait_ge(f_ready, nth(l, 4, ci + 1))
                    act.activation(gpad[:, :, 1:P + 1], gpad[:, :, 1:P + 1], ACT.Ln).then_inc(g_ready, 1)
                    if ci % 2 == 0:
                        act.wait_ge(s_zero, nth(l, 2, ci // 2 + 1))
                        for h in range(2):
                            for dr in range(2):
                                src = bass.AP(A["state"].tensor, l * 32768 + (dr * 16384 + (ci + h) * 4096), [[64, 64], [1, 64]])
                                act.dma_start(S[64 * h:64 * h + 64, dr, (2, 6)[dr], 64 * h:64 * h + 64], src).then_inc(s_init, 16)
                    for j in range(NL):
                        act.wait_ge(D_ready, nth(l, 32, 8 * ci + j + 1))
                        act.activation(Eb[:, j % 2], Eb[:, j % 2], ACT.Exp).then_inc(E_ready, 1)
                        if j and j - 1 in at:
                            projected(at[j - 1])
                    act.wait_ge(Q_ready, nth(l, 32, 8 * ci + 6))
                    act.wait_ge(K_ready, nth(l, 32, 8 * ci + 6))
                    beta = bsum[:, ci % 2, :, 1:P + 1] if c < 2 else bsum[:, ci % 2, :, 0:P]
                    act.activation(Eb[:, 1].rearrange("p (w t) -> p w t", w=NT), beta, ACT.Exp).then_inc(E_ready, 1)
                    act.wait_ge(D_ready, nth(l, 32, 8 * ci + 8))
                    act.activation(Eb[:, 0], Eb[:, 0], ACT.Exp).then_inc(E_ready, 1)
                    act.activation(eB[:, c, :], bsum[:, ci % 2, :, P], ACT.Exp).then_inc(E_ready, 1)
                    act.wait_ge(ke_t, nth(l, 4, ci + 1))
                    act.activation(KEn.rearrange("p w d -> p (w d)"), psum[:, 1536:1536 + T], ACT.Copy).then_inc(ke_evac, 1)
                    for place in (7, 8):
                        if place in at:
                            projected(at[place])
                    if c >= 2:
                        act.wait_ge(s_ready, nth(l, 4, ci + 1))
                        for h in range(2):
                            for dr in range(2):
                                dst = bass.AP(A["new_s"].tensor, l * 32768 + (dr * 16384 + (c - 2 + c - 2 + h) * 4096), [[64, 64], [1, 64]])
                                act.dma_start(dst, S[64 * h:64 * h + 64, dr, (1, 0)[dr], 64 * h:64 * h + 64]).then_inc(out_s, 16)

                act.wait_ge(o_mm, nth(l, 4, 4))
                act.dma_start(kT[:, :, 0:P], bass.AP(A["kcT"].tensor, l * 65536, [[512, P], [P, 4], [1, P]])).then_inc(kv_in, 16)
                for u in range(10):
                    act.wait_ge(r_tr, nth(l, 10, u + 1))
                    t = u % 5
                    if u < 5:
                        k0 = 640 if t == 0 else t * P
                        dst = kT[:, :, k0:k0 + P]
                    else:
                        dst = qT[:, :, t * P:(t + 1) * P]
                    act.activation(dst, bank(7 if u % 2 else 6).rearrange("p (h t) -> p h t", h=HA), ACT.Copy).then_inc(r_evac, 1)
                act.wait_ge(out_k, l * 16 + 16)
                act.dma_start(x[:], x_dram.rearrange("(t p) d -> p t d", p=P)).then_inc(x_back, 16)

                def exps(n):
                    nk = P if n < 4 else T
                    act.wait_ge(nm_ready, nth(l, 20, n + 1))
                    for m in range(2):
                        a = act.activation(Pb[:, n % 2, m, 0:nk], psum[:, (n % 2) * 1536 + m * 640:(n % 2) * 1536 + m * 640 + nk],
                                           ACT.Exp, bias=negm[:, 2 * n + m:2 * n + m + 1], scale=SCALE,
                                           accum_out=Z[:, 2 * n + m:2 * n + m + 1])
                    a.then_inc(p_ready, 1)

                exps(0)
                for n in range(20):
                    nk = P if n < 4 else T
                    if n + 1 < 20:
                        exps(n + 1)
                    act.wait_ge(at_tr, nth(l, 20, n + 1))
                    if n >= 2:
                        act.wait_ge(pv_done, nth(l, 20, n - 1))
                    act.activation(pdT[:, n % 2, 0:nk], psum[:, (n % 2) * 1536:(n % 2) * 1536 + nk], ACT.Copy).then_inc(at_evac, 1)

                act.wait_ge(pv_done, nth(l, 20, 20))
                act.wait_ge(out_v, l * 16 + 16)
                act.dma_start(gate_mod[:], mod_rows(l, 2, 1)).then_inc(m2_in, 16)
                act.wait_ge(mix_ready, l + 1)
                act.dma_start(lnb[:, 0, :], rows("ln_g", l * 2048, D)).then_inc(ln1_in, 16)
                act.dma_start(lnb[:, 1, :], rows("ln_b", l * 2048, D)).then_inc(ln1_in, 16)
                act.dma_start(shift2.rearrange("p y m d -> p y (m d)"), mod_rows(l, 3, 2)).then_inc(m34_in, 16)
                for t in range(NT):
                    tile_evac(NT + t, hT[:, :, t * P:(t + 1) * P])
                for t in range(NT):
                    act.wait_ge(h_ready, nth(l, 2 * NT, NT + t + 1))
                    act.dma_start(tok_dram[t * P:(t + 1) * P, :], hh[:, t % 2, :]).then_inc(h_stored[t % 2], 16)
                    if t:
                        act.wait_ge(rt_mm, nth(l, NT, t))
                    tile_evac(2 * NT + t, hTt)
                act.wait_ge(x1_ready, l + 1)
                act.dma_start(gate_mod[:], mod_rows(l, 5, 1)).then_inc(m5_in, 16)
                act.dma_start(lnb[:, 0, :], rows("ln_g", l * 2048 + D, D)).then_inc(ln2_in, 16)
                act.dma_start(lnb[:, 1, :], rows("ln_b", l * 2048 + D, D)).then_inc(ln2_in, 16)
                act.wait_ge(rt_mm, nth(l, NT, NT))
                act.activation(score.rearrange("p t e -> p (t e)"), bank(3)[:, 0:80], ACT.Sigmoid).then_inc(rt_score, 1)

                with act.Fori(0, NE // 2) as i:
                    for p in range(2):
                        act.wait_ge(xT_done, nth(l, 2 * NE, i * 4 + 2 * p + 1 + 2 * PRE))
                        act.activation(xgT[p][:, 0:4, :], bank(6).rearrange("p (k t) -> p k t", k=4), ACT.Copy).then_inc(xT_act, 1)
                    for p in range(2):
                        act.wait_ge(gate_done, nth(l, NE, i * 2 + p + 1 + PRE))
                        act.activation(sg[p], bank(2 * p), ACT.Silu).then_inc(sg_ready, 1)
                    for p in range(2):
                        act.wait_ge(aT_done, nth(l, NE, i * 2 + p + 1))
                        act.activation(aT[p], bank(6 + p).rearrange("p (k t) -> p k t", k=4), ACT.Copy).then_inc(aT_ready, 1)
                    act.wait_ge(yA_evac, nth(l, NE, i * 2 + 2))
                    act.dma_start(bass.AP(exp_dram.tensor, i * (2 * P * D), [[D, P], [1, D]]), yb[0]).then_inc(y_stored[0], 16)
                    for half in range(2):
                        act.wait_ge(y_done, nth(l, 2 * NE, i * 4 + 3 + half + 2 * PRE))
                        if half == 0:
                            act.wait_ge(y_stored[1], l * 128 + i * 16 + 16)
                        act.activation(yb[1][:, half * W:(half + 1) * W], bank(4 + half), ACT.Copy).then_inc(yB_evac, 1)
                    act.wait_ge(yB_evac, nth(l, NE, i * 2 + 2 + 2))
                    act.dma_start(bass.AP(exp_dram.tensor, i * (2 * P * D) + P * D, [[D, P], [1, D]]), yb[1]).then_inc(y_stored[1], 16)

                until(act, y_stored[0], l * 128 + 144)
                until(act, pos_ready, l + 1)
                nov = act.value_load(novi[0:1, :], min_val=0, max_val=OVB)
                with act.Fori(0, OVB) as j:
                    with act.If(nov > j):
                        act.wait_ge(ov_pe, l * (6 * OVB) + j * 6 + 7)
                        act.activation(xgT[0], psum[:, 3072:4096].rearrange("p (k t) -> p k t", k=KD), ACT.Copy).then_inc(ov_act, 1)
                        act.wait_ge(ov_pe, l * (6 * OVB) + j * 6 + 8)
                        act.activation(sg[0], bank(0), ACT.Silu).then_inc(ov_act, 1)
                        act.wait_ge(ov_pe, l * (6 * OVB) + j * 6 + 10)
                        act.activation(aT[0], bank(6).rearrange("p (k t) -> p k t", k=4), ACT.Copy).then_inc(ov_act, 1)
                        act.wait_ge(ov_pe, l * (6 * OVB) + j * 6 + 12)
                        act.activation(yb[0], psum[:, 2048:3072], ACT.Copy).then_inc(ov_act, 1)
                        act.wait_ge(ov_act, l * (4 * OVB) + j * 4 + 4)
                        act.dma_start(bass.AP(exp_dram.tensor, j * (P * D) + NE * P * D, [[D, P], [1, D]]), yb[0]).then_inc(ov_st, 16)
                        until(act, ov_st, l * (16 * OVB) + j * 16 + 16)
                    with act.Else():
                        act.drain()
                        act.sem_inc(ov_act, 4)
                        act.sem_inc(ov_st, 16)
                for t in range(NT):
                    act.wait_ge(cmb_in[t % 2], (l * 96 if t % 2 == 0 else l * 64) + 32 * (t // 2 + 1))
                    act.activation(xg[t % 2], xg[t % 2], ACT.Copy, scale=wt[:, t, 0:1]).then_inc(weighed, 1)

        @block.gpsimd
        def _(gp):
            gp.memset(mhalf, -0.5)
            gp.memset(yb[0], 0.0).then_inc(zero_ready, 1)
            with gp.Fori(0, DEPTH) as l:
                until(gp, x_ready, nth(l, NT, NT))

                def inv_sqrt(n, dst, src):
                    until(gp, var_ready, nth(l, N_VAR, n))
                    gp.tensor_scalar(dst, src, EPS, None, ALU.add)
                    gp.drain()
                    gp.tensor_tensor(dst, dst, mhalf[:, 0:dst.shape[1]], ALU.pow).then_inc(rstd_ready, 1)

                def add_shift(t):
                    until(gp, scaled, nth(l, NT, t + 1))
                    gp.tensor_tensor(x[:, t, :], x[:, t, :], lnb[:, 1, :], ALU.add).then_inc(x_ready, 1)

                def rotate(u):
                    t = u % 5
                    until(gp, pjA, nth(l, N_PJA, 26 + u))
                    raw = nat(u)
                    cos = cst[:, C_COS + (t - 1) * 64:C_COS + t * 64]
                    sin = cst[:, C_SIN + (t - 1) * 64:C_SIN + t * 64]
                    sn = sin.rearrange("p (a s e) -> p a s e", a=2, s=2)
                    for half in range(2):
                        part = raw[:, half * 256:half * 256 + 256]
                        gp.drain()
                        for s_ in range(2):
                            src = part.rearrange("p (g a s e) -> p g a s e", g=4, a=2, s=2)[:, :, :, 1 - s_, :]
                            out = ropeb.rearrange("p (g a s e) -> p g a s e", g=4, a=2, s=2)[:, :, :, s_, :]
                            gp.tensor_tensor(out, src, sn[:, :, s_, :].unsqueeze(1).to_broadcast([P, 4, 2, 16]), ALU.mult)
                        gp.drain()
                        p3 = part.rearrange("p (g d) -> p g d", g=4)
                        gp.tensor_tensor(p3, p3, cos.unsqueeze(1).to_broadcast([P, 4, 64]), ALU.mult)
                        gp.drain()
                        a = gp.tensor_tensor(part, part, ropeb, ALU.add)
                    gp.drain()
                    gp.sem_inc(r_ready, 1)

                turns = [1, 2, 3, 4, 6, 7, 8]
                for ci, c in enumerate(JOBS):
                    if ci % 2 == 0:
                        if ci:
                            until(gp, o_mm, nth(l, 4, 2))
                        else:
                            until(gp, tr_done, nth(l, N_TR, 10))
                        gp.memset(AT2, 0.0).then_inc(at_zero, 1)
                    until(gp, k_ready, nth(l, 4, ci + 1))
                    for j in range(1, NL + 1):
                        until(gp, E_ready, nth(l, 40, 10 * ci + j))
                        if ci or j > 1:
                            until(gp, lv_mm, nth(l, 64, 16 * ci + 2 * j - 2))
                        gp.tensor_tensor(Kb[:, j % 2], kf[:, c], Eb[:, (j - 1) % 2], ALU.mult).then_inc(K_ready, 1)
                        if ci == 3:
                            rotate(turns[j - 1])
                    until(gp, E_ready, nth(l, 40, 10 * ci + (9 if c < 2 else 8)))
                    until(gp, K_ready, nth(l, 32, 8 * ci + 7))
                    gp.tensor_tensor(kf[:, c], kf[:, c], Eb[:, 0 if c < 2 else 1], ALU.mult).then_inc(K_ready, 1)
                rotate(9)
                inv_sqrt(1, rstd, mv[:, :, 1])
                inv_sqrt(2, rs, ms)
                inv_sqrt(3, rs, ms)
                for t in range(NT):
                    inv_sqrt(4 + t, rstd[:, t:t + 1], mv[:, t, 1:2])
                until(gp, h_stored[0], l * 48 + 48)
                until(gp, h_stored[1], l * 32 + 32)
                until(gp, ids_ready, l + 1)
                with gp.Fori(0, NE // 2) as i:
                    for p in range(2):
                        until(gp, xT_done, nth(l, 2 * NE, i * 4 + 2 * p + 2))
                        gp.tensor_copy(ismall[:, 60 + p:61 + p], ismall[:, bass.ds(i * 2 + (10 + p), 1)])
                        gp.drain()
                        gp.indirect_dma_start(xg[p], None, tok_dram,
                                              bass.IndirectOffsetOnAxis(ap=ismall[:, 60 + p:61 + p], axis=0)).then_inc(xg_in[p], 16)
                until(gp, xT_done, nth(l, 2 * NE, 2 * NE + 2 * PRE))
                nov = gp.value_load(novi[0:1, :], min_val=0, max_val=OVB)
                with gp.Fori(0, OVB) as j:
                    with gp.If(nov > j):
                        until(gp, ov_pe, l * (6 * OVB) + j * 6 + 1)
                        gp.tensor_copy(ismall[:, 62:63], ismall[:, bass.ds(j + (10 + NE), 1)])
                        gp.drain()
                        gp.indirect_dma_start(xg[0], None, tok_dram,
                                              bass.IndirectOffsetOnAxis(ap=ismall[:, 62:63], axis=0)).then_inc(ov_g, 16)
                        until(gp, ov_g, l * (16 * OVB) + j * 16 + 16)
                    with gp.Else():
                        gp.dma_start(spare[0:1, bass.ds(j, 1)], bass.AP(A["router_bias"].tensor, 0, [[1, 1], [1, 1]])).then_inc(ov_g, 16)
                until(gp, ov_g, l * (16 * OVB) + 16 * OVB)
                until(gp, y_stored[0], l * 128 + 144)
                until(gp, y_stored[1], l * 128 + 144)
                until(gp, ov_st, l * (16 * OVB) + 16 * OVB)

                def fetch(t):
                    for q, dst in enumerate((xg[t % 2], yb[t % 2])):
                        gp.indirect_dma_start(dst, None, exp_dram,
                                              bass.IndirectOffsetOnAxis(ap=posi[:, t, q:q + 1], axis=0)).then_inc(cmb_in[t % 2], 16)

                fetch(0)
                fetch(1)
                until(gp, ln2_in, l * 32 + 32)
                for t in range(NT):
                    if t + 2 < NT:
                        until(gp, cmb_used, nth(l, NT, t + 1))
                        fetch(t + 2)
                    inv_sqrt(4 + NT + t, rstd[:, t:t + 1], mv[:, t, 1:2])
                    if t:
                        add_shift(t - 1)
                add_shift(NT - 1)

        @block.vector
        def _(v):
            dr_ = v.drain

            def tt(out, a, b, op=ALU.mult):
                return v.tensor_tensor(out, a, b, op)

            def ts(out, a, s1, s2=None, op0=ALU.mult, op1=ALU.add):
                return v.tensor_scalar(out, a, s1, s2, op0) if s2 is None else v.tensor_scalar(out, a, s1, s2, op0, op1)

            def stt(out, a, s, b, op0, op1):
                return v.scalar_tensor_tensor(out, a, s, b, op0, op1)

            v.wait_ge(consts, 80)
            v.wait_ge(lam_in, 16)
            v.tensor_copy(masks[:], maskf)
            v.tensor_copy(lbm, lbt[:, 0, :])
            for l_ in range(1, DEPTH):
                dr_()
                tt(lbm, lbm, lbt[:, l_, :], ALU.max)
            dr_()
            tt(lbx, lbt, lbm.unsqueeze(1).to_broadcast([P, DEPTH, 4]), ALU.subtract)
            tt(lamp[:, :, 0, :], lamb[:, :, 0, :], lamb[:, :, 1, :])
            tt(lamp[:, :, 1, :], lamb[:, :, 2, :], lamb[:, :, 3, :])
            dr_()
            v.tensor_reduce(lams.rearrange("p (l f) -> p l f", l=DEPTH), lamp, AXX, ALU.add).then_inc(lbs_ready, 1)
            v.wait_ge(lb_exp, 1)
            v.tensor_copy(lbm, lbx[:, 0, :])
            for l_ in range(1, DEPTH):
                dr_()
                tt(lbm, lbm, lbx[:, l_, :], ALU.add)
            dr_()
            v.reciprocal(lbm, lbm)
            dr_()
            tt(lbx, lbx, lbm.unsqueeze(1).to_broadcast([P, DEPTH, 4]))
            v.memset(lbt[:, 0, :], 0.0)
            for l_ in range(1, DEPTH):
                dr_()
                tt(lbt[:, l_, :], lbt[:, l_ - 1, :], lbx[:, l_, :], ALU.add)
            for l_ in range(DEPTH):
                dr_()
                tt(lamn[:, l_:l_ + 1], lams[:, 2 * l_ + 1:2 * l_ + 2], lams[:, 2 * l_:2 * l_ + 1], ALU.subtract)
                dr_()
                ts(lamn[:, l_:l_ + 1], lamn[:, l_:l_ + 1], -lam_init(l_), None, ALU.add)
                v.memset(oml[:, l_:l_ + 1], 1.0 - lam_init(l_))
            v.sem_inc(ada_free, 3)
            v.wait_ge(bias_in, 32)
            with v.Fori(0, 4 * DEPTH) as i:
                for j in range(3):
                    v.wait_ge(ada_mm, i * 3 + j + 4)
                    m_ = ar[0:2, bass.ds(i * (3 * W) + j * W, W)]
                    tt(m_, m_, bank(j)[0:2, :], ALU.add).then_inc(ada_free, 1)
            dr_()
            v.sem_inc(ada_ready, 1)
            v.wait_ge(mod_out, 16)
            v.sem_inc(yB_evac, 2)
            v.sem_inc(y_stored[0], 16)
            v.sem_inc(y_stored[1], 16)
            v.wait_ge(x_in, 16)
            v.sem_inc(x_ready, NT)

            with v.Fori(0, DEPTH) as l:
                dr_()
                v.tensor_copy(lb, lbt[:, bass.ds(l, 1), :].rearrange("p l c -> p (l c)"))
                v.tensor_copy(lamn_l, lamn[:, bass.ds(l, 1)])
                v.tensor_copy(oml_l, oml[:, bass.ds(l, 1)])
                dr_()
                ts(omlb, lb, -1.0, 1.0)
                dr_()
                ts(nomlb, omlb, -1.0)

                def modulated(dst, t, m):
                    y = 0 if t == 0 else 1
                    stt(dst, m[:, y, 1, :], 1.0, x[:, t, :], ALU.add, ALU.mult)
                    dr_()
                    return tt(dst, dst, m[:, y, 0, :], ALU.add)

                v.wait_ge(m01_in, l * 16 + 16)
                for t in range(NT):
                    if t >= 2:
                        v.wait_ge(tr_done, nth(l, N_TR, 2 * (t - 1)))
                    v.wait_ge(x_ready, nth(l, NT, t + 1))
                    modulated(hin[:, t % 2, :], t, ishift).then_inc(h_ready, 1)

                dr_()
                v.wait_ge(tr_done, nth(l, N_TR, 10))
                v.memset(gpad[:, :, 0:1], 0.0)
                v.wait_ge(prm_in, nth(l, 96, 96))
                ts(ag, ag, oml_l)
                def w5(ap):
                    return ap.rearrange("p (w t) -> p w t", w=NT)

                def distance(ci, c, j, dst):
                    m = LEVELS[j]
                    nb = P // (2 * m)
                    b0 = 1 if c < 2 else 0
                    beta = bsum[:, ci % 2, :, b0:b0 + P].rearrange("p w (b u m) -> p w b u m", b=nb, u=2)
                    out = dst.rearrange("p (w b u m) -> p w b u m", w=NT, b=nb, u=2)
                    mid = bsum[:, ci % 2, :, 1:P + 1].rearrange("p w (b u m) -> p w b u m", b=nb, u=2)[:, :, :, 0, m - 1:m]
                    midb = mid.to_broadcast([P, NT, nb, m])
                    tt(out[:, :, :, 1, :], beta[:, :, :, 1, :], midb, ALU.subtract)
                    return tt(out[:, :, :, 0, :], midb, beta[:, :, :, 0, :], ALU.subtract)

                for ci, c in enumerate(JOBS):
                    pair, dr = c % 2, c // 2
                    if ci == 0:
                        until(v, pjA, nth(l, N_PJA, 5))
                    if ci % 2 == 0:
                        if ci:
                            until(v, o_mm, nth(l, 4, 2))
                            until(v, out_s, l * 128 + 64)
                        dr_()
                        v.memset(S2, 0.0)
                        dr_()
                        v.sem_inc(s_zero, 1)
                    dr_()
                    ts(gpad[:, :, 1:P + 1], w5(kf[:, c]), omlb[:, c:c + 1], lb[:, c:c + 1]).then_inc(f_ready, 1)
                    dr_()
                    ts(kf[:, c], kf[:, c], nomlb[:, c:c + 1], omlb[:, c:c + 1]).then_inc(k_ready, 1)
                    v.wait_ge(g_ready, nth(l, 4, ci + 1))
                    v.tensor_tensor_scan(bsum2[:, ci % 2], cst[:, C_SCAN:C_SCAN + BW], gpad2, 0.0, ALU.mult, ALU.add)
                    dr_()
                    if ci:
                        v.wait_ge(K_ready, nth(l, 32, 8 * ci))
                    distance(ci, c, 0, Eb[:, 0]).then_inc(D_ready, 1)
                    distance(ci, c, 1, Eb[:, 1]).then_inc(D_ready, 1)
                    if ci % 2 == 0:
                        until(v, at_zero, nth(l, 2, ci // 2 + 1))

                    def take(j):
                        mk = masks[:, 0 if j == 0 else dr * NL + j, :].unsqueeze(1).to_broadcast([P, NT, P])
                        for h in range(2):
                            dr_()
                            until(v, lv_mm, nth(l, 64, 16 * ci + 2 * j + h + 1))
                            v.copy_predicated(w5(AT[:, dr, h, :]), mk,
                                              w5(psum[:, (3 + 2 * h) * 512:(3 + 2 * h) * 512 + T])).then_inc(lv_acc, 1)

                    if ci == 0:
                        v.wait_ge(pjA, nth(l, N_PJA, 10))
                    for j in range(1, NL + 1):
                        v.wait_ge(E_ready, nth(l, 40, 10 * ci + j))
                        if ci or j > 1:
                            v.wait_ge(lv_mm, nth(l, 64, 16 * ci + 2 * j - 2))
                        tt(Qb[:, j % 2], qf[:, c], Eb[:, (j - 1) % 2]).then_inc(Q_ready, 1)
                        take(j - 1)
                        if j + 1 < NL:
                            dr_()
                            v.wait_ge(K_ready, nth(l, 32, 8 * ci + j))
                            distance(ci, c, j + 1, Eb[:, (j + 1) % 2]).then_inc(D_ready, 1)
                    take(NL)
                    dr_()
                    v.wait_ge(K_ready, nth(l, 32, 8 * ci + 7))
                    b0 = 1 if c < 2 else 0
                    tt(w5(Eb[:, 0]), bsum[:, ci % 2, :, P:P + 1].to_broadcast([P, NT, P]), bsum[:, ci % 2, :, b0:b0 + P],
                       ALU.subtract).then_inc(D_ready, 1)
                    v.wait_ge(E_ready, nth(l, 40, 10 * ci + (8 if c < 2 else 9)))
                    tt(qf[:, c], qf[:, c], Eb[:, 1 if c < 2 else 0]).then_inc(Q_ready, 1)
                    v.wait_ge(E_ready, nth(l, 40, 10 * ci + 10))
                    v.wait_ge(ds_mm, nth(l, 4, ci + 1))
                    if ci % 2 == 0:
                        v.wait_ge(s_init, l * 128 + 64 * (ci // 2 + 1))
                    for w in ([0, 1, 2, 3] if dr == 0 else [0, 4, 3, 2]):
                        ent = (0 if w == 0 else 1 + w) if dr == 0 else (1 if w == 0 else 2 + w)
                        nxt = ent + 1 if dr == 0 else ent - 1
                        st = stt(S[:, dr, nxt, :], S[:, dr, ent, :], eB[:, c, w:w + 1],
                                 psum[:, 2560 + w * P:2560 + (w + 1) * P], ALU.mult, ALU.add)
                        dr_()
                    v.sem_inc(s_ready, 1)
                    if dr == 1:
                        for h in range(2):
                            v.wait_ge(o_mm, nth(l, 4, 2 * pair + h + 1))
                            c0 = (3 + 2 * h) * 512
                            v.tensor_copy(oc[:, :, (2 * pair + h) * 64:(2 * pair + h) * 64 + 64],
                                          w5(psum[:, c0:c0 + T])[:, :, 64 * h:64 * h + 64]).then_inc(o_evac, 1)

                v.wait_ge(pjA, nth(l, N_PJA, 20))
                vv_ = uv[:, :, 256:512]
                for t in range(NT):
                    v.bn_stats(stats[:, t, 0, :], uv[:, t, 256:512])
                dr_()
                for t in range(NT):
                    v.bn_aggr(mv[:, t, :], stats[:, t, 0, :])
                dr_()
                v.sem_inc(var_ready, 1)
                v.wait_ge(rstd_ready, nth(l, N_VAR, 1))
                for t in range(NT):
                    ts(uv[:, t, 256:512], uv[:, t, 256:512], mv[:, t, 0:1], rstd[:, t:t + 1], ALU.subtract, ALU.mult)
                dr_()
                tt(vv_, vv_, mg.unsqueeze(1).to_broadcast([P, NT, 256]))
                dr_()
                tt(vv_, vv_, mb.unsqueeze(1).to_broadcast([P, NT, 256]), ALU.add).then_inc(v_ready, 1)
                sq = view(HG + 8345, 1280, "p (t c) -> p t c", t=NT)
                sq4 = view(HG + 8345, 1280, "p (t h e) -> p (t h) e", t=NT, h=HC)
                oc4 = view(24860, 1280, "p (g e) -> p g e", e=64)
                tt(sq, oc, oc)
                dr_()
                v.tensor_reduce(ms, sq4, AXX, ALU.add)
                dr_()
                ts(ms, ms, 1.0 / 64)
                dr_()
                v.sem_inc(var_ready, 1)
                v.wait_ge(rstd_ready, nth(l, N_VAR, 2))
                tt(oc4, oc4, rs.unsqueeze(2).to_broadcast([P, 20, 64]))
                dr_()
                tt(oc, oc, hg.unsqueeze(1).to_broadcast([P, NT, 256]))
                dr_()
                tt(oc, oc, ig[:, :, 256:512])
                v.wait_ge(sp_mm, l + 1)
                for g in range(GB):
                    c0 = 1536 + g * 64
                    src = psum[:, 1536:2816].rearrange("p (t c) -> p t c", t=NT)[:, :, g * 64:g * 64 + 64]
                    ug = uv[:, :, g * 64:g * 64 + 64]
                    stt(ug, src, bsT[:, g:g + 1], ug, ALU.add, ALU.mult)
                dr_()
                v.sem_inc(sp_used, 1)

                def maxima(n):
                    nk = P if n < 4 else T
                    v.wait_ge(sc_done, nth(l, 20, n + 1))
                    c0 = (n % 2) * 1536
                    v.tensor_reduce(nmx, psum[:, c0:c0 + 1280].rearrange("p (m k) -> p m k", m=2)[:, :, 0:nk], AXX, ALU.max)
                    dr_()
                    ts(negm[:, 2 * n:2 * n + 2], nmx, -SCALE).then_inc(nm_ready, 1)
                    dr_()

                dr_()
                maxima(0)
                for n in range(20):
                    nk = P if n < 4 else T
                    if n + 1 < 20:
                        maxima(n + 1)
                    v.wait_ge(p_ready, nth(l, 20, n + 1))
                    v.reciprocal(rZ[:, 2 * n:2 * n + 2], Z[:, 2 * n:2 * n + 2])
                    dr_()
                    stt(cc[:, n:n + 1], Z[:, 2 * n:2 * n + 1], lamn_l, rZ[:, 2 * n + 1:2 * n + 2], ALU.mult, ALU.mult)
                    dr_()
                    if n >= 2:
                        v.wait_ge(at_tr, nth(l, 20, n - 1))
                    stt(pd[:, n % 2, 0:nk], Pb[:, n % 2, 1, 0:nk], cc[:, n:n + 1], Pb[:, n % 2, 0, 0:nk],
                        ALU.mult, ALU.add).then_inc(pd_ready, 1)
                    t = n // 4 - 1
                    if n % 4 == 1 and t >= 0 or n == 19:
                        for t in ([t] if n < 19 else [4]):
                            until(v, pv_done, nth(l, 20, 4 * t + 4))
                            rz0 = rZ[:, 8 * t:8 * t + 8].rearrange("p (h m) -> p h m", h=HA)[:, :, 0:1]
                            dr_()
                            tt(oa[:, t, :].rearrange("p (h e) -> p h e", h=HA),
                               bank(6 + t % 2).rearrange("p (h e) -> p h e", h=HA),
                               rz0.to_broadcast([P, HA, P])).then_inc(oa_evac, 1)
                dr_()
                sqa = view(HG + 13824, 2560, "p (t c) -> p t c", t=NT)
                tt(sqa, oa, oa)
                dr_()
                v.tensor_reduce(ms, view(HG + 13824, 2560, "p (g e) -> p g e", g=20), AXX, ALU.add)
                dr_()
                ts(ms, ms, 1.0 / P)
                dr_()
                v.sem_inc(var_ready, 1)
                v.wait_ge(rstd_ready, nth(l, N_VAR, 3))
                oa4 = view(HG + 8704, 2560, "p (g e) -> p g e", g=20)
                tt(oa4, oa4, rs.unsqueeze(2).to_broadcast([P, 20, P]))
                dr_()
                tt(oa4, oa4, ag.unsqueeze(1).to_broadcast([P, 20, P])).then_inc(mix_ready, 1)

                def variance(t):
                    dr_()
                    v.bn_aggr(mv[:, t, :], stats[:, t, :, :].rearrange("p s f -> p (s f)"))
                    dr_()
                    v.sem_inc(var_ready, 1)

                def normalised(n, t):
                    v.wait_ge(rstd_ready, nth(l, N_VAR, n + t))
                    ts(x[:, t, :], x[:, t, :], mv[:, t, 0:1], rstd[:, t:t + 1], ALU.subtract, ALU.mult)
                    dr_()
                    return tt(x[:, t, :], x[:, t, :], lnb[:, 0, :])

                def moe_input(t):
                    normalised(4, t)
                    dr_()
                    tt(x[:, t, :], x[:, t, :], lnb[:, 1, :], ALU.add)
                    dr_()
                    if t >= 2:
                        v.wait_ge(tr_done, nth(l, N_TR, 4 * NT + 2 * (t - 1)))
                        v.wait_ge(h_stored[t % 2], (l * 48 if t % 2 == 0 else l * 32) + 16 * (t // 2))
                    modulated(hh[:, t % 2, :], t, shift2).then_inc(h_ready, 1)

                until(v, x_back, l * 16 + 16)
                until(v, m2_in, l * 16 + 16)
                for t in range(NT):
                    y = 0 if t == 0 else 1
                    for half in range(2):
                        n = 35 + 2 * t + half
                        cs = slice(half * W, (half + 1) * W)
                        dr_()
                        v.wait_ge(pj_done, nth(l, N_PJ, n + 1))
                        tt(x1t[half], bank(n % 3), gate_mod[:, y, cs]).then_inc(pjV, 1)
                        dr_()
                        stt(x[:, t, cs], x[:, t, cs], ALPHA, x1t[half], ALU.mult, ALU.add)
                        dr_()
                        v.bn_stats(stats[:, t, half, :], x[:, t, cs])
                    variance(t)
                    if t == 0:
                        until(v, ln1_in, l * 32 + 32)
                        until(v, m34_in, l * 16 + 16)
                    else:
                        moe_input(t - 1)
                moe_input(NT - 1)
                dr_()
                v.sem_inc(x1_ready, 1)

                M, oh1, oh2, sel, key, eq, inm, pos, t1, t2 = R[0], R[1], R[2], R[3], R[4], R[5], R[6], R[7], R[8], R[9]
                g4 = [view(25884 + 800 + 20 * i, 20, "p (t g) -> p t g", t=NT) for i in range(8)]

                def over(v1, n=NE):
                    return v1.unsqueeze(1).to_broadcast([P, NT, n])

                def each_of(vt, n=NE):
                    return vt.to_broadcast([P, NT, n])

                v.wait_ge(rt_score, l + 1)
                tt(sel, score, over(rbias[:]), ALU.add)
                dr_()
                s4 = sel.rearrange("p t (g e) -> p (t g) e", g=4)

                def col(i):
                    return s4[:, :, i]

                def f(i):
                    return g4[i].rearrange("p t g -> p (t g)")

                tt(f(0), col(0), col(1), ALU.max)
                tt(f(1), col(0), col(1), ALU.min)
                tt(f(2), col(2), col(3), ALU.max)
                tt(f(3), col(2), col(3), ALU.min)
                dr_()
                tt(f(4), f(0), f(2), ALU.max)
                tt(f(5), f(0), f(2), ALU.min)
                tt(f(6), f(1), f(3), ALU.max)
                dr_()
                tt(f(5), f(5), f(6), ALU.max)
                dr_()
                tt(gt, g4[4], g4[5], ALU.add)
                dr_()

                def first_best(val, n, wts, best, eq_, onehot):
                    v.tensor_reduce(best, val, AXX, ALU.max)
                    dr_()
                    tt(eq_, val, best.unsqueeze(2).to_broadcast([P, NT, n]), ALU.is_equal)
                    dr_()
                    tt(eq_, eq_, over(wts, n))
                    dr_()
                    v.tensor_reduce(best, eq_, AXX, ALU.max)
                    dr_()
                    tt(onehot, eq_, best.unsqueeze(2).to_broadcast([P, NT, n]), ALU.is_equal)
                    dr_()

                bst = wsum
                first_best(gt, 4, cst[:, C_W4:C_W4 + 4], bst, g4[0], g4[1])
                inm4 = inm.rearrange("p t (g e) -> p (t g) e", g=4)
                v.tensor_copy(inm4, f(1).unsqueeze(2).to_broadcast([P, 20, 4]))
                dr_()
                tt(sel, sel, inm)
                ts(t1, inm, NEG, -NEG)
                dr_()
                tt(sel, sel, t1, ALU.add)
                dr_()
                first_best(sel, NE, cst[:, C_W16:C_W16 + NE], bst, key, oh1)
                stt(sel, oh1, -2 * NEG, sel, ALU.mult, ALU.add)
                dr_()
                first_best(sel, NE, cst[:, C_W16:C_W16 + NE], bst, key, oh2)
                tt(M, oh1, oh2, ALU.add).then_inc(m_ready, 1)
                for q, oh in enumerate((oh1, oh2)):
                    dr_()
                    tt(t1, oh, score)
                    dr_()
                    v.tensor_reduce(wt[:, :, q], t1, AXX, ALU.add)
                dr_()
                tt(wsum, wt[:, :, 0], wt[:, :, 1], ALU.add)
                dr_()
                v.reciprocal(wsum, wsum)
                dr_()
                tt(wt, wt, wsum.unsqueeze(2).to_broadcast([P, NT, 2]))
                v.wait_ge(rank_mm, l + 1)
                rank = bank(4)[:, 0:80].rearrange("p (t e) -> p t e", t=NT)
                cnt = bank(4)[:, 80:96]
                ts(ovc, cnt, 128.0, None, ALU.is_gt)
                for r_ in (256.0, 384.0, 512.0):
                    dr_()
                    stt(ovc, cnt, r_, ovc, ALU.is_gt, ALU.add)
                dr_()
                v.tensor_tensor_scan(ovi, cst[:, C_TRI + P:C_TRI + P + NE], ovc, 0.0, ALU.mult, ALU.add)
                dr_()
                tt(ovx, ovi, ovc, ALU.subtract)
                v.tensor_copy(novi, ovi[:, NE - 1:NE])
                tt(R9, ovi.unsqueeze(1).to_broadcast([P, OVB, NE]),
                   cst[:, C_IOTA:C_IOTA + OVB].unsqueeze(2).to_broadcast([P, OVB, NE]), ALU.is_le)
                dr_()
                v.tensor_reduce(R9s, R9, AXX, ALU.add)
                dr_()
                ts(R9s, R9s, float(NE - 1), None, ALU.min)
                dr_()
                v.tensor_copy(bexi, R9s)
                e128 = cst[:, C_E128:C_E128 + NE]
                ts(ovx, ovx, 128.0, float(NE * P - P))
                dr_()
                tt(ovx, ovx, e128, ALU.subtract)
                tt(pos, rank, over(e128), ALU.add)
                ts(t1, rank, 128.0, None, ALU.is_ge)
                dr_()
                tt(t1, t1, over(ovx))
                dr_()
                tt(pos, pos, t1, ALU.add)
                for q, oh in enumerate((oh1, oh2)):
                    dr_()
                    tt(t2, oh, pos)
                    dr_()
                    v.tensor_reduce(psn[:, :, q], t2, AXX, ALU.add)
                dr_()
                v.tensor_copy(posi, psn)
                dr_()
                v.sem_inc(pos_ready, 1)
                ts(rowi, ismall[:, 0:10], P - 1, None, ALU.bitwise_and)
                ts(blki, ismall[:, 0:10], 7, None, ALU.logical_shift_right)
                dr_()
                v.tensor_copy(rowf, rowi)
                v.tensor_copy(blkf, blki)
                dr_()
                for a in range(2 * NT):
                    tok = cst[:, C_TOK + a // 2:C_TOK + a // 2 + 1]
                    ts(at_row[:, a, :], cst[:, C_IOTA:C_IOTA + P], rowf[:, a:a + 1], None, ALU.is_equal)
                    ts(at_block[:, a, :], cst[:, C_IOTA:C_IOTA + NB], blkf[:, a:a + 1], tok, ALU.is_equal, ALU.mult)
                dr_()
                v.sem_inc(at_ready, 1)
                v.wait_ge(id_mm, l + 1)
                v.tensor_copy(ids, bank(5)[:, 0:NB])
                dr_()
                v.sem_inc(ids_ready, 1)

                with v.Fori(0, NE // 2) as i:
                    for p in range(2):
                        v.wait_ge(xT_done, nth(l, 2 * NE, i * 4 + 2 * p + 2 + 2 * PRE))
                        v.tensor_copy(xgT[p][:, 4:8, :], bank(7).rearrange("p (k t) -> p k t", k=4)).then_inc(xT_dve, 1)
                    for p in range(2):
                        v.wait_ge(up_done, nth(l, NE, i * 2 + p + 1 + PRE))
                        v.wait_ge(sg_ready, nth(l, NE, i * 2 + p + 1))
                        tt(av[p], sg[p], bank(2 * p + 1)).then_inc(a_ready, 1)
                    for half in range(2):
                        v.wait_ge(y_done, nth(l, 2 * NE, i * 4 + 1 + half + 2 * PRE))
                        if half == 0:
                            v.wait_ge(y_stored[0], l * 128 + i * 16 + 16)
                        v.tensor_copy(yb[0][:, half * W:(half + 1) * W], bank(4 + half)).then_inc(yA_evac, 1)
                dr_()
                nov = v.value_load(novi[0:1, :], min_val=0, max_val=OVB)
                with v.Fori(0, OVB) as j:
                    with v.If(nov > j):
                        v.wait_ge(ov_pe, l * (6 * OVB) + j * 6 + 9)
                        v.wait_ge(ov_act, l * (4 * OVB) + j * 4 + 2)
                        tt(av[0], sg[0], bank(1)).then_inc(ov_dve, 1)
                    with v.Else():
                        v.drain()
                        v.sem_inc(ov_dve, 1)

                until(v, m5_in, l * 16 + 16)
                for t in range(NT):
                    y = 0 if t == 0 else 1
                    a, b = xg[t % 2], yb[t % 2]
                    dr_()
                    v.wait_ge(cmb_in[t % 2], (l * 96 if t % 2 == 0 else l * 64) + 32 * (t // 2 + 1))
                    v.wait_ge(weighed, nth(l, NT, t + 1))
                    stt(a, b, wt[:, t, 1:2], a, ALU.mult, ALU.add)
                    dr_()
                    tt(a, a, gate_mod[:, y, :])
                    dr_()
                    stt(x[:, t, :], x[:, t, :], ALPHA, a, ALU.mult, ALU.add).then_inc(cmb_used, 1)
                    dr_()
                    for half in range(2):
                        v.bn_stats(stats[:, t, half, :], x[:, t, half * W:(half + 1) * W])
                    variance(t)
                    if t == 0:
                        until(v, ln2_in, l * 32 + 32)
                    else:
                        normalised(4 + NT, t - 1).then_inc(scaled, 1)
                normalised(4 + NT, NT - 1).then_inc(scaled, 1)


def shape_constants(np):
    c = np.zeros((P, C_END), np.float32)
    c[:, C_ID:C_ID + P] = np.eye(P)
    c[:, C_TRI:C_TRI + P] = np.triu(np.ones((P, P)), 1)
    c[:, C_TRI + P:C_TRI + 2 * P] = 1.0
    c[:, C_W4:C_W4 + 4] = np.arange(4, 0, -1)
    c[:, C_W16:C_W16 + NE] = np.arange(NE, 0, -1)
    c[:, C_E128:C_E128 + NE] = np.arange(NE) * P
    c[:, C_IOTA:C_IOTA + P] = np.arange(P)
    c[:, C_TOK:C_TOK + NT] = np.arange(P)[:, None] + P * np.arange(NT)[None]
    inv = (10000.0 ** (-np.arange(16, dtype=np.float32) / 16)).astype(np.float32)
    pos = np.arange(512)
    cos, sin = np.zeros((512, 64), np.float32), np.zeros((512, 64), np.float32)
    for half, q in enumerate((pos // 64, pos % 64)):
        ang = q[:, None].astype(np.float32) * inv
        o = half * 32
        cos[:, o:o + 16] = cos[:, o + 16:o + 32] = np.cos(ang)
        sin[:, o:o + 16], sin[:, o + 16:o + 32] = -np.sin(ang), np.sin(ang)
    c[:, C_COS:C_COS + 256] = cos.reshape(4, P, 64).transpose(1, 0, 2).reshape(P, 256)
    c[:, C_SIN:C_SIN + 256] = sin.reshape(4, P, 64).transpose(1, 0, 2).reshape(P, 256)
    scan = np.ones((NT, P + 1), np.float32)
    scan[:, 0] = 0
    c[:, C_SCAN:C_END] = scan.reshape(1, -1)
    m = np.zeros((P, 2 * NL + 1, P), np.float32)
    s, t = np.arange(P)[:, None], np.arange(P)[None]
    m[:, 0] = s == t
    for j, h in enumerate(LEVELS):
        same = s // (2 * h) == t // (2 * h)
        su, tu = (s // h) % 2, (t // h) % 2
        m[:, 1 + j] = same & (su == 0) & (tu == 1)
        m[:, 1 + NL + j] = same & (su == 1) & (tu == 0)
    return c, m


def kernel(**inputs):
    import numpy as np
    import concourse.bacc as bacc
    from concourse import mybir as mb
    from concourse.bass_utils import run_bass_kernel_spmd as run

    g = {k: np.asarray(a) for k, a in inputs.items()}
    cst, masks = shape_constants(np)
    cond = np.stack([g["c_ctx"], g["c"][0]])
    arrays = {
        "x": np.concatenate([g["x_prompt"][0], g["x_sample"][0]]),
        "condT": cond.reshape(2, KD, P).transpose(2, 1, 0),
        "w_ada": g["w_ada"], "b_ada": g["b_ada"], "w_in": g["w_in"], "w_out": g["w_out"],
        "diff_lambda": g["diff_lambda"], "attn_norm_g": g["attn_norm_g"],
        "mlp_ln_g": g["mlp_ln_g"], "mlp_ln_b": g["mlp_ln_b"],
        "wsT": g["w_spatial"].transpose(0, 3, 1, 2), "bsT": g["b_spatial"].transpose(0, 2, 1),
        "lbT": g["hgrn_lb"].reshape(2, DEPTH, 2, P).transpose(3, 1, 0, 2).reshape(P, DEPTH, 4),
        "hgrn_norm_g": g["hgrn_norm_g"], "ln_g": g["ln_g"], "ln_b": g["ln_b"],
        "w_router": g["w_router"], "router_bias": g["router_bias"],
        "w_gate": g["w_gate"], "w_up": g["w_up"], "w_down": g["w_down"],
        "kcT": g["cache_k"][0].transpose(0, 3, 4, 2, 1).reshape(DEPTH, P, HA, P),
        "cache_v": g["cache_v"][0].reshape(DEPTH, P, 512),
        "state": g["state_hgrn"][0],
        "cst": cst, "masks": masks,
    }
    outs = {"y": (T, D), "new_k": (DEPTH, P, 512), "new_v": (DEPTH, P, 512), "new_s": (DEPTH, 2, HC, 64, 64)}
    nc = bacc.Bacc("TRN2", target_bir_lowering=False, num_devices=1)
    A = {}
    for name in arrays:
        arrays[name] = np.ascontiguousarray(arrays[name])
        A[name] = nc.dram_tensor(name, list(arrays[name].shape), mb.dt.from_np(arrays[name].dtype), kind="ExternalInput").ap()
    for name, shape in outs.items():
        A[name] = nc.dram_tensor(name, list(shape), mb.dt.float32, kind="ExternalOutput").ap()
    build_program(nc, A)
    r = run(nc, [arrays], core_ids=[0]).results[0]
    y = r["y"]
    return (y[:P].reshape(1, P, D), y[P:].reshape(1, T - P, D),
            r["new_k"].reshape(1, DEPTH, P, HA, 2, DQ), r["new_v"].reshape(1, DEPTH, P, HA, 128),
            r["new_s"].reshape(1, DEPTH, 2, HC, 64, 64))
```

```python
import math
from contextlib import ExitStack

import concourse.bass as bass
from concourse import mybir
from concourse.alu_op_type import AluOpType as ALU

ACT = mybir.ActivationFunctionType
AXX = mybir.AxisListType.X
F32 = mybir.dt.float32
I32 = mybir.dt.int32
U8 = mybir.dt.uint8

P = 128
D = 1024
DEPTH = 2
NT = 5
T = NT * P
KD = D // P
NIN = 3584
HA = 4
DQ = 64
SCALE = DQ ** -0.5
HC = 4
JOBS = [0, 2, 1, 3]
UNITS = [
    [(10, 0, 0), (11, 1, 1), (12, 2, 2), (13, 3, 3), (14, 4, 4), (15, 5, 6), (16, 7, 8)],
    *[[(n, 0, 0), (n + 1, 1, 1), (n + 2, 2, 2), (n + 3, 3, 4), (n + 4, 5, 6), (n + 5, 7, 8)] for n in (17, 23, 29)]]
LEVELS = [64, 32, 16, 8, 4, 2, 1]
NL = len(LEVELS)
GB = 4
NE = 16
DFF = 512
OVB = 9
NB = NE + OVB
NEG = 1e30
ALPHA = (2 * DEPTH) ** 0.25
EPS = 1e-5
W = 512
SLOT = KD * W

COLS = {"F": 2304, "Q": 2816, "I": 2048, "G": 3328, "UV": 1536, "VA": 1024, "KA": 512, "QA": 0}

N_PJ, N_PJA, N_PJV = 45, 35, 10
N_TR, N_VAR, N_ROW = 6 * NT, 2 + 3 * NT, 16

C_ID, C_TRI, C_W4, C_W16, C_E128, C_IOTA, C_TOK, C_COS, C_SIN, C_SCAN, C_END = (
    0, 128, 384, 388, 404, 420, 548, 553, 809, 1065, 1710)


def nth(l, per, n):
    return l * per + n


def loadsA(l, j, uses):
    return l * (192 if j == 2 else 176) + (16 * DEPTH + 16 * uses + (16 if j == 2 else 0))


def lam_init(l):
    return 0.8 - 0.6 * math.exp(-0.3 * l)


def build_program(nc, A):
    with ExitStack() as ctx:
        def sb(name, shape, dt=F32):
            return ctx.enter_context(nc.sbuf_tensor("sb_" + name, shape, dt))

        def sem(name):
            return ctx.enter_context(nc.semaphore(name))

        def dram(name, shape):
            return nc.dram_tensor(name, shape, F32, kind="Internal").ap()

        mod_dram = dram("mod_dram", [DEPTH, 2, 6 * D])
        tok_dram = dram("tok_dram", [T, D])
        x_dram = dram("x_dram", [T, D])
        exp_dram = dram("exp_dram", [NB * P, D])

        wA = sb("wA", [P, 3 * SLOT])
        x = sb("x", [P, NT, D])
        gate_mod = sb("gate_mod", [P, 2, D])
        cst = sb("cst", [P, C_END])
        masks = sb("masks", [P, 2 * NL + 1, P], U8)
        prm = sb("prm", [P, 1412])
        rw = sb("rw", [P, KD, NE])
        rbias = sb("rbias", [P, NE])
        condT = sb("condT", [P, KD, 2])
        small = sb("small", [P, 640])
        ismall = sb("ismall", [P, 64], I32)
        arena = sb("arena", [P, 28956])
        psum = ctx.enter_context(nc.psum_tensor("psum", [P, 4096], F32))

        ident = cst[:, C_ID:C_ID + P]

        def nat(u):
            return x[:, u % 5, (u // 5) * 512:(u // 5) * 512 + 512]
        ar = arena

        def view(off, n, pattern=None, **kw):
            v = ar[:, off:off + n]
            return v.rearrange(pattern, **kw) if pattern else v

        HG = 5120
        hT = view(0, 5120, "p (k t) -> p k t", k=KD)
        kf = view(HG, 2560, "p (c t) -> p c t", c=4)
        qf = view(HG + 2560, 2560, "p (c t) -> p c t", c=4)
        BW = NT * (P + 1)
        bsum = view(HG + 5120, 2 * BW, "p (s w j) -> p s w j", s=2, w=NT)
        bsum2 = view(HG + 5120, 2 * BW, "p (s w) -> p s w", s=2)
        gpad = view(HG + 7700, BW, "p (w j) -> p w j", w=NT)
        gpad2 = view(HG + 7700, BW)
        Qb = view(HG + 8345, 1280, "p (s t) -> p s t", s=2)
        Kb = view(HG + 9625, 1280, "p (s t) -> p s t", s=2)
        Eb = view(HG + 10905, 1280, "p (s t) -> p s t", s=2)
        KEn = view(HG + 12185, 640, "p (w d) -> p w d", w=NT)
        AT = view(HG + 12825, 2560, "p (r h t) -> p r h t", r=2, h=2)
        AT2 = view(HG + 12825, 2560)
        S = view(HG + 15385, 1792, "p (r s e) -> p r s e", r=2, s=7)
        S2 = view(HG + 15385, 1792)
        ishift = view(HG + 7168, 4096, "p (y m d) -> p y m d", y=2, m=2)
        hin = view(HG + 13312, 2048, "p (s d) -> p s d", s=2)
        qT = view(HG, 2560, "p (h t) -> p h t", h=HA)
        kT = view(HG + 2560, 3072, "p (h t) -> p h t", h=HA)
        vv = [gate_mod[:, s // 2, (s % 2) * 512:(s % 2) * 512 + 512] for s in range(4)] + [
            view(HG + 6410, 512), view(HG + 6922, 512)]
        oa = view(HG + 8704, 2560, "p (t c) -> p t c", t=NT)
        Pb = view(HG + 11264, 2560, "p (s m k) -> p s m k", s=2, m=2)
        pd = view(HG + 13824, 1280, "p (s k) -> p s k", s=2)
        pdT = view(HG + 15104, 1280, "p (s k) -> p s k", s=2)
        ropeb = view(28700, 256)
        lnb = view(HG + 11264, 2048, "p (m d) -> p m d", m=2)
        ig = view(22300, 2560, "p (t c) -> p t c", t=NT)
        oc = view(24860, 1280, "p (t c) -> p t c", t=NT)
        uv = view(26140, 2560, "p (t c) -> p t c", t=NT)
        wB = 0
        shift2 = view(18432, 4096, "p (y m d) -> p y m d", y=2, m=2)
        hh = view(22528, 2048, "p (s d) -> p s d", s=2)
        hTt = view(24860, 1024, "p (k t) -> p k t", k=KD)
        xg = [view(25884 + 1024 * s, 1024) for s in range(2)]
        xgT = [view(12288 + 1024 * s, 1024, "p (k t) -> p k t", k=KD) for s in range(2)]
        av = [view(14336 + 512 * s, 512) for s in range(2)]
        aT = [view(15360 + 512 * s, 512, "p (k t) -> p k t", k=4) for s in range(2)]
        by_weight = view(0, 10 * P, "p (a r) -> p a r", a=10)
        late = [view(10 * P + i * D, D) for i in range(2 * NT - 4)]
        ysum = view(22528, 1024)
        x1t = [view(12288 + 512 * s, 512) for s in range(2)]
        sg = [view(22528 + 512 * s, 512) for s in range(2)]
        yb = [view(23552, 1024), view(27932, 1024)]
        expert_rows = [(xg[0], yb[0]), (xg[1], yb[1])] + [(late[2 * i], late[2 * i + 1]) for i in range(NT - 2)]
        slotM = view(0, SLOT)
        mrow = ar[0:2, SLOT:SLOT + DEPTH * 2 * D]
        mrow2 = ar[0:2, 0:4 * D]
        zeros = view(28700, 256)
        at_row = view(12288, 10 * P, "p (a r) -> p a r", a=10)
        at_block = view(12288 + 10 * P, 10 * NB, "p (a b) -> p a b", a=10)

        def slotA(j):
            return wA[:, j * SLOT:(j + 1) * SLOT]

        def slotB(j):
            return ar[:, wB + j * SLOT:wB + (j + 1) * SLOT]

        def bank(i, n=512):
            return psum[:, i * 512:i * 512 + n]

        ag, hg, mg, mb = prm[:, 0:128], prm[:, 128:384], prm[:, 384:640], prm[:, 640:896]
        wsT = prm[:, 896:1408].rearrange("p (g i) -> p g i", g=GB)
        bsT = prm[:, 1408:1412]

        o = [0]

        def sm(n):
            o[0] += n
            return small[:, o[0] - n:o[0]]

        lbt = sm(DEPTH * 4).rearrange("p (l c) -> p l c", l=DEPTH)
        lbx = sm(DEPTH * 4).rearrange("p (l c) -> p l c", l=DEPTH)
        lbm, lb, omlb, nomlb = sm(4), sm(4), sm(4), sm(4)
        lams, lamn, lamn_l, oml, oml_l = sm(DEPTH * 2), sm(DEPTH), sm(1), sm(DEPTH), sm(1)
        eB = sm(20).rearrange("p (c w) -> p c w", c=4)
        stats = sm(60).rearrange("p (t s f) -> p t s f", t=NT, s=2)
        mv = sm(10).rearrange("p (t f) -> p t f", t=NT)
        rstd, nmean, nmr = sm(NT), sm(NT), sm(NT)
        ms, rs, msa, rsa = sm(20), sm(20), sm(20), sm(20)
        nmx, negm = sm(2), sm(40)
        Z, rZ, cc = sm(40), sm(40), sm(20)
        score = sm(80).rearrange("p (t e) -> p t e", t=NT)
        gt = sm(20).rearrange("p (t g) -> p t g", t=NT)
        ovc, ovi, ovx = sm(NE), sm(NE), sm(NE)
        wt = sm(10).rearrange("p (t k) -> p t k", t=NT)
        psn = sm(10).rearrange("p (t k) -> p t k", t=NT)
        wsum = sm(NT)
        mhalf = sm(20)
        spare = sm(OVB)
        posi = ismall[:, 0:10].rearrange("p (t k) -> p t k", t=NT)
        rowi, blki = ismall[:, 50:60], sb("blki", [P, 10], I32)[:]
        rowf, blkf = sm(10), sm(10)
        ids = ismall[:, 10:10 + NB]
        novi = ismall[:, 36:37]
        bexi = ismall[:, 40:40 + OVB]
        R = [view(25884 + 80 * i, 80, "p (t e) -> p t e", t=NT) for i in range(12)]
        chosen = view(25884, 80)
        before = view(27300, 96)
        R9 = view(25884 + 960, OVB * NE, "p (j e) -> p j e", j=OVB)
        R9s = view(25884 + 960 + 144, OVB)
        lamb = view(12288, DEPTH * 4 * 64, "p (l f d) -> p l f d", l=DEPTH, f=4)
        maskf = view(14336, (2 * NL + 1) * P, "p (m t) -> p m t", m=2 * NL + 1)
        lamp = view(13312, DEPTH * 2 * 64, "p (l f d) -> p l f d", l=DEPTH, f=2)

        x_in, consts, lam_in = sem("x_in"), sem("consts"), sem("lam_in")
        bias_in = sem("bias_in")
        cond_ready, ada_mm, ada_free = sem("cond_ready"), sem("ada_mm"), sem("ada_free")
        ada_ready, mod_out = sem("ada_ready"), sem("mod_out")
        zero_out = sem("zero_out")
        lb_exp = sem("lb_exp")
        lbs_ready = sem("lbs_ready")
        landedA = [sem(f"landedA{j}") for j in range(3)]
        landedB = [sem(f"landedB{j}") for j in range(3)]
        landed_m, landed_h = sem("landed_m"), [sem("landed_h0"), sem("landed_h1")]
        row_mm, row_sum, bias2_in, m25_out = sem("row_mm"), sem("row_sum"), sem("bias2_in"), sem("m25_out")
        x_ready, x_spilled, x_back = sem("x_ready"), sem("x_spilled"), sem("x_back")
        m01_in, m2_in, prm_in, ln1_in = sem("m01_in"), sem("m2_in"), sem("prm_in"), sem("ln1_in")
        m34_in, m5_in, ln2_in, kv_in = sem("m34_in"), sem("m5_in"), sem("ln2_in"), sem("kv_in")
        h_ready, tr_done, tr_evac = sem("h_ready"), sem("tr_done"), sem("tr_evac")
        pj_done, pjA, pjV = sem("pj_done"), sem("pjA_evac"), sem("pjV_evac")
        f_ready, g_ready, k_ready = sem("f_ready"), sem("g_ready"), sem("k_ready")
        D_ready, E_ready, Q_ready, K_ready = sem("D_ready"), sem("E_ready"), sem("Q_ready"), sem("K_ready")
        lv_mm, lv_acc, at_zero = sem("lv_mm"), sem("lv_acc"), sem("at_zero")
        s_zero, s_init, s_ready = sem("s_zero"), sem("s_init"), sem("s_ready")
        ke_t, ke_evac, ds_mm = sem("ke_t"), sem("ke_evac"), sem("ds_mm")
        o_mm, o_evac = sem("o_mm"), sem("o_evac")
        var_ready, rstd_ready, centred, scaled = sem("var_ready"), sem("rstd_ready"), sem("centred"), sem("scaled")
        v_ready, sp_mm, sp_used = sem("v_ready"), sem("sp_mm"), sem("sp_used")
        r_ready, r_tr, r_evac = sem("r_ready"), sem("r_tr"), sem("r_evac")
        sc_done, nm_ready, p_ready, pd_ready = sem("sc_done"), sem("nm_ready"), sem("p_ready"), sem("pd_ready")
        sc_first = sem("sc_first")
        at_tr, at_evac, pv_done, oa_evac = sem("at_tr"), sem("at_evac"), sem("pv_done"), sem("oa_evac")
        mix_ready, x1_ready = sem("mix_ready"), sem("x1_ready")
        h_stored = [sem("h_stored0"), sem("h_stored1")]
        rt_mm, rt_score, m_ready, rank_mm = sem("rt_mm"), sem("rt_score"), sem("m_ready"), sem("rank_mm")
        pos_ready, at_ready, id_mm, ids_ready = sem("pos_ready"), sem("at_ready"), sem("id_mm"), sem("ids_ready")
        xg_in = [sem("xg_in0"), sem("xg_in1")]
        xT_done, xT_act, xT_dve = sem("xT_done"), sem("xT_act"), sem("xT_dve")
        gate_done, up_done, sg_ready, a_ready = sem("gate_done"), sem("up_done"), sem("sg_ready"), sem("a_ready")
        aT_done, aT_ready, y_done = sem("aT_done"), sem("aT_ready"), sem("y_done")
        yA_evac, yB_evac = sem("yA_evac"), sem("yB_evac")
        y_stored = [sem("y_stored0"), sem("y_stored1")]
        ov_w = [sem("ov_w0"), sem("ov_w1"), sem("ov_w2")]
        ov_g, ov_pe, ov_act, ov_dve, ov_st = (
            sem("ov_g"), sem("ov_pe"), sem("ov_act"), sem("ov_dve"), sem("ov_st"))
        cmb_in = [sem(f"cmb_in{t}") for t in range(NT)]
        cmb_mm, cmb_used, weights_ready = sem("cmb_mm"), sem("cmb_used"), sem("weights_ready")
        out_k, out_v, out_s, out_y = sem("out_k"), sem("out_v"), sem("out_s"), sem("out_y")

        passed = {e.engine: sem("passed_" + nm) for nm, e in (
            ("sp", nc.sync), ("pe", nc.tensor), ("act", nc.scalar), ("gp", nc.gpsimd), ("dve", nc.vector))}
        PRE = 2

        def until(eng, signal, n):
            eng.wait_ge(signal, n)
            eng.sem_inc(passed[eng.engine], 1)

        def in_block(l, c0, w=W):
            return bass.AP(A["w_in"].tensor, l * (D * NIN) + c0, [[NIN, P], [P * NIN, KD], [1, w]])

        def out_block(l, c0):
            return bass.AP(A["w_out"].tensor, l * (D * D) + c0, [[D, P], [P * D, KD], [1, W]])

        def gate_up(name, l, e):
            return bass.AP(A[name].tensor, (l * NE + e) * (D * DFF), [[DFF, P], [P * DFF, KD], [1, DFF]])

        def down(l, e):
            return bass.AP(A["w_down"].tensor, (l * NE + e) * (D * DFF), [[D, P], [P * D, 4], [1, D]])

        def rows(name, off, n):
            return bass.AP(A[name].tensor, off, [[0, P], [1, n]])

        def mod_rows(l, m, n):
            return bass.AP(mod_dram.tensor, l * (12 * D) + m * D, [[0, P], [6 * D, 2], [1, n * D]])

        def s3(v, k=KD):
            return v.rearrange("p (k c) -> p k c", k=k)

        def ada_block(l, c0, w):
            return bass.AP(A["w_ada"].tensor, l * (6 * D * D) + c0, [[6 * D, P], [P * 6 * D, KD], [1, w]])

        slots4, landed4 = [slotA(0), slotA(1), slotA(2), slotM], landedA + [landed_m]
        halves = [s3(slotA(0)[:, h * (SLOT // 2):(h + 1) * (SLOT // 2)]) for h in range(2)]

        block = ctx.enter_context(nc.Block())

        @block.sync
        def _(sp):
            sp.dma_start(condT[:], A["condT"]).then_inc(bias_in, 16)
            sp.dma_start(mrow.rearrange("y (l d) -> y l d", l=DEPTH),
                         bass.AP(A["b_ada"].tensor, 0, [[0, 2], [6 * D, DEPTH], [1, 2 * D]])).then_inc(bias_in, 16)
            with sp.Fori(0, DEPTH) as la:
                for j in range(4):
                    until(sp, ada_mm, nth(la, 4, j + 1))
                    sp.dma_start(s3(slots4[j]), ada_block(la, j * W, W)).then_inc(landed4[j], 16)
            with sp.Fori(0, DEPTH) as l:
                order = ["F", "Q", "I", "UV", "VA", "KA", "QA"]
                for b, nm in enumerate(order):
                    if b >= 3:
                        until(sp, pj_done, nth(l, N_PJ, 5 * (b - 2)))
                    else:
                        sp.wait_ge(ada_mm, 4 * DEPTH + b + 1)
                        sp.sem_inc(passed[sp.engine], 1)
                    dst = s3(slotA(b % 3))
                    if nm == "I":
                        sp.dma_start(dst[:, :, 0:256], in_block(l, COLS["I"], 256)).then_inc(landedA[2], 16)
                        sp.dma_start(dst[:, :, 256:512], in_block(l, COLS["G"], 256)).then_inc(landedA[2], 16)
                    else:
                        sp.dma_start(dst, in_block(l, COLS[nm])).then_inc(landedA[b % 3], 16)
                    if b == 0:
                        sp.wait_ge(mod_out, 16)
                        sp.sem_inc(passed[sp.engine], 1)
                        sp.wait_ge(lbs_ready, 1)
                        sp.sem_inc(passed[sp.engine], 1)
                        sp.dma_start(ishift.rearrange("p y m d -> p y (m d)"), mod_rows(l, 0, 2)).then_inc(m01_in, 16)
                for half in range(2):
                    b = 7 + half
                    until(sp, pj_done, nth(l, N_PJ, 5 * (b - 2)))
                    sp.dma_start(s3(slotA(b % 3)), out_block(l, half * W)).then_inc(landedA[b % 3], 16)
                until(sp, pj_done, nth(l, N_PJ, 35))
                for i in range(N_ROW):
                    if i >= 2:
                        until(sp, row_mm, nth(l, N_ROW, i - 1))
                    sp.dma_start(halves[i % 2], ada_block(l, 2 * D + i * 256, 256)).then_inc(landed_h[i % 2], 16)
                until(sp, pj_done, nth(l, N_PJ, N_PJ))
                with sp.Fori(0, NE // 2) as i:
                    for p in range(2):
                        slot, landed = ((slotA, landedA), (slotB, landedB))[p]
                        until(sp, gate_done, nth(l, NE, i * 2 + p + PRE - 1))
                        sp.dma_start(s3(slot(0)), gate_up("w_gate", l, i * 2 + p)).then_inc(landed[0], 16)
                        until(sp, up_done, nth(l, NE, i * 2 + p + PRE - 1))
                        sp.dma_start(s3(slot(1)), gate_up("w_up", l, i * 2 + p)).then_inc(landed[1], 16)
                        until(sp, y_done, nth(l, 2 * NE, i * 4 + 2 * p + 2))
                        sp.dma_start(s3(slot(2), 4), down(l, i * 2 + p)).then_inc(landed[2], 16)
                until(sp, pos_ready, l + 1)
                nov = sp.value_load(novi[0:1, :], min_val=0, max_val=OVB)
                with sp.Fori(0, OVB) as j:
                    with sp.If(nov > j):
                        ex = sp.value_load(bexi[0:1, bass.ds(j, 1)], min_val=0, max_val=NE - 1)
                        until(sp, gate_done, nth(l, NE, NE - 1 + PRE))
                        until(sp, ov_pe, l * (6 * OVB) + j * 6 + 2)
                        sp.dma_start(s3(slotA(0)), gate_up("w_gate", l, ex)).then_inc(ov_w[0], 16)
                        until(sp, up_done, nth(l, NE, NE - 1 + PRE))
                        until(sp, ov_pe, l * (6 * OVB) + j * 6 + 3)
                        sp.dma_start(s3(slotA(1)), gate_up("w_up", l, ex)).then_inc(ov_w[1], 16)
                        until(sp, y_done, nth(l, 2 * NE, 2 * NE - 2 + 2 * PRE))
                        until(sp, ov_pe, l * (6 * OVB) + j * 6 + 6)
                        sp.dma_start(s3(slotA(2), 4), down(l, ex)).then_inc(ov_w[2], 16)
                        for landed in ov_w:
                            until(sp, landed, l * (16 * OVB) + j * 16 + 16)
                    with sp.Else():
                        for landed in ov_w:
                            sp.sem_inc(landed, 16)
                until(sp, cmb_in[NT - 1], l * 32 + 32)
            for t in range(NT):
                sp.wait_ge(x_ready, DEPTH * NT + t + 1)
                sp.dma_start(A["y"][t * P:(t + 1) * P, :], x[:, t, :]).then_inc(out_y, 16)
            until(sp, out_y, 16 * NT)
            until(sp, out_k, 16 * DEPTH)
            until(sp, out_v, 16 * DEPTH)
            until(sp, out_s, 128 * DEPTH)

        @block.tensor
        def _(pe):
            pe.sem_inc(ada_mm, 4)
            pe.wait_ge(cond_ready, 1)
            with pe.Fori(0, DEPTH) as la:
                for j in range(4):
                    pe.wait_ge(landed4[j], la * 16 + 16)
                    pe.wait_ge(ada_free, nth(la, 4, j + 1))
                    w = s3(slots4[j])
                    for k in range(KD):
                        mm = pe.matmul(bank(j)[0:2, :], condT[:, k, :], w[:, k, :], start=k == 0, stop=k == KD - 1)
                    mm.then_inc(ada_mm, 1)
            pe.wait_ge(consts, 16 * 5)
            pe.sem_inc(gate_done, PRE)
            pe.sem_inc(up_done, PRE)
            pe.sem_inc(y_done, 2 * PRE)
            pe.sem_inc(xT_done, 2 * PRE)
            pe.sem_inc(ov_pe, 6)

            with pe.Fori(0, DEPTH) as l:

                def tile_transposes(n, chunks):
                    for half in range(2):
                        if n > 0:
                            pe.wait_ge(tr_evac, nth(l, N_TR, 2 * n - 1 + half))
                        for q in range(4):
                            mm = pe.transpose(bank(6 + half)[:, q * P:(q + 1) * P], chunks[4 * half + q], ident)
                        mm.then_inc(tr_done, 1)

                for t in range(NT):
                    pe.wait_ge(h_ready, nth(l, 2 * NT, t + 1))
                    tile_transposes(t, [hin[:, t % 2, k * P:(k + 1) * P] for k in range(KD)])
                pe.wait_ge(tr_evac, nth(l, N_TR, 2 * NT))

                def bank_free(n):
                    if 3 <= n < N_PJA + 3:
                        pe.wait_ge(pjA, nth(l, N_PJA, n - 2))
                    elif n >= N_PJA + 3:
                        pe.wait_ge(pjV, nth(l, N_PJV, n - 2 - N_PJA))

                def landed(b):
                    pe.wait_ge(landedA[b % 3], loadsA(l, b % 3, b // 3 + 1))

                def features_unit(b, c):
                    w, n = s3(slotA(b % 3)), 5 * b + c
                    bank_free(n)
                    for cc_ in ([c] if c < 4 else range(4)):
                        out, tok = ((bank(n % 3), slice(P, T)) if c < 4
                                    else (bank(n % 3)[:, cc_ * P:(cc_ + 1) * P], slice(0, P)))
                        for k in range(KD):
                            mm = pe.matmul(out, w[:, k, cc_ * P:(cc_ + 1) * P], hT[:, k, tok],
                                           start=k == 0, stop=k == KD - 1)
                    mm.then_inc(pj_done, 1)

                def unit_part(n, ks):
                    b, t = n // 5, n % 5
                    w = s3(slotA(b % 3))
                    for k in ks:
                        mm = pe.matmul(bank(n % 3), hT[:, k, t * P:(t + 1) * P], w[:, k, :],
                                       start=k == 0, stop=k == KD - 1)
                    return mm

                for b in range(2):
                    landed(b)
                    for c in range(5):
                        features_unit(b, c)

                def U(h):
                    return psum[:, (3 + 2 * h) * 512:(3 + 2 * h) * 512 + T]

                for ci, c in enumerate(JOBS):
                    def projections(place):
                        for n, first, second in UNITS[ci]:
                            if first == place:
                                if n % 5 == 0:
                                    landed(n // 5)
                                bank_free(n)
                                unit_part(n, range(0, 4))
                            if second == place:
                                unit_part(n, range(4, KD)).then_inc(pj_done, 1)

                    pair, dr = c % 2, c // 2
                    pe.wait_ge(k_ready, nth(l, 4, ci + 1))
                    if ci == 0:
                        pe.wait_ge(pjA, nth(l, N_PJA, 10))
                    for j in range(NL + 1):
                        if j:
                            pe.wait_ge(Q_ready, nth(l, 32, 8 * ci + j))
                            pe.wait_ge(K_ready, nth(l, 32, 8 * ci + j))
                        ks, qs = (kf[:, c], qf[:, c]) if j == 0 else (Kb[:, j % 2], Qb[:, j % 2])
                        for h in range(2):
                            if j:
                                pe.wait_ge(lv_acc, nth(l, 64, 16 * ci + 2 * j - 1 + h))
                            elif ci == 2:
                                pe.wait_ge(o_evac, nth(l, 4, h + 1))
                            elif ci and h == 1:
                                pe.wait_ge(s_ready, nth(l, 4, ci))
                            r = slice(64 * h, 64 * h + 64)
                            for w in range(NT):
                                tk = slice(w * P, (w + 1) * P)
                                mm = pe.matmul(U(h)[:, tk], ks[r, tk], qs[r, tk], start=True, stop=True)
                            mm.then_inc(lv_mm, 1)
                        if j < 7:
                            projections(j)
                    pe.wait_ge(K_ready, nth(l, 32, 8 * ci + 8))
                    pe.wait_ge(lv_acc, nth(l, 64, 16 * ci + 16))
                    for w in range(NT):
                        mm = pe.transpose(U(0)[:, w * P:(w + 1) * P], kf[:, c, w * P:(w + 1) * P], ident)
                    mm.then_inc(ke_t, 1)
                    projections(7)
                    pe.wait_ge(ke_evac, nth(l, 4, ci + 1))
                    for w in range(NT):
                        mm = pe.matmul(U(1)[:, w * P:(w + 1) * P], KEn[:, w, :], ig[:, w, pair * P:(pair + 1) * P],
                                       start=True, stop=True)
                    mm.then_inc(ds_mm, 1)
                    projections(8)
                    if dr == 1:
                        pe.wait_ge(s_ready, nth(l, 4, ci + 1))
                        pe.wait_ge(Q_ready, nth(l, 32, 8 * ci + 8))
                        for h in range(2):
                            r = slice(64 * h, 64 * h + 64)
                            for w in range(NT):
                                tk = slice(w * P, (w + 1) * P)
                                out = U(h)[:, tk]
                                iw = ig[:, w, pair * P:(pair + 1) * P]
                                pe.matmul(out, AT[:, 0, h, tk], iw, start=True, stop=False)
                                pe.matmul(out, AT[:, 1, h, tk], iw, start=False, stop=False)
                                ent = (0 if w == 0 else 1 + w, 1 if w == 0 else 2 + w)
                                pe.matmul(out, qf[r, pair, tk], S[r, 0, ent[0], :], start=False, stop=False)
                                mm = pe.matmul(out, qf[r, 2 + pair, tk], S[r, 1, ent[1], :], start=False, stop=True)
                            mm.then_inc(o_mm, 1)

                pe.wait_ge(o_evac, nth(l, 4, 4))
                for u in range(10):
                    if u % 5 == 0:
                        pe.wait_ge(pjA, nth(l, N_PJA, 26 + u))
                    else:
                        pe.wait_ge(r_ready, nth(l, 8, u - u // 5))
                    if u >= 2:
                        pe.wait_ge(r_evac, nth(l, 10, u - 1))
                    for q in range(4):
                        mm = pe.transpose(bank(7 if u % 2 else 6)[:, q * P:(q + 1) * P], nat(u)[:, q * P:(q + 1) * P], ident)
                    mm.then_inc(r_tr, 1)

                pe.wait_ge(v_ready, l + 1)
                pe.wait_ge(prm_in, nth(l, 96, 96))
                for t in range(NT):
                    for g in range(GB):
                        out = psum[:, 1536 + t * 256 + g * 64:1536 + t * 256 + g * 64 + 64]
                        mm = pe.matmul(out, wsT[:, g, :], uv[:, t, 256 + g * 64:256 + g * 64 + 64], start=True, stop=True)
                mm.then_inc(sp_mm, 1)

                def region(n):
                    return psum[:, (n % 2) * 1536:(n % 2) * 1536 + 1280]

                def keys(t):
                    return (640, 768, [5]) if t == 0 else (0, 640, list(range(5)))

                def scores(n):
                    t, h = n // 4, n % 4
                    k0, k1, _ = keys(t)
                    if n >= 2:
                        pe.wait_ge(at_evac, nth(l, 20, n - 1))
                    parts = ([(0, 0, P), (1, 0, P)] if t == 0 else
                             [(0, 512, 640), (0, 0, 512), (1, 384, 640), (1, 0, 384)])
                    for i, (m, a, b) in enumerate(parts):
                        r = slice(64 * m, 64 * m + 64)
                        if i == len(parts) - 1:
                            pe.wait_ge(sc_first, nth(l, 20, n + 1))
                        mm = pe.matmul(region(n)[:, m * 640 + a:m * 640 + b], qT[r, h, t * P:(t + 1) * P],
                                       kT[r, h, k0 + a:k0 + b], start=True, stop=True)
                        if i == 0:
                            mm.then_inc(sc_first, 1)
                    mm.then_inc(sc_done, 1)

                def probs_v(n):
                    t, h = n // 4, n % 4
                    pe.wait_ge(at_evac, nth(l, 20, n + 1))
                    if h == 0 and t:
                        pe.wait_ge(oa_evac, nth(l, NT, t))
                    vs = keys(t)[2]
                    for i, s_ in enumerate(vs):
                        mm = pe.matmul(bank(6)[:, h * P:(h + 1) * P], pdT[:, n % 2, i * P:(i + 1) * P],
                                       vv[s_][:, h * P:(h + 1) * P], start=i == 0, stop=i == len(vs) - 1)
                    mm.then_inc(pv_done, 1)

                pe.wait_ge(r_evac, nth(l, 10, 10))
                pe.wait_ge(kv_in, nth(l, 32, 32))
                pe.wait_ge(pjA, nth(l, N_PJA, N_PJA))
                pe.wait_ge(sp_used, l + 1)
                def row_products(n, ks):
                    if n >= N_ROW:
                        return
                    if ks[0] == 0:
                        pe.wait_ge(landed_h[n % 2], l * (8 * N_ROW) + 16 * (n // 2 + 1))
                        if n:
                            pe.wait_ge(row_sum, nth(l, N_ROW, n))
                    for k in ks:
                        mm = pe.matmul(bank(7)[0:2, 0:256], condT[:, k, :], halves[n % 2][:, k, :], start=k == 0, stop=k == KD - 1)
                    if ks[-1] == KD - 1:
                        mm.then_inc(row_mm, 1)

                scores(0)
                for n in range(20):
                    if n + 1 < 20:
                        scores(n + 1)
                    if n:
                        probs_v(n - 1)
                    row_products(n, range(0, 4))
                    pe.wait_ge(pd_ready, nth(l, 20, n + 1))
                    for i in range(len(keys(n // 4)[2])):
                        mm = pe.transpose(region(n)[:, i * P:(i + 1) * P], pd[:, n % 2, i * P:(i + 1) * P], ident)
                    mm.then_inc(at_tr, 1)
                    row_products(n, range(4, KD))
                probs_v(19)

                pe.wait_ge(mix_ready, l + 1)
                for t in range(NT):
                    tile_transposes(NT + t, [oa[:, t, k * P:(k + 1) * P] for k in range(4)]
                                    + [uv[:, t, k * P:(k + 1) * P] for k in range(2)]
                                    + [oc[:, t, k * P:(k + 1) * P] for k in range(2)])
                landed(7)
                landed(8)
                def router(t):
                    pe.wait_ge(h_ready, nth(l, 2 * NT, NT + t + 1))
                    tile_transposes(2 * NT + t, [hh[:, t % 2, k * P:(k + 1) * P] for k in range(KD)])
                    pe.wait_ge(tr_evac, nth(l, N_TR, 4 * NT + 2 * t + 2))
                    for k in range(KD):
                        mm = pe.matmul(bank(3)[:, t * NE:(t + 1) * NE], hTt[:, k, :], rw[:, k, :],
                                       start=k == 0, stop=k == KD - 1)
                    mm.then_inc(rt_mm, 1)

                for t in range(NT):
                    pe.wait_ge(tr_evac, nth(l, N_TR, 2 * NT + 2 * t + 2))
                    for half in range(2):
                        n = 35 + 2 * t + half
                        if n >= 38:
                            bank_free(n)
                        w = s3(slotA((7 + half) % 3))
                        for k in range(KD):
                            mm = pe.matmul(bank(n % 3), hT[:, k, t * P:(t + 1) * P], w[:, k, :],
                                           start=k == 0, stop=k == KD - 1)
                        mm.then_inc(pj_done, 1)
                    if t >= 2:
                        router(t - 2)
                router(NT - 2)
                router(NT - 1)
                pe.wait_ge(m_ready, l + 1)
                pe.matmul(bank(4)[:, 0:96], cst[:, C_TRI + P:C_TRI + 2 * P], before, start=True, stop=False)
                pe.matmul(bank(4)[:, 0:80], cst[:, C_TRI:C_TRI + P], chosen, start=False, stop=True).then_inc(rank_mm, 1)
                pe.wait_ge(at_ready, l + 1)
                for a in range(2 * NT):
                    mm = pe.matmul(bank(5)[:, 0:NB], at_row[:, a, :], at_block[:, a, :],
                                   start=a == 0, stop=a == 2 * NT - 1)
                mm.then_inc(id_mm, 1)

                with pe.Fori(0, NE // 2) as i:
                    def tokens_in(p):
                        pe.wait_ge(xg_in[p], l * 128 + i * 16 + 16)
                        if p:
                            pe.wait_ge(xT_dve, nth(l, NE // 2, i + 1))
                        for half in range(2):
                            for q in range(4):
                                k = 4 * half + q
                                mm = pe.transpose(bank(6 + half)[:, q * P:(q + 1) * P], xg[p][:, k * P:(k + 1) * P], ident)
                            mm.then_inc(xT_done, 1)

                    def weights(p, j):
                        base = loadsA(l, j, 3) if p == 0 else l * 128
                        pe.wait_ge((landedA, landedB)[p][j], base + i * 16 + 16)
                        return (slotA, slotB)[p](j)

                    def hidden(p, j, done):
                        w = s3(weights(p, j))
                        for k in range(KD):
                            mm = pe.matmul(bank(2 * p + j), xgT[p][:, k, :], w[:, k, :], start=k == 0, stop=k == KD - 1)
                        mm.then_inc(done, 1)

                    def turn_hidden(p):
                        pe.wait_ge(a_ready, nth(l, NE, i * 2 + p + 1))
                        for q in range(4):
                            mm = pe.transpose(bank(6 + p)[:, q * P:(q + 1) * P], av[p][:, q * P:(q + 1) * P], ident)
                        mm.then_inc(aT_done, 1)

                    def outputs(p, half):
                        w = s3(weights(p, 2), 4)
                        for k in range(4):
                            mm = pe.matmul(bank(4 + half), aT[p][:, k, :], w[:, k, half * W:(half + 1) * W],
                                           start=k == 0, stop=k == 3)
                        mm.then_inc(y_done, 1)

                    tokens_in(0)
                    pe.wait_ge(xT_dve, nth(l, NE // 2, i + 1))
                    hidden(0, 0, gate_done)
                    tokens_in(1)
                    hidden(0, 1, up_done)
                    pe.wait_ge(xT_act, nth(l, NE // 2, i + 1))
                    hidden(1, 0, gate_done)
                    turn_hidden(0)
                    hidden(1, 1, up_done)
                    pe.wait_ge(aT_ready, nth(l, NE, i * 2 + 1))
                    pe.wait_ge(yB_evac, nth(l, NE, i * 2 + 2))
                    outputs(0, 0)
                    turn_hidden(1)
                    outputs(0, 1)
                    pe.wait_ge(aT_ready, nth(l, NE, i * 2 + 2))
                    pe.wait_ge(yA_evac, nth(l, NE, i * 2 + 1))
                    outputs(1, 0)
                    pe.wait_ge(yA_evac, nth(l, NE, i * 2 + 2))
                    outputs(1, 1)
                until(pe, yB_evac, nth(l, NE, NE + 2))
                nov = pe.value_load(novi[0:1, :], min_val=0, max_val=OVB)
                with pe.Fori(0, OVB) as j:
                    with pe.If(nov > j):
                        pe.wait_ge(ov_g, l * (16 * OVB) + j * 16 + 16)
                        for half in range(2):
                            for q in range(4):
                                k = 4 * half + q
                                mm = pe.transpose(bank(6 + half)[:, q * P:(q + 1) * P], xg[0][:, k * P:(k + 1) * P], ident)
                        mm.then_inc(ov_pe, 1)
                        pe.wait_ge(ov_act, l * (4 * OVB) + j * 4 + 1)
                        for s_ in range(2):
                            pe.wait_ge(ov_w[s_], l * (16 * OVB) + j * 16 + 16)
                            for k in range(KD):
                                mm = pe.matmul(bank(s_), xgT[0][:, k, :], s3(slotA(s_))[:, k, :],
                                               start=k == 0, stop=k == KD - 1)
                            mm.then_inc(ov_pe, 1)
                        pe.wait_ge(ov_dve, l * OVB + j + 1)
                        for q in range(4):
                            mm = pe.transpose(bank(6)[:, q * P:(q + 1) * P], av[0][:, q * P:(q + 1) * P], ident)
                        mm.then_inc(ov_pe, 1)
                        pe.wait_ge(ov_act, l * (4 * OVB) + j * 4 + 3)
                        pe.wait_ge(ov_w[2], l * (16 * OVB) + j * 16 + 16)
                        for half in range(2):
                            for k in range(4):
                                mm = pe.matmul(bank(4 + half), aT[0][:, k, :],
                                               s3(slotA(2), 4)[:, k, half * W:(half + 1) * W],
                                               start=k == 0, stop=k == 3)
                            mm.then_inc(ov_pe, 1)
                    with pe.Else():
                        pe.drain()
                        pe.sem_inc(ov_pe, 6)

                for t in range(NT):
                    pe.wait_ge(weights_ready, nth(l, NT, t + 1))
                    pe.wait_ge(cmb_in[t], l * 32 + 32)
                    if t >= 2:
                        pe.wait_ge(cmb_used, nth(l, NT, t - 1))
                    for half in range(2):
                        cs = slice(half * W, (half + 1) * W)
                        out = bank(2 * (t % 2) + half)
                        pe.matmul(out, by_weight[:, 2 * t, :], expert_rows[t][0][:, cs], start=True, stop=False)
                        mm = pe.matmul(out, by_weight[:, 2 * t + 1, :], expert_rows[t][1][:, cs], start=False, stop=True)
                    mm.then_inc(cmb_mm, 1)

        @block.scalar
        def _(act):
            act.dma_start(cst[:], A["cst"]).then_inc(consts, 16)
            act.dma_start(maskf, A["masks"]).then_inc(consts, 16)
            act.dma_start(rw[:], A["w_router"].rearrange("(k p) e -> p k e", p=P)).then_inc(consts, 16)
            act.dma_start(rbias[:], rows("router_bias", 0, NE)).then_inc(consts, 16)
            act.dma_start(lbt, A["lbT"]).then_inc(consts, 16)
            act.dma_start(lamb, bass.AP(A["diff_lambda"].tensor, 0, [[0, P], [1, DEPTH * 256]])
                          .rearrange("p (l f d) -> p l f d", l=DEPTH, f=4)).then_inc(lam_in, 16)
            act.dma_start(x[:], A["x"].rearrange("(t p) d -> p t d", p=P)).then_inc(x_in, 16)
            act.wait_ge(bias_in, 32)
            act.activation(condT[:], condT[:], ACT.Silu).then_inc(cond_ready, 1)
            act.wait_ge(ada_ready, 1)
            act.dma_start(mod_dram.rearrange("l y d -> y l d")[:, :, 0:2 * D],
                          mrow.rearrange("y (l d) -> y l d", l=DEPTH)).then_inc(mod_out, 16)
            act.wait_ge(lbs_ready, 1)
            act.activation(lbx, lbx, ACT.Exp)
            act.activation(lams, lams, ACT.Exp).then_inc(lb_exp, 1)

            with act.Fori(0, DEPTH) as l:
                act.dma_start(ag, rows("attn_norm_g", l * 128, 128)).then_inc(prm_in, 16)
                act.dma_start(hg, rows("hgrn_norm_g", l * 256, 256)).then_inc(prm_in, 16)
                act.dma_start(mg, rows("mlp_ln_g", l * 256, 256)).then_inc(prm_in, 16)
                act.dma_start(mb, rows("mlp_ln_b", l * 256, 256)).then_inc(prm_in, 16)
                act.dma_start(wsT.rearrange("p g i -> p (g i)"), bass.AP(A["wsT"].tensor, l * (P * 512), [[512, P], [1, 512]])).then_inc(prm_in, 16)
                act.dma_start(bsT, bass.AP(A["bsT"].tensor, l * (P * 4), [[4, P], [1, 4]])).then_inc(prm_in, 16)
                act.wait_ge(x_ready, nth(l, NT, NT))
                act.dma_start(vv[0], bass.AP(A["cache_v"].tensor, l * 65536, [[512, P], [1, 512]])).then_inc(kv_in, 16)
                act.dma_start(x_dram.rearrange("(t p) d -> p t d", p=P), x[:]).then_inc(x_spilled, 16)

                def tile_evac(n, dst):
                    for half in range(2):
                        act.wait_ge(tr_done, nth(l, N_TR, 2 * n + half + 1))
                        act.activation(dst[:, 4 * half:4 * half + 4, :],
                                       bank(6 + half).rearrange("p (k t) -> p k t", k=4), ACT.Copy).then_inc(tr_evac, 1)

                for t in range(NT):
                    tile_evac(t, hT[:, :, t * P:(t + 1) * P])

                def unit_ready(n):
                    act.wait_ge(pj_done, nth(l, N_PJ, n + 1))
                    return bank(n % 3)

                for b, dst, fn in ((0, kf, ACT.Sigmoid), (1, qf, ACT.Copy)):
                    for c in range(5):
                        pb = unit_ready(5 * b + c)
                        if c < 4:
                            a = act.activation(dst[:, c, P:T], pb, fn)
                        else:
                            a = act.activation(dst[:, :, 0:P], pb.rearrange("p (c t) -> p c t", c=4), fn)
                        a.then_inc(pjA, 1)

                def projected(n):
                    pb, b, t = unit_ready(n), n // 5, n % 5
                    if b == 2:
                        act.activation(ig[:, t, 0:256], pb[:, 0:256], ACT.Copy)
                        a = act.activation(ig[:, t, 256:512], pb[:, 256:512], ACT.Silu)
                    elif b == 3:
                        a = act.activation(uv[:, t, :], pb, ACT.Gelu_apprx_tanh)
                    elif b == 4:
                        a = act.activation(vv[5 if t == 0 else t], pb, ACT.Copy)
                    else:
                        if n == 25:
                            act.wait_ge(x_spilled, l * 16 + 16)
                        a = act.activation(nat(n - 25), pb, ACT.Copy)
                    a.then_inc(pjA, 1)
                    if n == 20 or n == 25:
                        act.wait_ge(pjA, nth(l, N_PJA, n + 1))
                        name, src, done = ("new_v", vv[5], out_v) if n == 20 else ("new_k", nat(0), out_k)
                        act.dma_start(bass.AP(A[name].tensor, l * 65536, [[512, P], [1, 512]]), src).then_inc(done, 16)

                for ci, c in enumerate(JOBS):
                    at = {second: n for n, first, second in UNITS[ci]}
                    act.wait_ge(f_ready, nth(l, 4, ci + 1))
                    act.activation(gpad[:, :, 1:P + 1], gpad[:, :, 1:P + 1], ACT.Ln).then_inc(g_ready, 1)
                    if ci % 2 == 0:
                        act.wait_ge(s_zero, nth(l, 2, ci // 2 + 1))
                        for h in range(2):
                            for dr in range(2):
                                src = bass.AP(A["state"].tensor, l * 32768 + (dr * 16384 + (ci + h) * 4096), [[64, 64], [1, 64]])
                                act.dma_start(S[64 * h:64 * h + 64, dr, (2, 6)[dr], 64 * h:64 * h + 64], src).then_inc(s_init, 16)
                    for j in range(NL):
                        act.wait_ge(D_ready, nth(l, 32, 8 * ci + j + 1))
                        act.activation(Eb[:, j % 2], Eb[:, j % 2], ACT.Exp).then_inc(E_ready, 1)
                        if j and j - 1 in at:
                            projected(at[j - 1])
                    act.wait_ge(Q_ready, nth(l, 32, 8 * ci + 6))
                    act.wait_ge(K_ready, nth(l, 32, 8 * ci + 6))
                    beta = bsum[:, ci % 2, :, 1:P + 1] if c < 2 else bsum[:, ci % 2, :, 0:P]
                    act.activation(Eb[:, 1].rearrange("p (w t) -> p w t", w=NT), beta, ACT.Exp).then_inc(E_ready, 1)
                    projected(at[6])
                    act.wait_ge(D_ready, nth(l, 32, 8 * ci + 8))
                    act.activation(Eb[:, 0], Eb[:, 0], ACT.Exp).then_inc(E_ready, 1)
                    act.activation(eB[:, c, :], bsum[:, ci % 2, :, P], ACT.Exp).then_inc(E_ready, 1)
                    act.wait_ge(ke_t, nth(l, 4, ci + 1))
                    act.activation(KEn.rearrange("p w d -> p (w d)"), psum[:, 1536:1536 + T], ACT.Copy).then_inc(ke_evac, 1)
                    projected(at[8])
                    if c >= 2:
                        act.wait_ge(s_ready, nth(l, 4, ci + 1))
                        for h in range(2):
                            for dr in range(2):
                                dst = bass.AP(A["new_s"].tensor, l * 32768 + (dr * 16384 + (c - 2 + c - 2 + h) * 4096), [[64, 64], [1, 64]])
                                act.dma_start(dst, S[64 * h:64 * h + 64, dr, (1, 0)[dr], 64 * h:64 * h + 64]).then_inc(out_s, 16)

                act.wait_ge(o_mm, nth(l, 4, 4))
                act.dma_start(kT[:, :, 0:P], bass.AP(A["kcT"].tensor, l * 65536, [[512, P], [P, 4], [1, P]])).then_inc(kv_in, 16)
                for u in range(10):
                    act.wait_ge(r_tr, nth(l, 10, u + 1))
                    t = u % 5
                    if u < 5:
                        k0 = 640 if t == 0 else t * P
                        dst = kT[:, :, k0:k0 + P]
                    else:
                        dst = qT[:, :, t * P:(t + 1) * P]
                    act.activation(dst, bank(7 if u % 2 else 6).rearrange("p (h t) -> p h t", h=HA), ACT.Copy).then_inc(r_evac, 1)
                act.dma_start(mrow2, bass.AP(A["b_ada"].tensor, l * (6 * D) + 2 * D, [[0, 2], [1, 4 * D]])).then_inc(bias2_in, 16)
                act.wait_ge(out_k, l * 16 + 16)
                act.dma_start(x[:], x_dram.rearrange("(t p) d -> p t d", p=P)).then_inc(x_back, 16)

                def exps(n):
                    nk = P if n < 4 else T
                    act.wait_ge(nm_ready, nth(l, 20, n + 1))
                    for m in range(2):
                        a = act.activation(Pb[:, n % 2, m, 0:nk], psum[:, (n % 2) * 1536 + m * 640:(n % 2) * 1536 + m * 640 + nk],
                                           ACT.Exp, bias=negm[:, 2 * n + m:2 * n + m + 1], scale=SCALE,
                                           accum_out=Z[:, 2 * n + m:2 * n + m + 1])
                    a.then_inc(p_ready, 1)

                exps(0)
                for n in range(20):
                    nk = P if n < 4 else T
                    if n + 1 < 20:
                        exps(n + 1)
                    act.wait_ge(at_tr, nth(l, 20, n + 1))
                    if n >= 2:
                        act.wait_ge(pv_done, nth(l, 20, n - 1))
                    act.activation(pdT[:, n % 2, 0:nk], psum[:, (n % 2) * 1536:(n % 2) * 1536 + nk], ACT.Copy).then_inc(at_evac, 1)

                act.wait_ge(row_sum, nth(l, N_ROW, N_ROW))
                act.dma_start(bass.AP(mod_dram.tensor, l * (12 * D) + 2 * D, [[6 * D, 2], [1, 4 * D]]), mrow2).then_inc(m25_out, 16)
                act.wait_ge(m25_out, l * 16 + 16)
                act.wait_ge(pv_done, nth(l, 20, 20))
                act.wait_ge(out_v, l * 16 + 16)
                act.dma_start(gate_mod[:], mod_rows(l, 2, 1)).then_inc(m2_in, 16)
                act.wait_ge(mix_ready, l + 1)
                act.dma_start(lnb[:, 0, :], rows("ln_g", l * 2048, D)).then_inc(ln1_in, 16)
                act.dma_start(lnb[:, 1, :], rows("ln_b", l * 2048, D)).then_inc(ln1_in, 16)
                act.dma_start(shift2.rearrange("p y m d -> p y (m d)"), mod_rows(l, 3, 2)).then_inc(m34_in, 16)
                for t in range(NT):
                    tile_evac(NT + t, hT[:, :, t * P:(t + 1) * P])
                for t in range(NT):
                    act.wait_ge(h_ready, nth(l, 2 * NT, NT + t + 1))
                    act.dma_start(tok_dram[t * P:(t + 1) * P, :], hh[:, t % 2, :]).then_inc(h_stored[t % 2], 16)
                    if t:
                        act.wait_ge(rt_mm, nth(l, NT, t))
                    tile_evac(2 * NT + t, hTt)
                act.wait_ge(x1_ready, l + 1)
                act.dma_start(gate_mod[:], mod_rows(l, 5, 1)).then_inc(m5_in, 16)
                act.dma_start(lnb[:, 0, :], rows("ln_g", l * 2048 + D, D)).then_inc(ln2_in, 16)
                act.dma_start(lnb[:, 1, :], rows("ln_b", l * 2048 + D, D)).then_inc(ln2_in, 16)
                act.wait_ge(rt_mm, nth(l, NT, NT))
                act.activation(score.rearrange("p t e -> p (t e)"), bank(3)[:, 0:80], ACT.Sigmoid).then_inc(rt_score, 1)

                with act.Fori(0, NE // 2) as i:
                    for p in range(2):
                        if p:
                            act.wait_ge(xT_done, nth(l, 2 * NE, i * 4 + 4 + 2 * PRE))
                            act.activation(xgT[1], psum[:, 3072:4096].rearrange("p (k t) -> p k t", k=KD), ACT.Copy).then_inc(xT_act, 1)
                        act.wait_ge(gate_done, nth(l, NE, i * 2 + p + 1 + PRE))
                        act.activation(sg[p], bank(2 * p), ACT.Silu).then_inc(sg_ready, 1)
                    for p in range(2):
                        act.wait_ge(aT_done, nth(l, NE, i * 2 + p + 1))
                        act.activation(aT[p], bank(6 + p).rearrange("p (k t) -> p k t", k=4), ACT.Copy).then_inc(aT_ready, 1)
                    act.wait_ge(yA_evac, nth(l, NE, i * 2 + 2))
                    act.dma_start(bass.AP(exp_dram.tensor, i * (2 * P * D), [[D, P], [1, D]]), yb[0]).then_inc(y_stored[0], 16)
                    for half in range(2):
                        act.wait_ge(y_done, nth(l, 2 * NE, i * 4 + 3 + half + 2 * PRE))
                        if half == 0:
                            act.wait_ge(y_stored[1], l * 128 + i * 16 + 16)
                        act.activation(yb[1][:, half * W:(half + 1) * W], bank(4 + half), ACT.Copy).then_inc(yB_evac, 1)
                    act.wait_ge(yB_evac, nth(l, NE, i * 2 + 2 + 2))
                    act.dma_start(bass.AP(exp_dram.tensor, i * (2 * P * D) + P * D, [[D, P], [1, D]]), yb[1]).then_inc(y_stored[1], 16)

                until(act, y_stored[0], l * 128 + 144)
                until(act, pos_ready, l + 1)
                nov = act.value_load(novi[0:1, :], min_val=0, max_val=OVB)
                with act.Fori(0, OVB) as j:
                    with act.If(nov > j):
                        act.wait_ge(ov_pe, l * (6 * OVB) + j * 6 + 7)
                        act.activation(xgT[0], psum[:, 3072:4096].rearrange("p (k t) -> p k t", k=KD), ACT.Copy).then_inc(ov_act, 1)
                        act.wait_ge(ov_pe, l * (6 * OVB) + j * 6 + 8)
                        act.activation(sg[0], bank(0), ACT.Silu).then_inc(ov_act, 1)
                        act.wait_ge(ov_pe, l * (6 * OVB) + j * 6 + 10)
                        act.activation(aT[0], bank(6).rearrange("p (k t) -> p k t", k=4), ACT.Copy).then_inc(ov_act, 1)
                        act.wait_ge(ov_pe, l * (6 * OVB) + j * 6 + 12)
                        until(act, ov_st, l * (16 * OVB) + j * 16 + 16)
                        act.activation(yb[0], psum[:, 2048:3072], ACT.Copy).then_inc(ov_act, 1)
                        act.wait_ge(ov_act, l * (4 * OVB) + j * 4 + 4)
                        act.dma_start(bass.AP(exp_dram.tensor, j * (P * D) + NE * P * D, [[D, P], [1, D]]), yb[0]).then_inc(ov_st, 16)
                    with act.Else():
                        until(act, ov_st, l * (16 * OVB) + j * 16 + 16)
                        act.drain()
                        act.sem_inc(ov_act, 4)
                        act.sem_inc(ov_st, 16)
                for t in range(NT):
                    for q in range(2):
                        a = act.activation(by_weight[:, 2 * t + q, :], ident, ACT.Copy, scale=wt[:, t, q:q + 1])
                    a.then_inc(weights_ready, 1)
                for t in range(NT):
                    act.wait_ge(rstd_ready, nth(l, N_VAR, 3 + 2 * NT + t))
                    act.activation(x[:, t, :], x[:, t, :], ACT.Identity, bias=nmr[:, t:t + 1],
                                   scale=rstd[:, t:t + 1]).then_inc(centred, 1)

        @block.gpsimd
        def _(gp):
            gp.memset(mhalf, -0.5)
            gp.memset(zeros, 0.0)
            gp.drain()
            gp.wait_ge(m01_in, 16)
            gp.dma_start(bass.AP(exp_dram.tensor, NE * P * D, [[OVB * D, P], [256, OVB * D // 256], [1, 256]]),
                         zeros.unsqueeze(1).to_broadcast([P, OVB * D // 256, 256])).then_inc(zero_out, 16)
            gp.wait_ge(zero_out, 16)
            with gp.Fori(0, DEPTH) as l:
                until(gp, x_ready, nth(l, NT, NT))

                def inv_sqrt(n, dst, src):
                    until(gp, var_ready, nth(l, N_VAR, n))
                    gp.tensor_tensor(dst, src, mhalf[:, 0:dst.shape[1]], ALU.pow).then_inc(rstd_ready, 1)

                def add_shift(t):
                    until(gp, scaled, nth(l, NT, t + 1))
                    gp.tensor_tensor(x[:, t, :], x[:, t, :], lnb[:, 1, :], ALU.add).then_inc(x_ready, 1)

                def rotate(u):
                    t = u % 5
                    until(gp, pjA, nth(l, N_PJA, 26 + u))
                    raw = nat(u)
                    cos = cst[:, C_COS + (t - 1) * 64:C_COS + t * 64]
                    sin = cst[:, C_SIN + (t - 1) * 64:C_SIN + t * 64]
                    sn = sin.rearrange("p (a s e) -> p a s e", a=2, s=2)
                    for half in range(2):
                        part = raw[:, half * 256:half * 256 + 256]
                        gp.drain()
                        for s_ in range(2):
                            src = part.rearrange("p (g a s e) -> p g a s e", g=4, a=2, s=2)[:, :, :, 1 - s_, :]
                            out = ropeb.rearrange("p (g a s e) -> p g a s e", g=4, a=2, s=2)[:, :, :, s_, :]
                            gp.tensor_tensor(out, src, sn[:, :, s_, :].unsqueeze(1).to_broadcast([P, 4, 2, 16]), ALU.mult)
                        gp.drain()
                        p3 = part.rearrange("p (g d) -> p g d", g=4)
                        gp.tensor_tensor(p3, p3, cos.unsqueeze(1).to_broadcast([P, 4, 64]), ALU.mult)
                        gp.drain()
                        a = gp.tensor_tensor(part, part, ropeb, ALU.add)
                    gp.drain()
                    gp.sem_inc(r_ready, 1)

                rotated_between = [1, 2, 3, 4, 6, 7]
                for ci, c in enumerate(JOBS):
                    if ci % 2 == 0:
                        if ci:
                            until(gp, o_mm, nth(l, 4, 2))
                        else:
                            until(gp, tr_done, nth(l, N_TR, 10))
                        gp.memset(AT2, 0.0).then_inc(at_zero, 1)
                    until(gp, k_ready, nth(l, 4, ci + 1))
                    for j in range(1, NL + 1):
                        until(gp, E_ready, nth(l, 40, 10 * ci + j))
                        if ci or j > 1:
                            until(gp, lv_mm, nth(l, 64, 16 * ci + 2 * j - 2))
                        gp.tensor_tensor(Kb[:, j % 2], kf[:, c], Eb[:, (j - 1) % 2], ALU.mult).then_inc(K_ready, 1)
                        if ci == 2 and j == 1:
                            inv_sqrt(1, rstd, mv[:, :, 1])
                        if ci == 3 and j < NL:
                            rotate(rotated_between[j - 1])
                    until(gp, E_ready, nth(l, 40, 10 * ci + (9 if c < 2 else 8)))
                    until(gp, K_ready, nth(l, 32, 8 * ci + 7))
                    gp.tensor_tensor(kf[:, c], kf[:, c], Eb[:, 0 if c < 2 else 1], ALU.mult).then_inc(K_ready, 1)
                rotate(8)
                rotate(9)
                inv_sqrt(2, rs, ms)
                for t in range(NT):
                    inv_sqrt(3 + t, rsa[:, 4 * t:4 * t + 4], msa[:, 4 * t:4 * t + 4])
                for t in range(NT):
                    inv_sqrt(3 + NT + t, rstd[:, t:t + 1], mv[:, t, 1:2])
                until(gp, h_stored[0], l * 48 + 48)
                until(gp, h_stored[1], l * 32 + 32)
                until(gp, ids_ready, l + 1)
                with gp.Fori(0, NE // 2) as i:
                    for p in range(2):
                        until(gp, xT_done, nth(l, 2 * NE, i * 4 + 2 * p + 2))
                        gp.tensor_copy(ismall[:, 60 + p:61 + p], ismall[:, bass.ds(i * 2 + (10 + p), 1)])
                        gp.drain()
                        gp.indirect_dma_start(xg[p], None, tok_dram,
                                              bass.IndirectOffsetOnAxis(ap=ismall[:, 60 + p:61 + p], axis=0)).then_inc(xg_in[p], 16)
                until(gp, xT_done, nth(l, 2 * NE, 2 * NE + 2 * PRE))
                nov = gp.value_load(novi[0:1, :], min_val=0, max_val=OVB)
                with gp.Fori(0, OVB) as j:
                    with gp.If(nov > j):
                        until(gp, ov_pe, l * (6 * OVB) + j * 6 + 1)
                        gp.tensor_copy(ismall[:, 62:63], ismall[:, bass.ds(j + (10 + NE), 1)])
                        gp.drain()
                        gp.indirect_dma_start(xg[0], None, tok_dram,
                                              bass.IndirectOffsetOnAxis(ap=ismall[:, 62:63], axis=0)).then_inc(ov_g, 16)
                        until(gp, ov_g, l * (16 * OVB) + j * 16 + 16)
                    with gp.Else():
                        gp.dma_start(spare[0:1, bass.ds(j, 1)], bass.AP(A["router_bias"].tensor, 0, [[1, 1], [1, 1]])).then_inc(ov_g, 16)
                until(gp, ov_g, l * (16 * OVB) + 16 * OVB)
                until(gp, y_stored[0], l * 128 + 144)
                until(gp, y_stored[1], l * 128 + 144)
                until(gp, ov_st, l * (16 * OVB) + nov * 16 + 16)

                for t in range(NT):
                    for q in range(2):
                        gp.indirect_dma_start(expert_rows[t][q], None, exp_dram,
                                              bass.IndirectOffsetOnAxis(ap=posi[:, t, q:q + 1], axis=0)).then_inc(cmb_in[t], 16)
                until(gp, ln2_in, l * 32 + 32)
                for t in range(NT):
                    until(gp, var_ready, nth(l, N_VAR, 3 + 2 * NT + t))
                    gp.tensor_tensor(rstd[:, t:t + 1], mv[:, t, 1:2], mhalf[:, 0:1], ALU.pow)
                    gp.drain()
                    gp.tensor_tensor(nmr[:, t:t + 1], nmean[:, t:t + 1], rstd[:, t:t + 1], ALU.mult).then_inc(rstd_ready, 1)
                    if t:
                        add_shift(t - 1)
                add_shift(NT - 1)

        @block.vector
        def _(v):
            dr_ = v.drain

            def tt(out, a, b, op=ALU.mult):
                return v.tensor_tensor(out, a, b, op)

            def ts(out, a, s1, s2=None, op0=ALU.mult, op1=ALU.add):
                return v.tensor_scalar(out, a, s1, None, op0) if s2 is None else v.tensor_scalar(out, a, s1, s2, op0, op1)

            def stt(out, a, s, b, op0, op1):
                return v.scalar_tensor_tensor(out, a, s, b, op0, op1)

            v.sem_inc(ada_free, 4)
            v.wait_ge(bias_in, 32)
            with v.Fori(0, DEPTH) as la:
                for j in range(4):
                    v.wait_ge(ada_mm, nth(la, 4, j + 5))
                    m_ = ar[0:2, bass.ds(la * (2 * D) + (SLOT + j * W), W)]
                    tt(m_, m_, bank(j)[0:2, :], ALU.add).then_inc(ada_free, 1)
            dr_()
            v.sem_inc(ada_ready, 1)
            v.wait_ge(consts, 80)
            v.wait_ge(lam_in, 16)
            v.tensor_copy(masks[:], maskf)
            v.tensor_copy(lbm, lbt[:, 0, :])
            for l_ in range(1, DEPTH):
                dr_()
                tt(lbm, lbm, lbt[:, l_, :], ALU.max)
            dr_()
            tt(lbx, lbt, lbm.unsqueeze(1).to_broadcast([P, DEPTH, 4]), ALU.subtract)
            tt(lamp[:, :, 0, :], lamb[:, :, 0, :], lamb[:, :, 1, :])
            tt(lamp[:, :, 1, :], lamb[:, :, 2, :], lamb[:, :, 3, :])
            dr_()
            v.tensor_reduce(lams.rearrange("p (l f) -> p l f", l=DEPTH), lamp, AXX, ALU.add).then_inc(lbs_ready, 1)
            v.wait_ge(lb_exp, 1)
            v.tensor_copy(lbm, lbx[:, 0, :])
            for l_ in range(1, DEPTH):
                dr_()
                tt(lbm, lbm, lbx[:, l_, :], ALU.add)
            dr_()
            v.reciprocal(lbm, lbm)
            dr_()
            tt(lbx, lbx, lbm.unsqueeze(1).to_broadcast([P, DEPTH, 4]))
            v.memset(lbt[:, 0, :], 0.0)
            for l_ in range(1, DEPTH):
                dr_()
                tt(lbt[:, l_, :], lbt[:, l_ - 1, :], lbx[:, l_, :], ALU.add)
            for l_ in range(DEPTH):
                dr_()
                tt(lamn[:, l_:l_ + 1], lams[:, 2 * l_ + 1:2 * l_ + 2], lams[:, 2 * l_:2 * l_ + 1], ALU.subtract)
                dr_()
                ts(lamn[:, l_:l_ + 1], lamn[:, l_:l_ + 1], -lam_init(l_), None, ALU.add)
                v.memset(oml[:, l_:l_ + 1], 1.0 - lam_init(l_))
            v.wait_ge(mod_out, 16)
            v.sem_inc(yB_evac, 2)
            v.sem_inc(ov_st, 16)
            v.sem_inc(y_stored[0], 16)
            v.sem_inc(y_stored[1], 16)
            v.wait_ge(x_in, 16)
            v.sem_inc(x_ready, NT)

            with v.Fori(0, DEPTH) as l:
                def modulated(dst, t, m):
                    y = 0 if t == 0 else 1
                    stt(dst, m[:, y, 1, :], 1.0, x[:, t, :], ALU.add, ALU.mult)
                    dr_()
                    return tt(dst, dst, m[:, y, 0, :], ALU.add)

                v.wait_ge(m01_in, l * 16 + 16)
                for t in range(NT):
                    if t >= 2:
                        v.wait_ge(tr_done, nth(l, N_TR, 2 * (t - 1)))
                    v.wait_ge(x_ready, nth(l, NT, t + 1))
                    modulated(hin[:, t % 2, :], t, ishift).then_inc(h_ready, 1)

                dr_()
                v.tensor_copy(lb, lbt[:, bass.ds(l, 1), :].rearrange("p l c -> p (l c)"))
                v.tensor_copy(lamn_l, lamn[:, bass.ds(l, 1)])
                v.tensor_copy(oml_l, oml[:, bass.ds(l, 1)])
                dr_()
                ts(omlb, lb, -1.0, 1.0)
                dr_()
                ts(nomlb, omlb, -1.0)

                dr_()
                v.wait_ge(tr_done, nth(l, N_TR, 10))
                v.memset(gpad[:, :, 0:1], 0.0)
                v.wait_ge(prm_in, nth(l, 96, 96))
                ts(ag, ag, oml_l)
                def w5(ap):
                    return ap.rearrange("p (w t) -> p w t", w=NT)

                def distance(ci, c, j, dst):
                    m = LEVELS[j]
                    nb = P // (2 * m)
                    b0 = 1 if c < 2 else 0
                    beta = bsum[:, ci % 2, :, b0:b0 + P].rearrange("p w (b u m) -> p w b u m", b=nb, u=2)
                    out = dst.rearrange("p (w b u m) -> p w b u m", w=NT, b=nb, u=2)
                    mid = bsum[:, ci % 2, :, 1:P + 1].rearrange("p w (b u m) -> p w b u m", b=nb, u=2)[:, :, :, 0, m - 1:m]
                    midb = mid.to_broadcast([P, NT, nb, m])
                    tt(out[:, :, :, 1, :], beta[:, :, :, 1, :], midb, ALU.subtract)
                    return tt(out[:, :, :, 0, :], midb, beta[:, :, :, 0, :], ALU.subtract)

                vg = uv[:, :, 256:512]

                def gmlp_norm(step):
                    if step == 0:
                        until(v, pjA, nth(l, N_PJA, 20))
                        for t in range(NT):
                            v.bn_stats(stats[:, t, 0, :], uv[:, t, 256:512])
                        dr_()
                        for t in range(NT):
                            v.bn_aggr(mv[:, t, :], stats[:, t, 0, :])
                        dr_()
                        ts(mv[:, :, 1], mv[:, :, 1], EPS, None, ALU.add)
                        dr_()
                        v.sem_inc(var_ready, 1)
                    elif step == 1:
                        v.wait_ge(rstd_ready, nth(l, N_VAR, 1))
                        for t in range(NT):
                            ts(uv[:, t, 256:512], uv[:, t, 256:512], mv[:, t, 0:1], rstd[:, t:t + 1], ALU.subtract, ALU.mult)
                    elif step == 2:
                        dr_()
                        tt(vg, vg, mg.unsqueeze(1).to_broadcast([P, NT, 256]))
                    elif step == 3:
                        dr_()
                        tt(vg, vg, mb.unsqueeze(1).to_broadcast([P, NT, 256]), ALU.add).then_inc(v_ready, 1)

                for ci, c in enumerate(JOBS):
                    pair, dr = c % 2, c // 2
                    if ci == 0:
                        until(v, pjA, nth(l, N_PJA, 5))
                    if ci % 2 == 0:
                        if ci:
                            until(v, o_mm, nth(l, 4, 2))
                            until(v, out_s, l * 128 + 64)
                        dr_()
                        v.memset(S2, 0.0)
                        dr_()
                        v.sem_inc(s_zero, 1)
                    dr_()
                    ts(gpad[:, :, 1:P + 1], w5(kf[:, c]), omlb[:, c:c + 1], lb[:, c:c + 1]).then_inc(f_ready, 1)
                    dr_()
                    ts(kf[:, c], kf[:, c], nomlb[:, c:c + 1], omlb[:, c:c + 1]).then_inc(k_ready, 1)
                    v.wait_ge(g_ready, nth(l, 4, ci + 1))
                    v.tensor_tensor_scan(bsum2[:, ci % 2], cst[:, C_SCAN:C_SCAN + BW], gpad2, 0.0, ALU.mult, ALU.add)
                    dr_()
                    if ci:
                        v.wait_ge(K_ready, nth(l, 32, 8 * ci))
                    distance(ci, c, 0, Eb[:, 0]).then_inc(D_ready, 1)
                    distance(ci, c, 1, Eb[:, 1]).then_inc(D_ready, 1)
                    if ci % 2 == 0:
                        until(v, at_zero, nth(l, 2, ci // 2 + 1))

                    def take(j):
                        mk = masks[:, 0 if j == 0 else dr * NL + j, :].unsqueeze(1).to_broadcast([P, NT, P])
                        for h in range(2):
                            dr_()
                            until(v, lv_mm, nth(l, 64, 16 * ci + 2 * j + h + 1))
                            v.copy_predicated(w5(AT[:, dr, h, :]), mk,
                                              w5(psum[:, (3 + 2 * h) * 512:(3 + 2 * h) * 512 + T])).then_inc(lv_acc, 1)

                    if ci == 0:
                        v.wait_ge(pjA, nth(l, N_PJA, 10))
                    for j in range(1, NL + 1):
                        v.wait_ge(E_ready, nth(l, 40, 10 * ci + j))
                        if ci or j > 1:
                            v.wait_ge(lv_mm, nth(l, 64, 16 * ci + 2 * j - 2))
                        tt(Qb[:, j % 2], qf[:, c], Eb[:, (j - 1) % 2]).then_inc(Q_ready, 1)
                        take(j - 1)
                        if j + 1 < NL:
                            dr_()
                            v.wait_ge(K_ready, nth(l, 32, 8 * ci + j))
                            distance(ci, c, j + 1, Eb[:, (j + 1) % 2]).then_inc(D_ready, 1)
                        if ci == 2:
                            gmlp_norm(j - 1)
                    take(NL)
                    dr_()
                    v.wait_ge(K_ready, nth(l, 32, 8 * ci + 7))
                    b0 = 1 if c < 2 else 0
                    tt(w5(Eb[:, 0]), bsum[:, ci % 2, :, P:P + 1].to_broadcast([P, NT, P]), bsum[:, ci % 2, :, b0:b0 + P],
                       ALU.subtract).then_inc(D_ready, 1)
                    v.wait_ge(E_ready, nth(l, 40, 10 * ci + (8 if c < 2 else 9)))
                    tt(qf[:, c], qf[:, c], Eb[:, 1 if c < 2 else 0]).then_inc(Q_ready, 1)
                    v.wait_ge(E_ready, nth(l, 40, 10 * ci + 10))
                    v.wait_ge(ds_mm, nth(l, 4, ci + 1))
                    if ci % 2 == 0:
                        v.wait_ge(s_init, l * 128 + 64 * (ci // 2 + 1))
                    for w in ([0, 1, 2, 3] if dr == 0 else [0, 4, 3, 2]):
                        ent = (0 if w == 0 else 1 + w) if dr == 0 else (1 if w == 0 else 2 + w)
                        nxt = ent + 1 if dr == 0 else ent - 1
                        st = stt(S[:, dr, nxt, :], S[:, dr, ent, :], eB[:, c, w:w + 1],
                                 psum[:, 2560 + w * P:2560 + (w + 1) * P], ALU.mult, ALU.add)
                        dr_()
                    v.sem_inc(s_ready, 1)
                    if dr == 1:
                        for h in range(2):
                            v.wait_ge(o_mm, nth(l, 4, 2 * pair + h + 1))
                            c0 = (3 + 2 * h) * 512
                            v.tensor_copy(oc[:, :, (2 * pair + h) * 64:(2 * pair + h) * 64 + 64],
                                          w5(psum[:, c0:c0 + T])[:, :, 64 * h:64 * h + 64]).then_inc(o_evac, 1)

                sq = view(HG + 8345, 1280, "p (t c) -> p t c", t=NT)
                sq4 = view(HG + 8345, 1280, "p (t h e) -> p (t h) e", t=NT, h=HC)
                oc4 = view(24860, 1280, "p (g e) -> p g e", e=64)
                dr_()
                tt(sq, oc, oc)
                dr_()
                v.tensor_reduce(ms, sq4, AXX, ALU.add)
                dr_()
                ts(ms, ms, 1.0 / 64, EPS)
                dr_()
                v.sem_inc(var_ready, 1)
                v.wait_ge(sp_mm, l + 1)
                for g in range(GB):
                    c0 = 1536 + g * 64
                    src = psum[:, 1536:2816].rearrange("p (t c) -> p t c", t=NT)[:, :, g * 64:g * 64 + 64]
                    ug = uv[:, :, g * 64:g * 64 + 64]
                    stt(ug, src, bsT[:, g:g + 1], ug, ALU.add, ALU.mult)
                dr_()
                v.sem_inc(sp_used, 1)
                v.wait_ge(rstd_ready, nth(l, N_VAR, 2))
                tt(oc4, oc4, rs.unsqueeze(2).to_broadcast([P, 20, 64]))
                dr_()
                tt(oc, oc, hg.unsqueeze(1).to_broadcast([P, NT, 256]))
                dr_()
                tt(oc, oc, ig[:, :, 256:512])

                def maxima(n):
                    nk = P if n < 4 else T
                    v.wait_ge(sc_done, nth(l, 20, n + 1))
                    c0 = (n % 2) * 1536
                    v.tensor_reduce(nmx, psum[:, c0:c0 + 1280].rearrange("p (m k) -> p m k", m=2)[:, :, 0:nk], AXX, ALU.max)
                    dr_()
                    ts(negm[:, 2 * n:2 * n + 2], nmx, -SCALE).then_inc(nm_ready, 1)
                    dr_()

                sqa = view(HG + 13824 + 2560, 512)

                def heads(ap):
                    return ap.rearrange("p (h e) -> p h e", h=HA)

                def rms_normalised(t):
                    v.wait_ge(rstd_ready, nth(l, N_VAR, 3 + t))
                    tt(heads(oa[:, t, :]), heads(oa[:, t, :]), rsa[:, 4 * t:4 * t + 4].unsqueeze(2).to_broadcast([P, HA, P]))
                    dr_()
                    return tt(heads(oa[:, t, :]), heads(oa[:, t, :]), ag.unsqueeze(1).to_broadcast([P, HA, P]))

                dr_()
                maxima(0)
                v.wait_ge(bias2_in, l * 16 + 16)
                for n in range(20):
                    nk = P if n < 4 else T
                    if n and n <= N_ROW:
                        v.wait_ge(row_mm, nth(l, N_ROW, n))
                        m_ = mrow2[:, (n - 1) * 256:n * 256]
                        tt(m_, m_, bank(7)[0:2, 0:256], ALU.add).then_inc(row_sum, 1)
                    v.wait_ge(p_ready, nth(l, 20, n + 1))
                    v.reciprocal(rZ[:, 2 * n:2 * n + 2], Z[:, 2 * n:2 * n + 2])
                    dr_()
                    stt(cc[:, n:n + 1], Z[:, 2 * n:2 * n + 1], lamn_l, rZ[:, 2 * n + 1:2 * n + 2], ALU.mult, ALU.mult)
                    dr_()
                    if n >= 2:
                        v.wait_ge(at_tr, nth(l, 20, n - 1))
                    stt(pd[:, n % 2, 0:nk], Pb[:, n % 2, 1, 0:nk], cc[:, n:n + 1], Pb[:, n % 2, 0, 0:nk],
                        ALU.mult, ALU.add).then_inc(pd_ready, 1)
                    if n + 1 < 20:
                        maxima(n + 1)
                    if n % 4 == 0 and n or n == 19:
                        t = n // 4 - (n < 19)
                        until(v, pv_done, nth(l, 20, 4 * t + 4))
                        rz0 = rZ[:, 8 * t:8 * t + 8].rearrange("p (h m) -> p h m", h=HA)[:, :, 0:1]
                        dr_()
                        tt(heads(oa[:, t, :]), heads(bank(6)), rz0.to_broadcast([P, HA, P])).then_inc(oa_evac, 1)
                        dr_()
                        tt(sqa, oa[:, t, :], oa[:, t, :])
                        dr_()
                        v.tensor_reduce(msa[:, 4 * t:4 * t + 4], heads(sqa), AXX, ALU.add)
                        dr_()
                        ts(msa[:, 4 * t:4 * t + 4], msa[:, 4 * t:4 * t + 4], 1.0 / P, EPS)
                        dr_()
                        v.sem_inc(var_ready, 1)
                    if n % 4 == 1 and n > 4:
                        rms_normalised(n // 4 - 1)
                rms_normalised(NT - 1).then_inc(mix_ready, 1)

                def variance(t):
                    dr_()
                    v.bn_aggr(mv[:, t, :], stats[:, t, :, :].rearrange("p s f -> p (s f)"))
                    dr_()
                    ts(mv[:, t, 1:2], mv[:, t, 1:2], EPS, None, ALU.add)
                    dr_()
                    v.sem_inc(var_ready, 1)

                def normalised(n, t):
                    v.wait_ge(rstd_ready, nth(l, N_VAR, n + t))
                    ts(x[:, t, :], x[:, t, :], mv[:, t, 0:1], rstd[:, t:t + 1], ALU.subtract, ALU.mult)
                    dr_()
                    return tt(x[:, t, :], x[:, t, :], lnb[:, 0, :])

                def moe_input(t):
                    normalised(3 + NT, t)
                    dr_()
                    tt(x[:, t, :], x[:, t, :], lnb[:, 1, :], ALU.add)
                    dr_()
                    if t >= 2:
                        v.wait_ge(tr_done, nth(l, N_TR, 4 * NT + 2 * (t - 1)))
                        v.wait_ge(h_stored[t % 2], (l * 48 if t % 2 == 0 else l * 32) + 16 * (t // 2))
                    modulated(hh[:, t % 2, :], t, shift2).then_inc(h_ready, 1)

                until(v, x_back, l * 16 + 16)
                until(v, m2_in, l * 16 + 16)
                for t in range(NT):
                    y = 0 if t == 0 else 1
                    for half in range(2):
                        n = 35 + 2 * t + half
                        cs = slice(half * W, (half + 1) * W)
                        dr_()
                        v.wait_ge(pj_done, nth(l, N_PJ, n + 1))
                        tt(x1t[half], bank(n % 3), gate_mod[:, y, cs]).then_inc(pjV, 1)
                        dr_()
                        stt(x[:, t, cs], x[:, t, cs], ALPHA, x1t[half], ALU.mult, ALU.add)
                        dr_()
                        v.bn_stats(stats[:, t, half, :], x[:, t, cs])
                    variance(t)
                    if t == 0:
                        until(v, ln1_in, l * 32 + 32)
                        until(v, m34_in, l * 16 + 16)
                    else:
                        moe_input(t - 1)
                moe_input(NT - 1)
                dr_()
                v.sem_inc(x1_ready, 1)

                M, oh1, oh2, sel, key, eq, inm, pos, t1, t2 = R[0], R[1], R[2], R[3], R[4], R[5], R[6], R[7], R[8], R[9]
                g4 = [view(25884 + 800 + 20 * i, 20, "p (t g) -> p t g", t=NT) for i in range(8)]

                def over(v1, n=NE):
                    return v1.unsqueeze(1).to_broadcast([P, NT, n])

                def each_of(vt, n=NE):
                    return vt.to_broadcast([P, NT, n])

                v.wait_ge(rt_score, l + 1)
                tt(sel, score, over(rbias[:]), ALU.add)
                dr_()
                s4 = sel.rearrange("p t (g e) -> p (t g) e", g=4)

                def col(i):
                    return s4[:, :, i]

                def f(i):
                    return g4[i].rearrange("p t g -> p (t g)")

                tt(f(0), col(0), col(1), ALU.max)
                tt(f(1), col(0), col(1), ALU.min)
                tt(f(2), col(2), col(3), ALU.max)
                tt(f(3), col(2), col(3), ALU.min)
                dr_()
                tt(f(4), f(0), f(2), ALU.max)
                tt(f(5), f(0), f(2), ALU.min)
                tt(f(6), f(1), f(3), ALU.max)
                dr_()
                tt(f(5), f(5), f(6), ALU.max)
                dr_()
                tt(gt, g4[4], g4[5], ALU.add)
                dr_()

                def first_best(val, n, wts, best, eq_, onehot):
                    v.tensor_reduce(best, val, AXX, ALU.max)
                    dr_()
                    tt(eq_, val, best.unsqueeze(2).to_broadcast([P, NT, n]), ALU.is_equal)
                    dr_()
                    tt(eq_, eq_, over(wts, n))
                    dr_()
                    v.tensor_reduce(best, eq_, AXX, ALU.max)
                    dr_()
                    tt(onehot, eq_, best.unsqueeze(2).to_broadcast([P, NT, n]), ALU.is_equal)
                    dr_()

                bst = wsum
                first_best(gt, 4, cst[:, C_W4:C_W4 + 4], bst, g4[0], g4[1])
                inm4 = inm.rearrange("p t (g e) -> p (t g) e", g=4)
                v.tensor_copy(inm4, f(1).unsqueeze(2).to_broadcast([P, 20, 4]))
                dr_()
                tt(sel, sel, inm)
                ts(t1, inm, NEG, -NEG)
                dr_()
                tt(sel, sel, t1, ALU.add)
                dr_()
                first_best(sel, NE, cst[:, C_W16:C_W16 + NE], bst, key, oh1)
                stt(sel, oh1, -2 * NEG, sel, ALU.mult, ALU.add)
                dr_()
                first_best(sel, NE, cst[:, C_W16:C_W16 + NE], bst, key, oh2)
                v.memset(before[:, 0:NE], 0.0)
                tt(M, oh1, oh2, ALU.add)
                for t in range(NT):
                    dr_()
                    a = tt(before[:, (t + 1) * NE:(t + 2) * NE], before[:, t * NE:(t + 1) * NE], M[:, t, :], ALU.add)
                a.then_inc(m_ready, 1)
                v.wait_ge(rank_mm, l + 1)
                rank = bank(4)[:, 0:80].rearrange("p (t e) -> p t e", t=NT)
                cnt = bank(4)[:, 80:96]
                ts(ovc, cnt, 128.0, None, ALU.is_gt)
                for r_ in (256.0, 384.0, 512.0):
                    dr_()
                    stt(ovc, cnt, r_, ovc, ALU.is_gt, ALU.add)
                dr_()
                v.tensor_tensor_scan(ovi, cst[:, C_TRI + P:C_TRI + P + NE], ovc, 0.0, ALU.mult, ALU.add)
                dr_()
                tt(ovx, ovi, ovc, ALU.subtract)
                dr_()
                e128 = cst[:, C_E128:C_E128 + NE]
                ts(ovx, ovx, 128.0, float(NE * P - P))
                dr_()
                tt(ovx, ovx, e128, ALU.subtract)
                tt(pos, rank, over(e128), ALU.add)
                ts(t1, rank, 128.0, None, ALU.is_ge)
                dr_()
                tt(t1, t1, over(ovx))
                dr_()
                tt(pos, pos, t1, ALU.add)
                for q, oh in enumerate((oh1, oh2)):
                    dr_()
                    tt(t2, oh, pos)
                    dr_()
                    v.tensor_reduce(psn[:, :, q], t2, AXX, ALU.add)
                dr_()
                v.tensor_copy(posi, psn)
                dr_()
                ts(rowi, ismall[:, 0:10], P - 1, None, ALU.bitwise_and)
                ts(blki, ismall[:, 0:10], 7, None, ALU.logical_shift_right)
                dr_()
                v.tensor_copy(rowf, rowi)
                v.tensor_copy(blkf, blki)
                dr_()
                tt(at_block, blkf.unsqueeze(2).to_broadcast([P, 2 * NT, NB]),
                   cst[:, C_IOTA:C_IOTA + NB].unsqueeze(1).to_broadcast([P, 2 * NT, NB]), ALU.is_equal)
                tt(at_row, rowf.unsqueeze(2).to_broadcast([P, 2 * NT, P]),
                   cst[:, C_IOTA:C_IOTA + P].unsqueeze(1).to_broadcast([P, 2 * NT, P]), ALU.is_equal)
                dr_()
                tokens = at_block.rearrange("p (t q) b -> p t (q b)", q=2)
                tt(tokens, tokens, cst[:, C_TOK:C_TOK + NT].unsqueeze(2).to_broadcast([P, NT, 2 * NB]))
                dr_()
                v.sem_inc(at_ready, 1)
                v.tensor_copy(novi, ovi[:, NE - 1:NE])
                tt(R9, ovi.unsqueeze(1).to_broadcast([P, OVB, NE]),
                   cst[:, C_IOTA:C_IOTA + OVB].unsqueeze(2).to_broadcast([P, OVB, NE]), ALU.is_le)
                dr_()
                v.tensor_reduce(R9s, R9, AXX, ALU.add)
                dr_()
                ts(R9s, R9s, float(NE - 1), None, ALU.min)
                dr_()
                v.tensor_copy(bexi, R9s)
                for q, oh in enumerate((oh1, oh2)):
                    dr_()
                    tt(t1, oh, score)
                    dr_()
                    v.tensor_reduce(wt[:, :, q], t1, AXX, ALU.add)
                dr_()
                tt(wsum, wt[:, :, 0], wt[:, :, 1], ALU.add)
                dr_()
                v.reciprocal(wsum, wsum)
                dr_()
                tt(wt, wt, wsum.unsqueeze(2).to_broadcast([P, NT, 2]))
                dr_()
                v.sem_inc(pos_ready, 1)
                v.wait_ge(id_mm, l + 1)
                v.tensor_copy(ids, bank(5)[:, 0:NB])
                dr_()
                v.sem_inc(ids_ready, 1)

                with v.Fori(0, NE // 2) as i:
                    v.wait_ge(xT_done, nth(l, 2 * NE, i * 4 + 2 + 2 * PRE))
                    v.tensor_copy(xgT[0], psum[:, 3072:4096].rearrange("p (k t) -> p k t", k=KD)).then_inc(xT_dve, 1)
                    for p in range(2):
                        v.wait_ge(up_done, nth(l, NE, i * 2 + p + 1 + PRE))
                        v.wait_ge(sg_ready, nth(l, NE, i * 2 + p + 1))
                        tt(av[p], sg[p], bank(2 * p + 1)).then_inc(a_ready, 1)
                    for half in range(2):
                        v.wait_ge(y_done, nth(l, 2 * NE, i * 4 + 1 + half + 2 * PRE))
                        if half == 0:
                            v.wait_ge(y_stored[0], l * 128 + i * 16 + 16)
                        v.tensor_copy(yb[0][:, half * W:(half + 1) * W], bank(4 + half)).then_inc(yA_evac, 1)
                dr_()
                nov = v.value_load(novi[0:1, :], min_val=0, max_val=OVB)
                with v.Fori(0, OVB) as j:
                    with v.If(nov > j):
                        v.wait_ge(ov_pe, l * (6 * OVB) + j * 6 + 9)
                        v.wait_ge(ov_act, l * (4 * OVB) + j * 4 + 2)
                        tt(av[0], sg[0], bank(1)).then_inc(ov_dve, 1)
                    with v.Else():
                        v.drain()
                        v.sem_inc(ov_dve, 1)

                def times_g(t):
                    v.wait_ge(centred, nth(l, NT, t + 1))
                    tt(x[:, t, :], x[:, t, :], lnb[:, 0, :]).then_inc(scaled, 1)

                until(v, m5_in, l * 16 + 16)
                for t in range(NT):
                    y = 0 if t == 0 else 1
                    dr_()
                    v.wait_ge(cmb_mm, nth(l, NT, t + 1))
                    tt(ysum, psum[:, (t % 2) * 1024:(t % 2) * 1024 + 1024], gate_mod[:, y, :]).then_inc(cmb_used, 1)
                    dr_()
                    stt(x[:, t, :], x[:, t, :], ALPHA, ysum, ALU.mult, ALU.add)
                    dr_()
                    for half in range(2):
                        v.bn_stats(stats[:, t, half, :], x[:, t, half * W:(half + 1) * W])
                    dr_()
                    v.bn_aggr(mv[:, t, :], stats[:, t, :, :].rearrange("p s f -> p (s f)"))
                    dr_()
                    ts(nmean[:, t:t + 1], mv[:, t, 0:1], -1.0)
                    ts(mv[:, t, 1:2], mv[:, t, 1:2], EPS, None, ALU.add).then_inc(var_ready, 1)
                    if t == 0:
                        until(v, ln2_in, l * 32 + 32)
                    else:
                        times_g(t - 1)
                times_g(NT - 1)


def shape_constants(np):
    c = np.zeros((P, C_END), np.float32)
    c[:, C_ID:C_ID + P] = np.eye(P)
    c[:, C_TRI:C_TRI + P] = np.triu(np.ones((P, P)), 1)
    c[:, C_TRI + P:C_TRI + 2 * P] = 1.0
    c[:, C_W4:C_W4 + 4] = np.arange(4, 0, -1)
    c[:, C_W16:C_W16 + NE] = np.arange(NE, 0, -1)
    c[:, C_E128:C_E128 + NE] = np.arange(NE) * P
    c[:, C_IOTA:C_IOTA + P] = np.arange(P)
    c[:, C_TOK:C_TOK + NT] = np.arange(P)[:, None] + P * np.arange(NT)[None]
    inv = (10000.0 ** (-np.arange(16, dtype=np.float32) / 16)).astype(np.float32)
    pos = np.arange(512)
    cos, sin = np.zeros((512, 64), np.float32), np.zeros((512, 64), np.float32)
    for half, q in enumerate((pos // 64, pos % 64)):
        ang = q[:, None].astype(np.float32) * inv
        o = half * 32
        cos[:, o:o + 16] = cos[:, o + 16:o + 32] = np.cos(ang)
        sin[:, o:o + 16], sin[:, o + 16:o + 32] = -np.sin(ang), np.sin(ang)
    c[:, C_COS:C_COS + 256] = cos.reshape(4, P, 64).transpose(1, 0, 2).reshape(P, 256)
    c[:, C_SIN:C_SIN + 256] = sin.reshape(4, P, 64).transpose(1, 0, 2).reshape(P, 256)
    scan = np.ones((NT, P + 1), np.float32)
    scan[:, 0] = 0
    c[:, C_SCAN:C_END] = scan.reshape(1, -1)
    m = np.zeros((P, 2 * NL + 1, P), np.float32)
    s, t = np.arange(P)[:, None], np.arange(P)[None]
    m[:, 0] = s == t
    for j, h in enumerate(LEVELS):
        same = s // (2 * h) == t // (2 * h)
        su, tu = (s // h) % 2, (t // h) % 2
        m[:, 1 + j] = same & (su == 0) & (tu == 1)
        m[:, 1 + NL + j] = same & (su == 1) & (tu == 0)
    return c, m


def kernel(**inputs):
    import numpy as np
    import concourse.bacc as bacc
    from concourse import mybir as mb
    from concourse.bass_utils import run_bass_kernel_spmd as run

    g = {k: np.asarray(a) for k, a in inputs.items()}
    cst, masks = shape_constants(np)
    cond = np.stack([g["c_ctx"], g["c"][0]])
    arrays = {
        "x": np.concatenate([g["x_prompt"][0], g["x_sample"][0]]),
        "condT": cond.reshape(2, KD, P).transpose(2, 1, 0),
        "w_ada": g["w_ada"], "b_ada": g["b_ada"], "w_in": g["w_in"], "w_out": g["w_out"],
        "diff_lambda": g["diff_lambda"], "attn_norm_g": g["attn_norm_g"],
        "mlp_ln_g": g["mlp_ln_g"], "mlp_ln_b": g["mlp_ln_b"],
        "wsT": g["w_spatial"].transpose(0, 3, 1, 2), "bsT": g["b_spatial"].transpose(0, 2, 1),
        "lbT": g["hgrn_lb"].reshape(2, DEPTH, 2, P).transpose(3, 1, 0, 2).reshape(P, DEPTH, 4),
        "hgrn_norm_g": g["hgrn_norm_g"], "ln_g": g["ln_g"], "ln_b": g["ln_b"],
        "w_router": g["w_router"], "router_bias": g["router_bias"],
        "w_gate": g["w_gate"], "w_up": g["w_up"], "w_down": g["w_down"],
        "kcT": g["cache_k"][0].transpose(0, 3, 4, 2, 1).reshape(DEPTH, P, HA, P),
        "cache_v": g["cache_v"][0].reshape(DEPTH, P, 512),
        "state": g["state_hgrn"][0],
        "cst": cst, "masks": masks,
    }
    outs = {"y": (T, D), "new_k": (DEPTH, P, 512), "new_v": (DEPTH, P, 512), "new_s": (DEPTH, 2, HC, 64, 64)}
    nc = bacc.Bacc("TRN2", target_bir_lowering=False, num_devices=1)
    A = {}
    for name in arrays:
        arrays[name] = np.ascontiguousarray(arrays[name])
        A[name] = nc.dram_tensor(name, list(arrays[name].shape), mb.dt.from_np(arrays[name].dtype), kind="ExternalInput").ap()
    for name, shape in outs.items():
        A[name] = nc.dram_tensor(name, list(shape), mb.dt.float32, kind="ExternalOutput").ap()
    build_program(nc, A)
    r = run(nc, [arrays], core_ids=[0]).results[0]
    y = r["y"]
    return (y[:P].reshape(1, P, D), y[P:].reshape(1, T - P, D),
            r["new_k"].reshape(1, DEPTH, P, HA, 2, DQ), r["new_v"].reshape(1, DEPTH, P, HA, 128),
            r["new_s"].reshape(1, DEPTH, 2, HC, 64, 64))
```
